# Optimizing a Trainium2 kernel written in Bass

```python
import math
import jax, jax.numpy as jnp
from jax import lax
import numpy as np

D_MODEL = 1024
BATCH = 1
SEQ = 512
DEPTH = 2
DEC_BATCH = 8
DEC_SEQ = 1
PAST_LEN = 1024
PAGE_SIZE = 128

N_A_LAYERS = DEPTH // 2
N_B_LAYERS = DEPTH - N_A_LAYERS
RET_HEADS = 4
RET_DK = D_MODEL // RET_HEADS
RET_DV = 2 * RET_DK
RET_CHUNK = 128
ROPE_BASE = 10000.0
DIFF_HEADS = 8
DIFF_DH = D_MODEL // (2 * DIFF_HEADS)
DIFF_W = DIFF_HEADS * 2 * DIFF_DH
Q_BLOCK = 128
REL_BUCKETS = 32
REL_MAX_DIST = 128
FFN_DIM = 2816
LN_EPS = 1e-5
DEEPNORM_ALPHA = (2.0 * DEPTH) ** 0.25
DEEPNORM_BETA = (8.0 * DEPTH) ** -0.25

kernel_name = "yoco_retention_diffattn_decoder_step"

def layer_norm(x, g, b):
    xf = x.astype(jnp.float32)
    mu = jnp.mean(xf, -1, keepdims=True)
    var = jnp.mean(jnp.square(xf - mu), -1, keepdims=True)
    return ((xf - mu) * lax.rsqrt(var + LN_EPS) * g + b).astype(x.dtype)

def post_norm(x, fx, g, b):
    return layer_norm(DEEPNORM_ALPHA * x + fx, g, b)

def swiglu(x, w_in, w_out):
    gate, up = jnp.split(x @ w_in, 2, axis=-1)
    return (jax.nn.silu(gate) * up) @ w_out

def rope(x, pos):
    half = x.shape[-1] // 2
    inv = ROPE_BASE ** (-jnp.arange(half, dtype=jnp.float32) / half)
    ang = pos.astype(jnp.float32)[:, None] * inv[None, :]
    cos = jnp.cos(ang)[None, :, None, :]
    sin = jnp.sin(ang)[None, :, None, :]
    x1, x2 = x[..., :half], x[..., half:]
    return jnp.concatenate([x1 * cos - x2 * sin, x1 * sin + x2 * cos], axis=-1)

def retention_log_decay():
    return jnp.log(1.0 - 2.0 ** (-5.0 - jnp.arange(RET_HEADS, dtype=jnp.float32)))

def retention_scan(q, k, v, s0, log_gamma):
    b, t, h, _ = q.shape
    c = math.gcd(t, RET_CHUNK)
    n = t // c
    idx = jnp.arange(c, dtype=jnp.float32)
    diff = idx[:, None] - idx[None, :]
    intra = jnp.where(diff >= 0, jnp.exp(jnp.maximum(diff, 0.0)[None] * log_gamma[:, None, None]), 0.0)
    cross = jnp.exp((idx + 1.0)[None, :] * log_gamma[:, None]).T[None, :, :, None]
    to_end = jnp.exp((c - 1.0 - idx)[None, :] * log_gamma[:, None]).T[None, :, :, None]
    chunk_decay = jnp.exp(c * log_gamma)[None, :, None, None]

    def chunk(a):
        return jnp.moveaxis(a.reshape(b, n, c, h, a.shape[-1]), 1, 0)

    def step(s, qkv):
        qc, kc, vc = qkv
        scores = jnp.einsum('bihd,bjhd->bhij', qc, kc) * intra[None]
        o = jnp.einsum('bhij,bjhe->bihe', scores, vc)
        o = o + jnp.einsum('bihd,bhde->bihe', qc, s) * cross
        s = s * chunk_decay + jnp.einsum('bjhd,bjhe->bhde', kc * to_end, vc)
        return s, o

    s, o = lax.scan(step, s0, (chunk(q), chunk(k), chunk(v)))
    o = jnp.moveaxis(o, 0, 1).reshape(b, t, h, o.shape[-1])
    return o, s

def retention_mixer(x, pos, s0, w_in, w_out):
    b, t, _ = x.shape
    nq = RET_HEADS * RET_DK
    nv = RET_HEADS * RET_DV
    proj = x @ w_in
    q, k, v, g = jnp.split(proj, [nq, 2 * nq, 2 * nq + nv], axis=-1)
    q = rope(q.reshape(b, t, RET_HEADS, RET_DK).astype(jnp.float32), pos)
    k = rope(k.reshape(b, t, RET_HEADS, RET_DK).astype(jnp.float32), pos) * (RET_DK ** -0.5)
    v = v.reshape(b, t, RET_HEADS, RET_DV).astype(jnp.float32)
    o, s = retention_scan(q, k, v, s0.astype(jnp.float32), retention_log_decay())
    mu = jnp.mean(o, -1, keepdims=True)
    var = jnp.mean(jnp.square(o - mu), -1, keepdims=True)
    o = ((o - mu) * lax.rsqrt(var + LN_EPS)).reshape(b, t, nv).astype(x.dtype)
    return (jax.nn.silu(g) * o) @ w_out, s

def rel_bucket(qpos, kpos):
    n = jnp.maximum(qpos[:, None] - kpos[None, :], 0)
    max_exact = REL_BUCKETS // 2
    nf = jnp.maximum(n, 1).astype(jnp.float32)
    large = max_exact + (jnp.log(nf / max_exact) / math.log(REL_MAX_DIST / max_exact)
                         * (REL_BUCKETS - max_exact)).astype(jnp.int32)
    large = jnp.minimum(large, REL_BUCKETS - 1)
    return jnp.where(n < max_exact, n, large)

def diff_attention(q, qpos, k_past, v_past, k_new, v_new, rel_bias, lam):
    b, t = q.shape[:2]
    p = k_past.shape[1]
    qb = math.gcd(t, Q_BLOCK)
    nb = t // qb
    kpos = jnp.concatenate([jnp.arange(p, dtype=jnp.int32), qpos])
    scale = DIFF_DH ** -0.5

    def block(i):
        qi = lax.dynamic_slice_in_dim(q, i * qb, qb, axis=1)
        pi = lax.dynamic_slice_in_dim(qpos, i * qb, qb)
        s = jnp.concatenate([
            jnp.einsum('bqhmd,bkhmd->bhmqk', qi, k_past, preferred_element_type=jnp.float32),
            jnp.einsum('bqhmd,bkhmd->bhmqk', qi, k_new, preferred_element_type=jnp.float32)], axis=-1) * scale
        bias = jnp.take(rel_bias, rel_bucket(pi, kpos), axis=0)
        s = s + jnp.transpose(bias, (2, 0, 1)).astype(jnp.float32)[None, :, None]
        s = jnp.where((kpos[None, :] <= pi[:, None])[None, None, None], s, -jnp.inf)
        a = jax.nn.softmax(s, axis=-1)
        w = a[:, :, 0] - lam * a[:, :, 1]
        return (jnp.einsum('bhqk,bkhe->bqhe', w[..., :p], v_past)
                + jnp.einsum('bhqk,bkhe->bqhe', w[..., p:], v_new))

    o = lax.map(block, jnp.arange(nb))
    return jnp.moveaxis(o, 0, 1).reshape(b, t, DIFF_HEADS, 2 * DIFF_DH)

def diff_mixer(x, pos, k_past, v_past, k_new, v_new, w_q, w_o, lam_vecs, subln_g, rel_bias, lambda_init):
    b, t, _ = x.shape
    q = (x @ w_q).reshape(b, t, DIFF_HEADS, 2, DIFF_DH)
    lv = lam_vecs.astype(jnp.float32)
    lam = jnp.exp(jnp.sum(lv[0] * lv[1])) - jnp.exp(jnp.sum(lv[2] * lv[3])) + lambda_init
    o = diff_attention(q, pos, k_past, v_past, k_new, v_new, rel_bias, lam).astype(jnp.float32)
    o = o * lax.rsqrt(jnp.mean(o * o, -1, keepdims=True) + LN_EPS) * subln_g * (1.0 - lambda_init)
    return o.reshape(b, t, DIFF_W).astype(x.dtype) @ w_o

def trunk(x, past_len, ret_s0, k_past, v_past, ln_g, ln_b, ffn_w_in, ffn_w_out,
          ret_w_in, ret_w_out, w_kv, diff_w_q, diff_w_o, diff_lambda, diff_subln_g, rel_bias):
    b, t, _ = x.shape
    pos = past_len + jnp.arange(t, dtype=jnp.int32)
    new_states = []
    k_new = None
    v_new = None
    for l in range(DEPTH):
        x = post_norm(x, 0.5 * swiglu(x, ffn_w_in[l, 0], ffn_w_out[l, 0]), ln_g[l, 0], ln_b[l, 0])
        if l < N_A_LAYERS:
            h, s = retention_mixer(x, pos, ret_s0[l], ret_w_in[l], ret_w_out[l])
            new_states.append(s)
        else:
            j = l - N_A_LAYERS
            if j == 0:
                kv = x @ w_kv
                k_new = kv[..., :DIFF_W].reshape(b, t, DIFF_HEADS, 2, DIFF_DH)
                v_new = kv[..., DIFF_W:].reshape(b, t, DIFF_HEADS, 2 * DIFF_DH)
            lambda_init = 0.8 - 0.6 * math.exp(-0.3 * l)
            h = diff_mixer(x, pos, k_past, v_past, k_new, v_new, diff_w_q[j], diff_w_o[j],
                           diff_lambda[j], diff_subln_g[j], rel_bias, lambda_init)
        x = post_norm(x, h, ln_g[l, 1], ln_b[l, 1])
        x = post_norm(x, 0.5 * swiglu(x, ffn_w_in[l, 1], ffn_w_out[l, 1]), ln_g[l, 2], ln_b[l, 2])
    return x, jnp.stack(new_states), k_new.reshape(b, t, DIFF_HEADS, 2 * DIFF_DH), v_new

def setup_inputs(seed: int = 0) -> dict:
    key = jax.random.key(seed)
    ks = jax.random.split(key, 20)
    f32 = jnp.float32
    n_pages = PAST_LEN // PAGE_SIZE
    n_used = DEC_BATCH * n_pages
    n_pool = n_used + n_used // 4

    def nrm(k, shape, scale):
        return jax.random.normal(k, shape, f32) * scale

    perm = jax.random.permutation(ks[5], n_pool)[:n_used]
    return {
        "x_prompt": nrm(ks[0], (BATCH, SEQ, D_MODEL), 1.0),
        "x_sample": nrm(ks[1], (DEC_BATCH, DEC_SEQ, D_MODEL), 1.0),
        "state_ret": nrm(ks[2], (N_A_LAYERS, DEC_BATCH, RET_HEADS, RET_DK, RET_DV), 0.5),
        "cache_k": nrm(ks[3], (n_pool, PAGE_SIZE, DIFF_HEADS, 2 * DIFF_DH), 1.0),
        "cache_v": nrm(ks[4], (n_pool, PAGE_SIZE, DIFF_HEADS, 2 * DIFF_DH), 1.0),
        "page_table": perm.reshape(DEC_BATCH, n_pages).astype(jnp.int32),
        "ln_g": 1.0 + nrm(ks[6], (DEPTH, 3, D_MODEL), 0.02),
        "ln_b": nrm(ks[7], (DEPTH, 3, D_MODEL), 0.02),
        "ffn_w_in": nrm(ks[8], (DEPTH, 2, D_MODEL, 2 * FFN_DIM), D_MODEL ** -0.5),
        "ffn_w_out": nrm(ks[9], (DEPTH, 2, FFN_DIM, D_MODEL), DEEPNORM_BETA * FFN_DIM ** -0.5),
        "ret_w_in": nrm(ks[10], (N_A_LAYERS, D_MODEL, 2 * RET_HEADS * RET_DK + 2 * RET_HEADS * RET_DV), D_MODEL ** -0.5),
        "ret_w_out": nrm(ks[11], (N_A_LAYERS, RET_HEADS * RET_DV, D_MODEL), DEEPNORM_BETA * (RET_HEADS * RET_DV) ** -0.5),
        "w_kv": nrm(ks[12], (D_MODEL, 2 * DIFF_W), D_MODEL ** -0.5),
        "diff_w_q": nrm(ks[13], (N_B_LAYERS, D_MODEL, DIFF_W), D_MODEL ** -0.5),
        "diff_w_o": nrm(ks[14], (N_B_LAYERS, DIFF_W, D_MODEL), DEEPNORM_BETA * DIFF_W ** -0.5),
        "diff_lambda": nrm(ks[15], (N_B_LAYERS, 4, DIFF_DH), 0.1),
        "diff_subln_g": 1.0 + nrm(ks[16], (N_B_LAYERS, 2 * DIFF_DH), 0.02),
        "rel_bias": nrm(ks[17], (REL_BUCKETS, DIFF_HEADS), 0.5),
    }

def reference(x_prompt, x_sample, state_ret, cache_k, cache_v, page_table, ln_g, ln_b,
              ffn_w_in, ffn_w_out, ret_w_in, ret_w_out, w_kv, diff_w_q, diff_w_o,
              diff_lambda, diff_subln_g, rel_bias):
    bp = x_prompt.shape[0]
    s0_prompt = jnp.zeros((N_A_LAYERS, bp, RET_HEADS, RET_DK, RET_DV), jnp.float32)
    k_empty = jnp.zeros((bp, 0, DIFF_HEADS, 2, DIFF_DH), x_prompt.dtype)
    v_empty = jnp.zeros((bp, 0, DIFF_HEADS, 2 * DIFF_DH), x_prompt.dtype)
    y_prompt, state_ret_prompt, k_prompt, v_prompt = trunk(
        x_prompt, 0, s0_prompt, k_empty, v_empty, ln_g, ln_b, ffn_w_in, ffn_w_out,
        ret_w_in, ret_w_out, w_kv, diff_w_q, diff_w_o, diff_lambda, diff_subln_g, rel_bias)

    db, n_pages = page_table.shape
    past_len = n_pages * cache_k.shape[1]
    k_past = cache_k[page_table].reshape(db, past_len, DIFF_HEADS, 2, DIFF_DH)
    v_past = cache_v[page_table].reshape(db, past_len, DIFF_HEADS, 2 * DIFF_DH)
    y_sample, state_ret_sample, k_sample, v_sample = trunk(
        x_sample, past_len, state_ret, k_past, v_past, ln_g, ln_b, ffn_w_in, ffn_w_out,
        ret_w_in, ret_w_out, w_kv, diff_w_q, diff_w_o, diff_lambda, diff_subln_g, rel_bias)

    return (y_prompt, y_sample, state_ret_prompt, state_ret_sample, k_prompt, v_prompt, k_sample, v_sample)


_drawn_inputs = setup_inputs


def setup_inputs(seed=0):
    import zlib

    import numpy as np

    out = dict(_drawn_inputs(seed))
    spreads = {}
    factors = {'diff_subln_g': 65.531}
    for name, (base, spread) in spreads.items():
        noise = np.random.default_rng([zlib.crc32(name.encode()), seed]).standard_normal(out[name].shape)
        drawn = base * np.exp(spread * noise) if base else spread * noise
        out[name] = __import__('jax').numpy.asarray(drawn.astype(out[name].dtype))
    for name, factor in factors.items():
        out[name] = (out[name] * factor).astype(out[name].dtype)
    return out
```

```python
import math
from contextlib import ExitStack

import numpy as np

import concourse.bass as bass
from concourse import mybir

F32 = mybir.dt.float32
F32R = mybir.dt.float32r
I32 = mybir.dt.int32
ACT = mybir.ActivationFunctionType
ALU = mybir.AluOpType
AX = mybir.AxisListType

P = 128
D = 1024
SEQ = 512
DEC = 8
T = SEQ + DEC
HALF = T // 2
KT = D // P
FFN = 2816
FT = FFN // P
DEPTH = 2
PAST = 1024
PAGE = 128
NPG = PAST // PAGE
RH = 4
DK = D // RH
DV = 2 * DK
DH = 64
NH = 8
TB = SEQ // P
BUCKETS = 32
EPS = 1e-5
ALPHA = (2.0 * DEPTH) ** 0.25
LAMBDA_INIT = 0.8 - 0.6 * math.exp(-0.3)
MASKED = -1e30

UC = 256
UK = 8
USZ = UK * UC
LINE = 640

STAGES = [("in0", 22), ("out0", 12), ("ret_in", 24), ("ret_out", 8), ("in1", 22), ("out1", 12),
          ("in2", 22), ("out2", 12), ("q", 4), ("kv", 8), ("o", 4), ("in3", 22), ("out3", 12)]
UB, UNITS = {}, 0
for _name, _nu in STAGES:
    UB[_name] = UNITS
    UNITS += _nu


def trunk_kernel(nc, x_t, w_in, w_out, w_ret_in, w_ret_out, w_q, w_kv, w_o, ln_g, ln_b, state,
                 cache_kt, cache_v, pages, lam_vecs, subln_g, rel_bias,
                 identity, rope, ret_tab, onehot_line, line_mask, onehot_past,
                 y_t, state_p, state_s, k_t, v_p, v_s, bias_rep, v_rows):
    ctx = ExitStack()
    with ctx:
        base = [(nc.sbuf_base + 31) // 32 * 32]

        def at(name, shape, dt, off):
            return nc.alloc_sbuf_tensor_at(name, shape, dt, offset=off)

        def size(shape):
            return int(np.prod(shape[1:])) * 4

        def new(name, shape, dt=F32):
            off = base[0]
            base[0] += (size(shape) + 31) // 32 * 32
            return at(name, shape, dt, off)

        def sem(name):
            return ctx.enter_context(nc.semaphore(name))

        WR = new("WR", [P, 2, UK, UC])
        WH = new("WH", [P, 2, UK, UC], F32R)
        WL = new("WL", [P, 2, UK, UC], F32R)
        XH = new("XH", [P, KT, T], F32R)
        XL = new("XL", [P, KT, T], F32R)
        off_hh = base[0]
        HH = new("HH", [P, FT, T], F32R)
        off_hl = base[0]
        HL = new("HL", [P, FT, T], F32R)
        off_x = base[0]
        X = new("X", [P, KT, T])
        off_ft = base[0]
        SG = new("SG", [P, 2, T])
        HF = new("HF", [P, 2, T])
        IDN = new("IDN", [P, P])
        ONES = new("ONES", [P, P])
        LNG = new("LNG", [P, 6, KT])
        LNB = new("LNB", [P, 6, KT])
        COL = new("COL", [P, 16])
        BD = new("BD", [P, NPG, NH, 2])
        BN = new("BN", [P, NH, 2])
        PTAB = new("PTAB", [1, DEC * NPG], I32)
        off_sp = base[0]
        EPS_LN, EPS_1, SUBG, NLAM, LAMW = (COL[:, i:i + 1] for i in range(5))
        DOT, EXPD = COL[:, 6:8], COL[:, 8:10]
        SQ = SG
        RS = at("RS", [P, T], F32, off_ft + 2 * T * 4)
        ACC = at("ACC", [P, T], F32, off_ft + 3 * T * 4)

        OHL = at("OHL", [BUCKETS, LINE], F32, off_hh)
        LMASK = at("LMASK", [NH, LINE], F32, off_hh + 2560)
        OHP = at("OHP", [BUCKETS, NPG + 1, P], F32, off_hh + 5120)
        RB = at("RB", [BUCKETS, NH], F32, off_hh + 9728)
        LN8 = at("LN8", [NH, LINE], F32, off_hh + 9792)
        LV = at("LV", [P, 4, DH], F32, off_hh + 12352)
        LPR = at("LPR", [P, 2, DH], F32, off_hh + 13376)

        VBC = at("VBC", [P, DEC, DV], F32, off_hh)
        VT = at("VT", [P, 4, T], F32, off_hh + 16384)
        RO = at("RO", [P, 4, T], F32, off_hh + 16384)
        GT = at("GT", [P, 4, T], F32, off_hh + 24704)
        VTK = at("VTK", [P, TB, DV], F32, off_hh + 33024)
        KTK = at("KTK", [P, TB, DK], F32, off_hh + 41216)
        OG = at("OG", [P, 4 * RH, T], F32, off_hl)
        SB = at("SB", [P, 2, 2, DV], F32, off_hl + 4 * RH * T * 4)
        TMP = at("TMP", [P, 2, DV], F32, off_hl + 4 * RH * T * 4 + 8192)
        RQ = at("RQ", [P, 2, T], F32, off_x)
        RK = at("RK", [P, 2, T], F32, off_x + 4160)
        RT = at("RT", [P, T], F32, off_x + 8320)
        PT = at("PT", [P, 1280], F32, off_x + 10400)
        COS = at("COS", [P, T], F32, off_sp)
        SIN = at("SIN", [P, T], F32, off_sp + 2080)
        SPR = at("SPR", [P, 2, DV], F32, off_sp + 4160)
        V8 = at("V8", [DEC, DV], F32, off_sp + 8256)
        RX = at("RX", [P, 2, T], F32, off_ft)
        RA = at("RA", [P, 2, T], F32, off_ft + 4160)

        QT = at("QT", [P, NH, T], F32, off_hh)
        KTT = at("KTT", [P, NH, T], F32, off_hh + 16640)
        WT = at("WT", [P, TB, SEQ], F32, off_hh + 33280)
        STRIP = at("STRIP", [P, 2, SEQ], F32, off_hh + 41472)
        OF = at("OF", [P, NH, T], F32, off_hl)
        o = off_hl + 16640
        VTOK = at("VTOK", [P, TB, D], F32, o)
        SS = at("SS", [P, 2, SEQ], F32, o + 16384)
        WW = at("WW", [P, SEQ], F32, o + 20480)
        QHD = at("QHD", [P, SEQ], F32, o + 22528)
        KHD = at("KHD", [P, SEQ], F32, o + 24576)
        VHD = at("VHD", [P, TB, P], F32, o + 26624)
        PG = at("PG", [P, 4, D], F32, off_x)
        SCA = at("SCA", [P, DEC, NPG, 2 * NH], F32, off_sp)
        QB = at("QB", [P, DEC, NH, 2], F32, off_sp + 4096)
        VN = at("VN", [P, NH, DEC], F32, off_sp + 4608)
        ST = at("ST", [P, 16], F32, off_sp + 4864)
        V8D = at("V8D", [DEC, D], F32, off_sp + 4928)
        VS = at("VS", [P, 2, T], F32, off_ft)
        small = [at(f"DS{i}", [P, P], F32, off_ft + 512 * i) for i in range(8)]
        M1, DG, PRD, SN, MB, SUMS, RC, WN = small
        WD = at("WD", [P, DEC, NPG, NH], F32, off_ft + 4160)
        end = max(off_sp + 8256 + DV * 4, off_sp + 4928 + D * 4)
        assert end <= nc.sbuf_usable_end, end - nc.sbuf_usable_end

        PS = ctx.enter_context(nc.psum_tensor("PS", [P, 8, 512], F32))

        raw_loaded = [sem("raw_loaded0"), sem("raw_loaded1")]
        hi_ready = sem("hi_ready")
        lo_ready = sem("lo_ready")
        half_done = sem("half_done")
        gate_ready = [sem("gate_ready0"), sem("gate_ready1")]
        h_ready = [sem("h_ready0"), sem("h_ready1")]
        hh_ready = sem("hh_ready")
        hl_ready = sem("hl_ready")
        y_ready = sem("y_ready")
        acc_ready = sem("acc_ready")
        mean_ready = sem("mean_ready")
        cent_ready = sem("cent_ready")
        sq_ready = sem("sq_ready")
        sqm_done = sem("sqm_done")
        ln_step = sem("ln_step")
        rs_ready = sem("rs_ready")
        scaled = sem("scaled")
        xh_ready = sem("xh_ready")
        x_ready = sem("x_ready")
        xl_ready = sem("xl_ready")
        x_loaded = sem("x_loaded")
        const_loaded = sem("const_loaded")
        ones_ready = sem("ones_ready")
        line_mm = sem("line_mm")
        line_sb = sem("line_sb")
        line_out = sem("line_out")
        bd_mm = sem("bd_mm")
        bd_ready = sem("bd_ready")
        lam_step = sem("lam_step")
        lam_exp = sem("lam_exp")
        rope_in = [sem("rope_in0"), sem("rope_in1")]
        rope_step = sem("rope_step")
        v_ready = [sem("v_ready0"), sem("v_ready1")]
        g_ready = [sem("g_ready0"), sem("g_ready1")]
        rt_loaded = sem("rt_loaded")
        ktr_done = sem("ktr_done")
        ktk_ready = sem("ktk_ready")
        vtr_done = sem("vtr_done")
        vtk_ready = sem("vtk_ready")
        v8_mm = sem("v8_mm")
        v8_ready = sem("v8_ready")
        v8_out = sem("v8_out")
        vbc_loaded = sem("vbc_loaded")
        rsc_done = sem("rsc_done")
        pt_ready = sem("pt_ready")
        ro_done = sem("ro_done")
        ro_ready = sem("ro_ready")
        rst_done = sem("rst_done")
        spr_ready = sem("spr_ready")
        spr_out = sem("spr_out")
        s0_loaded = [sem("s0_loaded0"), sem("s0_loaded1")]
        kv_ready = sem("kv_ready")
        sn_ready = sem("sn_ready")
        snq_done = sem("snq_done")
        s_out = [sem("s_out0"), sem("s_out1")]
        rod_ready = sem("rod_ready")
        rn_sum = sem("rn_sum")
        rn_mean = sem("rn_mean")
        rn_cent = sem("rn_cent")
        rn_sq = sem("rn_sq")
        rn_sqm = sem("rn_sqm")
        rn_step = sem("rn_step")
        rn_rs = sem("rn_rs")
        rn_mul = sem("rn_mul")
        rn_done = sem("rn_done")
        og_hi = sem("og_hi")
        og_lo = sem("og_lo")
        q_ready = [sem("q_ready0"), sem("q_ready1")]
        k_ready = [sem("k_ready0"), sem("k_ready1")]
        k_out = sem("k_out")
        qb_zero = sem("qb_zero")
        qb_ready = sem("qb_ready")
        vs_ready = [sem("vs_ready0"), sem("vs_ready1")]
        vn_ready = sem("vn_ready")
        dvt_done = sem("dvt_done")
        dvt_ready = sem("dvt_ready")
        v8d_done = sem("v8d_done")
        v8d_ready = sem("v8d_ready")
        v_out = sem("v_out")
        head_copied = sem("head_copied")
        strip_loaded = [sem("strip_loaded0"), sem("strip_loaded1")]
        sc_done = sem("sc_done")
        ss_ready = sem("ss_ready")
        mx_ready = sem("mx_ready")
        ex_ready = sem("ex_ready")
        rc_ready = sem("rc_ready")
        s0n_ready = sem("s0n_ready")
        ww_ready = sem("ww_ready")
        wtr_done = sem("wtr_done")
        wt_ready = sem("wt_ready")
        pv_done = sem("pv_done")
        of_ready = sem("of_ready")
        pt_loaded = sem("pt_loaded")
        page_loaded = [sem(f"page_loaded{i}") for i in range(4)]
        page_used = [sem(f"page_used{i}") for i in range(4)]
        sca_ready = sem("sca_ready")
        pagemax_ready = sem("pagemax_ready")
        pagemax_turned = sem("pagemax_turned")
        maxdiag_ready = sem("maxdiag_ready")
        max_spread = sem("max_spread")
        newprod_ready = sem("newprod_ready")
        newscore_done = sem("newscore_done")
        shifted = sem("shifted")
        dec_exp = sem("dec_exp")
        pagesum_ready = sem("pagesum_ready")
        sum_spread = sem("sum_spread")
        wd_ready = sem("wd_ready")
        soft_step = sem("soft_step")
        res_done = [sem("res_done0"), sem("res_done1")]
        acc_zero = sem("acc_zero")
        dof_ready = sem("dof_ready")
        new_step = sem("new_step")
        on_sq = sem("on_sq")
        on_mm = sem("on_mm")
        on_step = sem("on_step")
        on_rs = sem("on_rs")
        on_mul = sem("on_mul")
        on_hi = sem("on_hi")
        on_lo = sem("on_lo")
        y_out = sem("y_out")

        block = ctx.enter_context(nc.Block())

        def halves(ap):
            return ap.rearrange("p (h c) -> p h c", h=2)

        def tile_ps(c):
            return PS[:, 2 * c:2 * c + 2, 0:HALF]

        def strip_at(jb):
            return sum(SEQ - P * j for j in range(jb))

        @block.sync
        def _(sp):
            sp.dma_start(X[:, :, :], x_t).then_inc(x_loaded, 16)

            def load(src, u, r, nk):
                sp.wait_ge(lo_ready, u * 2 + r)
                sp.dma_start(WR[:, r, 0:nk, :], src).then_inc(raw_loaded[r], 16)

            def ffn_loads(n):
                u_in, u_out = UB[f"in{n}"] // 2, UB[f"out{n}"] // 2
                with sp.Fori(0, 11) as i:
                    for r in range(2):
                        load(w_in[bass.ds(i * 2 + (22 * n + r), 1)].rearrange("a p k c -> (a p) k c"),
                             i + u_in, r, UK)
                with sp.Fori(0, 2) as i:
                    for j in range(6):
                        k0 = UK * (j % 3)
                        nk = min(UK, FT - k0)
                        load(w_out[bass.ds(i * 2 + (4 * n + j // 3), 1)][:, :, k0:k0 + nk, :]
                             .rearrange("a p k c -> (a p) k c"), i * 3 + (u_out + j // 2), j % 2, nk)

            def plain_loads(w, stage, n):
                u0 = UB[stage] // 2
                with sp.Fori(0, n // 2) as i:
                    for r in range(2):
                        load(w[bass.ds(i * 2 + r, 1)].rearrange("a p k c -> (a p) k c"), i + u0, r, UK)

            ffn_loads(0)
            plain_loads(w_ret_in, "ret_in", 24)
            with sp.Fori(0, 4) as i:
                for r in range(2):
                    load(w_ret_out[bass.ds(i, 1)][:, :, UK * r:UK * r + UK, :]
                         .rearrange("a p k c -> (a p) k c"), i + UB["ret_out"] // 2, r, UK)
            ffn_loads(1)
            ffn_loads(2)
            plain_loads(w_q, "q", 4)
            plain_loads(w_kv, "kv", 8)
            for r in range(2):
                load(w_o[r], UB["o"] // 2, r, UK)
            sp.dma_start(PTAB[:, :], pages).then_inc(pt_loaded, 16)
            sp.wait_ge(pt_loaded, 16)
            sp.wait_ge(v_out, 16 * (TB + 1))
            with sp.Fori(0, DEC) as b:
                for pg in range(NPG):
                    s = pg % 4
                    sp.wait_ge(page_used[s], b * 2 + pg // 4)
                    page = sp.value_load(PTAB[0:1, bass.ds(b * NPG + pg, 1)], min_val=0,
                                         max_val=cache_kt.shape[0] - 1)
                    sp.dma_start(PG[:, s, :], cache_kt[bass.ds(page, 1)].rearrange("a p c -> (a p) c")
                                 ).then_inc(page_loaded[s], 16)
            with sp.Fori(0, DEC) as b:
                for pg in range(NPG):
                    s = pg % 4
                    sp.wait_ge(page_used[s], b * 2 + (16 + pg // 4))
                    page = sp.value_load(PTAB[0:1, bass.ds(b * NPG + pg, 1)], min_val=0,
                                         max_val=cache_v.shape[0] - 1)
                    sp.dma_start(PG[:, s, :], cache_v[bass.ds(page, 1)].rearrange("a p c -> (a p) c")
                                 ).then_inc(page_loaded[s], 16)
            for r in range(2):
                load(w_o[2 + r], UB["o"] // 2 + 1, r, UK)
            ffn_loads(3)

        @block.gpsimd
        def _(pool):
            pool.memset(ONES[:, :], 1.0).then_inc(ones_ready, 1)
            pool.memset(COL[:, 0:1], EPS / ALPHA ** 2).then_inc(ones_ready, 1)
            pool.memset(COL[:, 1:2], EPS).then_inc(ones_ready, 1)
            for dst, src in ((IDN[:, :], identity), (LNG[:, :, :], ln_g), (LNB[:, :, :], ln_b),
                             (OHL[:, :], onehot_line), (LMASK[:, :], line_mask), (OHP[:, :, :], onehot_past),
                             (RB[:, :], rel_bias), (COL[:, 2:3], subln_g), (LV[:, :, :], lam_vecs),
                             (COS[:, :], rope[0]), (SIN[:, :], rope[1])):
                pool.dma_start(dst, src).then_inc(const_loaded, 16)
            pool.wait_ge(line_sb, 1)
            pool.dma_start(bias_rep.rearrange("h (p c) -> h p c", p=P),
                           LN8[:, :].unsqueeze(1).to_broadcast([NH, P, LINE])).then_inc(line_out, 16)
            pool.wait_ge(line_out, 16)

            def strip(h):
                return (bias_rep[bass.ds(h, 1), P - 1:P - 1 + P * (LINE - 1)]
                        .rearrange("a (p c) -> (a p) c", p=P)[:, 0:SEQ])

            for h in range(RH):
                pool.wait_ge(sn_ready, h * 16)
                pool.wait_ge(x_ready, KT)
                pool.wait_ge(xl_ready, KT * 2)
                pool.dma_start(RT[:, :], ret_tab[bass.ds(h, 1)].rearrange("a p c -> (a p) c")
                               ).then_inc(rt_loaded, 16)
                for b in range(DEC):
                    s = b % 2
                    pool.wait_ge(s_out[s], h * 64 + 16 * (b // 2))
                    if b < 2:
                        pool.wait_ge(snq_done, h * 8)
                        pool.wait_ge(half_done, 2 * UB["ret_in"])
                    else:
                        pool.wait_ge(snq_done, h * 8 + (b - 1))
                    pool.dma_start(SB[:, s, :, :], state[b, bass.ds(h, 1)].rearrange("a p t e -> (a p) t e")
                                   ).then_inc(s0_loaded[s], 16)
                    if b == 1:
                        pool.wait_ge(v8_ready, h + 1)
                        pool.dma_start(v_rows, V8[:, :]).then_inc(v8_out, 16)
                        pool.wait_ge(v8_out, h * 16 + 16)
                        pool.wait_ge(kv_ready, h * 16)
                        pool.dma_start(VBC[:, :, :], bass.AP(tensor=v_rows.tensor, offset=v_rows.offset,
                                                             ap=[[0, P], [DV, DEC], [1, DV]])
                                       ).then_inc(vbc_loaded, 16)
                        pool.wait_ge(spr_ready, h * 2 + 2)
                        pool.dma_start(state_p[bass.ds(h, 1)].rearrange("a p t e -> (a p) t e"), SPR[:, :, :]
                                       ).then_inc(spr_out, 16)
                    if b >= 1:
                        pool.wait_ge(sn_ready, h * 16 + 2 * b)
                        pool.dma_start(state_s[b - 1, bass.ds(h, 1)].rearrange("a p t e -> (a p) t e"),
                                       SB[:, 1 - s, :, :]).then_inc(s_out[1 - s], 16)
                pool.wait_ge(sn_ready, h * 16 + 16)
                pool.dma_start(state_s[DEC - 1, bass.ds(h, 1)].rearrange("a p t e -> (a p) t e"),
                               SB[:, 1, :, :]).then_inc(s_out[1], 16)

            pool.wait_ge(half_done, 2 * UB["q"])
            pool.memset(QB[:, :, :, :], 0.0).then_inc(qb_zero, 1)
            for i in range(4):
                pool.wait_ge(k_ready[0], i + 1)
                pool.wait_ge(k_ready[1], i + 1)
                pool.dma_start(k_t[:, bass.ds(i * 2, 2), :], KTT[:, bass.ds(i * 2, 2), :]).then_inc(k_out, 16)
            pool.wait_ge(dvt_ready, 8 * TB // 2)
            for j in range(TB):
                pool.dma_start(v_p[j], VTOK[:, j, :]).then_inc(v_out, 16)
            pool.wait_ge(v8d_ready, 8)
            pool.dma_start(v_s, V8D[:, :]).then_inc(v_out, 16)
            for r in range(2):
                pool.dma_start(STRIP[:, r, :], strip(r)).then_inc(strip_loaded[r], 16)

            def head_pair(i, more):
                for r in range(2):
                    pool.wait_ge(pv_done, i * 2 + r)
                    for dst, src in ((QHD[:, :], QT[:, bass.ds(i * 2 + r, 1), 0:SEQ]),
                                     (KHD[:, :], KTT[:, bass.ds(i * 2 + r, 1), 0:SEQ])):
                        pool.tensor_copy(dst, src.rearrange("p a c -> p (a c)")).then_inc(head_copied, 1)
                    pool.tensor_copy(VHD[:, :, :], VTOK[:, :, bass.ds(i * (2 * P) + r * P, P)]
                                     ).then_inc(head_copied, 1)
                    if more:
                        pool.wait_ge(ss_ready, i * 16 + 8 * (r + 1))
                        pool.dma_start(STRIP[:, r, :], strip(i * 2 + (r + 2))).then_inc(strip_loaded[r], 16)

            for i in range(NH // 2):
                head_pair(i, i < NH // 2 - 1)
            pool.wait_ge(x_ready, 6 * KT)
            pool.dma_start(y_t, X[:, :, :]).then_inc(y_out, 16)
            for r in range(2):
                pool.wait_ge(strip_loaded[r], 16 * (NH // 2))
                pool.wait_ge(s_out[r], 16 * RH * 4)
            pool.wait_ge(spr_out, 16 * RH)
            pool.wait_ge(k_out, 16 * 4)
            pool.wait_ge(v_out, 16 * (TB + 1))
            pool.wait_ge(v8_out, 16 * RH)
            pool.wait_ge(y_out, 16)

        @block.tensor
        def _(pe):
            def unit(u, r, nk, k0, xh, xl, first, last, free):
                pe.wait_ge(lo_ready, u + 2)
                for c in range(2):
                    if first and free:
                        pe.wait_ge(free[0][c], free[1])
                    for k in range(nk):
                        for w, a, n in ((WH, xh, 0), (WH, xl, 1), (WL, xh, 2)):
                            for h in range(2):
                                mm = pe.matmul(PS[:, 2 * c + h, 0:HALF], w[:, r, k, c * P:c * P + P],
                                               a[:, k0 + k, h * HALF:(h + 1) * HALF],
                                               start=(first and k == 0 and n == 0),
                                               stop=(last and k == nk - 1 and n == 2))
                    mm.then_inc(half_done, 1)

            def plain(stage, n, ready, base):
                with pe.Fori(0, n // 2) as i:
                    for r in range(2):
                        unit(i * 2 + (UB[stage] + r), r, UK, 0, XH, XL, True, True, (ready, i * 2 + (base + r)))

            def ffn(n, ln):
                pe.wait_ge(xl_ready, KT * (ln + 1))
                with pe.Fori(0, 11) as i:
                    unit(i * 2 + UB[f"in{n}"], 0, UK, 0, XH, XL, True, True, (h_ready, i + 11 * n))
                    unit(i * 2 + (UB[f"in{n}"] + 1), 1, UK, 0, XH, XL, True, True, (gate_ready, i + (11 * n + 1)))
                pe.wait_ge(hl_ready, FT * (n + 1))
                with pe.Fori(0, 2) as i:
                    for j in range(6):
                        k0 = UK * (j % 3)
                        unit(i * 6 + (UB[f"out{n}"] + j), j % 2, min(UK, FT - k0), k0, HH, HL,
                             j % 3 == 0, j % 3 == 2, (res_done, i * 2 + (4 * ln + j // 3)))

            def layer_norm(n):
                pe.wait_ge(acc_ready, KT * (n + 1))
                for h in range(2):
                    mm = pe.matmul(PS[:, 4 + h, 0:HALF], ONES[:, :], ACC[:, h * HALF:(h + 1) * HALF],
                                   start=True, stop=True)
                mm.then_inc(mean_ready, 1)
                for d in range(KT):
                    pe.wait_ge(sq_ready, KT * n + d + 1)
                    for h in range(2):
                        mm = pe.matmul(PS[:, 6 + h, 0:HALF], ONES[:, :], SQ[:, d % 2, h * HALF:(h + 1) * HALF],
                                       start=(d == 0), stop=(d == KT - 1))
                    mm.then_inc(sqm_done, 1)

            pe.wait_ge(const_loaded, 16 * 11)
            pe.wait_ge(ones_ready, 3)
            for h in range(2):
                mm = pe.matmul(PS[0:NH, 4 + h, 0:LINE // 2], RB[:, :], OHL[:, h * (LINE // 2):(h + 1) * (LINE // 2)],
                               start=True, stop=True)
            mm.then_inc(line_mm, 1)
            for g in range(NPG + 1):
                mm = pe.matmul(PS[:, 6, g * NH:(g + 1) * NH], OHP[:, g, :], RB[:, :], start=True, stop=True)
            mm.then_inc(bd_mm, 1)

            ffn(0, 0)
            layer_norm(0)

            pe.wait_ge(xl_ready, KT * 2)
            with pe.Fori(0, RH) as h:
                for j in range(6):
                    free = ((g_ready, 0), (rope_in, 1), (rope_in, 2), (v_ready, 1), (v_ready, 2), (g_ready, 1))[j]
                    unit(h * 6 + (UB["ret_in"] + j), j % 2, UK, 0, XH, XL, True, True, (free[0], h * 2 + free[1]))
                pe.wait_ge(rope_step, h * 12 + 12)
                pe.wait_ge(rn_rs, h)
                pe.wait_ge(rn_cent, h * 4)
                for t in range(2):
                    for jb in range(TB):
                        mm = pe.transpose(PS[:, 4 + t, jb * P:(jb + 1) * P], RK[:, t, jb * P:(jb + 1) * P], IDN[:, :])
                    mm.then_inc(ktr_done, 1)
                pe.wait_ge(v_ready[0], h * 2 + 2)
                pe.wait_ge(v_ready[1], h * 2 + 2)
                for jb in range(TB):
                    if jb >= 2:
                        pe.wait_ge(vtk_ready, h * 4 + jb - 1)
                    for e in range(4):
                        mm = pe.transpose(PS[:, 6 + jb % 2, e * P:(e + 1) * P], VT[:, e, jb * P:(jb + 1) * P], IDN[:, :])
                    mm.then_inc(vtr_done, 1)
                pe.wait_ge(ktk_ready, h * 2 + 2)
                for e in range(4):
                    mm = pe.transpose(PS[0:DEC, 4, e * P:(e + 1) * P], VT[:, e, SEQ:T], IDN[:, :])
                mm.then_inc(v8_mm, 1)
                pe.wait_ge(vtk_ready, h * 4 + 4)
                pe.wait_ge(v8_ready, h + 1)
                for jb in range(TB):
                    for t in range(2):
                        mm = pe.matmul(PS[:, 4 + jb, 0:SEQ - P * jb], RK[:, t, jb * P:(jb + 1) * P],
                                       RQ[:, t, jb * P:SEQ], start=(t == 0), stop=(t == 1))
                    mm.then_inc(rsc_done, 1)
                pe.wait_ge(pt_ready, h * 4 + 4)
                for e in range(4):
                    for jb in range(TB):
                        mm = pe.matmul(PS[:, 4 + e, jb * P:SEQ], VTK[:, jb, e * P:(e + 1) * P],
                                       PT[:, strip_at(jb):strip_at(jb + 1)], start=(jb == 0), stop=(jb == TB - 1))
                    mm.then_inc(ro_done, 1)
                for t in range(2):
                    pe.wait_ge(ro_ready, h * 4 + t + 1)
                    for jb in range(TB):
                        mm = pe.matmul(PS[:, 4 + t, :], KTK[:, jb, t * P:(t + 1) * P], VTK[:, jb, :],
                                       start=(jb == 0), stop=(jb == TB - 1))
                    mm.then_inc(rst_done, 1)
                pe.wait_ge(ro_ready, h * 4 + 3)
                for b in range(DEC):
                    pe.wait_ge(sn_ready, h * 16 + 2 * b + 2)
                    for e in range(4):
                        for t in range(2):
                            mm = pe.matmul(PS[:, 6, e * DEC + b:e * DEC + b + 1], SB[:, b % 2, t, e * P:(e + 1) * P],
                                           RQ[:, t, SEQ + b:SEQ + b + 1], start=(t == 0), stop=(t == 1))
                    mm.then_inc(snq_done, 1)
                pe.wait_ge(rn_sum, h * 3 + 3)
                pe.wait_ge(spr_ready, h * 2 + 2)
                for g in range(2):
                    mm = pe.matmul(PS[:, 4 + g, 0:HALF], ONES[:, :], RA[:, 1, g * HALF:(g + 1) * HALF],
                                   start=True, stop=True)
                mm.then_inc(rn_mean, 1)
                pe.wait_ge(rod_ready, h + 1)
                pe.wait_ge(ro_ready, h * 4 + 4)
                for e in range(4):
                    pe.wait_ge(rn_sq, h * 4 + e + 1)
                    for g in range(2):
                        mm = pe.matmul(PS[:, 6 + g, 0:HALF], ONES[:, :], RX[:, e % 2, g * HALF:(g + 1) * HALF],
                                       start=(e == 0), stop=(e == 3))
                    mm.then_inc(rn_sqm, 1)
            pe.wait_ge(og_lo, 4 * RH)
            with pe.Fori(0, 4) as i:
                for r in range(2):
                    unit(i * 2 + (UB["ret_out"] + r), r, UK, UK * r, HH, HL, r == 0, r == 1, (res_done, i + 4))
            layer_norm(1)
            ffn(1, 2)
            layer_norm(2)
            ffn(2, 3)
            layer_norm(3)

            pe.wait_ge(xl_ready, KT * 5)
            plain("q", 4, q_ready, 0)
            for c in range(2):
                pe.wait_ge(q_ready[c], 4)
            plain("kv", 4, k_ready, 0)
            for c in range(2):
                pe.wait_ge(k_ready[c], 4)
            with pe.Fori(0, 2) as i:
                for r in range(2):
                    unit(i * 2 + (UB["kv"] + 4 + r), r, UK, 0, XH, XL, True, True, (vs_ready, i * 2 + r))
                    for c in range(2):
                        pe.wait_ge(vs_ready[c], i * 2 + (r + 1))
                        pe.wait_ge(dvt_ready, i * 8 + 4 * r + 2 * c)
                        for jb in range(TB):
                            mm = pe.transpose(PS[:, 4 + jb // 2, (jb % 2) * P:(jb % 2 + 1) * P],
                                              VS[:, c, jb * P:(jb + 1) * P], IDN[:, :])
                            if jb % 2:
                                mm.then_inc(dvt_done, 1)
                        pe.wait_ge(v8d_ready, i * 4 + 2 * r + c)
                        pe.transpose(PS[0:DEC, 6, 0:P], VS[:, c, SEQ:T], IDN[:, :]).then_inc(v8d_done, 1)
            pe.wait_ge(qb_ready, 2)
            pe.wait_ge(v8d_ready, 8)
            with pe.Fori(0, NH // 2) as i:
                for r in range(2):
                    pe.wait_ge(head_copied, i * 6 + 3 * r + 3)
                    for qb in range(TB):
                        n = qb + 4 * r
                        kw = (qb + 1) * P
                        pe.wait_ge(ss_ready, i * 16 + 2 * n)
                        for m in range(2):
                            mm = pe.matmul(PS[:, 4 + m, 0:kw], QHD[m * DH:(m + 1) * DH, qb * P:(qb + 1) * P],
                                           KHD[m * DH:(m + 1) * DH, 0:kw], start=True, stop=True)
                        mm.then_inc(sc_done, 1)
                        for pg in (2 * qb, 2 * qb + 1):
                            pe.wait_ge(page_loaded[pg % 4], i * 64 + 32 * r + 16 * (pg // 4) + 16)
                            if pg == 0:
                                pe.wait_ge(sca_ready, i * 2 + r)
                            for hd in range(NH):
                                mm = pe.matmul(PS[:, 0, pg * 16 + 2 * hd:pg * 16 + 2 * hd + 2],
                                               PG[:, pg % 4, hd * P:(hd + 1) * P],
                                               QB[:, bass.ds(i * 2 + r, 1), hd, :].rearrange("p a m -> p (a m)"),
                                               start=True, stop=True)
                            mm.then_inc(page_used[pg % 4], 1)
                        pe.wait_ge(ww_ready, i * 8 + n + 1)
                        pe.wait_ge(wt_ready, i * 8 + n)
                        for kb in range(qb + 1):
                            mm = pe.transpose(PS[:, 6, kb * P:(kb + 1) * P], WW[:, kb * P:(kb + 1) * P], IDN[:, :])
                        mm.then_inc(wtr_done, 1)
                    pe.wait_ge(wt_ready, i * 8 + 4 * r + 4)
                    pe.wait_ge(of_ready, i * 2 + r)
                    for kb in range(TB):
                        mm = pe.matmul(PS[:, 7, kb * P:SEQ], VHD[:, kb, :], WT[:, kb, kb * P:SEQ],
                                       start=(kb == 0), stop=(kb == TB - 1))
                    mm.then_inc(pv_done, 1)
            pe.wait_ge(pagemax_ready, 1)
            pe.wait_ge(ss_ready, 8 * NH)
            pe.transpose(PS[:, 4, 0:P], M1[:, :], IDN[:, :]).then_inc(pagemax_turned, 1)
            pe.wait_ge(maxdiag_ready, 1)
            pe.matmul(PS[:, 5, 0:P], ONES[:, :], DG[:, :], start=True, stop=True).then_inc(max_spread, 1)
            pe.wait_ge(newprod_ready, 1)
            pe.wait_ge(wt_ready, 4 * NH)
            for m in range(2):
                mm = pe.matmul(PS[:, (6, 2)[m], 0:DEC * NH], ONES[m * DH:(m + 1) * DH, :],
                               PRD[m * DH:(m + 1) * DH, 0:64], start=True, stop=True)
            mm.then_inc(newscore_done, 1)
            pe.wait_ge(pagesum_ready, 1)
            pe.wait_ge(of_ready, NH)
            pe.matmul(PS[:, 7, 0:P], ONES[:, :], SUMS[:, :], start=True, stop=True).then_inc(sum_spread, 1)
            pe.wait_ge(wd_ready, 1)
            with pe.Fori(0, DEC // 2) as i:
                for r in range(2):
                    pe.wait_ge(dof_ready, i * 2 + r)
                    for pg in range(NPG):
                        pe.wait_ge(page_loaded[pg % 4], i * 64 + 32 * r + (16 * (pg // 4) + 16 + 16 * 16))
                        for hd in range(NH):
                            mm = pe.matmul(PS[:, r, hd:hd + 1], PG[:, pg % 4, hd * P:(hd + 1) * P],
                                           WD[:, bass.ds(i * 2 + r, 1), pg, hd:hd + 1].rearrange("p a m -> p (a m)"),
                                           start=(pg == 0 and hd == 0), stop=(pg == NPG - 1),
                                           skip_group_check=True)
                        mm.then_inc(page_used[pg % 4], 1)
            for d in range(NH):
                pe.wait_ge(on_sq, d + 1)
                if d >= 1:
                    pe.wait_ge(on_rs, d)
                for g in range(2):
                    mm = pe.matmul(PS[:, 6 + g, 0:HALF], ONES[:, :], SG[:, d % 2, g * HALF:(g + 1) * HALF],
                                   start=True, stop=True)
                mm.then_inc(on_mm, 1)
            pe.wait_ge(on_lo, NH)
            with pe.Fori(0, 2) as i:
                for r in range(2):
                    unit(i * 2 + (UB["o"] + r), r, UK, 0, HH, HL, True, True, (res_done, i * 2 + (4 * 4 + r)))
            layer_norm(4)
            ffn(3, 5)
            layer_norm(5)

        @block.scalar
        def _(act):
            def ahead(half_u, r, first=False):
                act.wait_ge(raw_loaded[r], half_u * 16 + 16)
                if not first:
                    act.wait_ge(half_done, half_u * 4 + (2 * r - 2))
                act.activation(WH[:, r, :, :], WR[:, r, :, :], ACT.Copy).then_inc(hi_ready, 1)

            def ffn(n):
                u0 = UB[f"in{n}"] // 2
                with act.Fori(0, 11) as i:
                    for c in range(2):
                        act.wait_ge(half_done, i * 4 + (4 * u0 + c + 1))
                        act.wait_ge(h_ready[c], i + 11 * n)
                        act.activation(halves(SG[:, c, :]), tile_ps(c), ACT.Silu).then_inc(gate_ready[c], 1)
                    ahead(i + (u0 + 1), 0)
                    for c in range(2):
                        act.wait_ge(h_ready[c], i + (11 * n + 1))
                        act.activation(HH[:, bass.ds(i * 2 + c, 1), :].rearrange("p a c -> p (a c)"),
                                       HF[:, c, :], ACT.Copy).then_inc(hh_ready, 1)
                    ahead(i + (u0 + 1), 1)
                u0 = UB[f"out{n}"] // 2
                if n < 3:
                    with act.Fori(0, 2) as i:
                        for j in range(6):
                            ahead(i * 3 + (u0 + j // 2 + 1), j % 2)
                else:
                    for j in range(10):
                        ahead(u0 + j // 2 + 1, j % 2)

            def layer_norm(n):
                for d in range(KT):
                    act.wait_ge(cent_ready, KT * n + d + 1)
                    if d >= 2:
                        act.wait_ge(sqm_done, KT * n + d - 1)
                    act.activation(SQ[:, d % 2, :], X[:, d, :], ACT.Square).then_inc(sq_ready, 1)
                act.wait_ge(sqm_done, KT * (n + 1))
                act.activation(halves(RS[:, :]), PS[:, 6:8, 0:HALF], ACT.Ln, bias=EPS_LN, scale=1.0 / D).then_inc(ln_step, 1)
                act.wait_ge(ln_step, n + 1)
                act.activation(RS[:, :], RS[:, :], ACT.Exp, scale=-0.5).then_inc(rs_ready, 1)
                for d in range(KT):
                    act.wait_ge(scaled, KT * n + d + 1)
                    act.activation(XH[:, d, :], X[:, d, :], ACT.Identity, bias=LNB[:, n, d:d + 1]).then_inc(xh_ready, 1)
                    act.wait_ge(xh_ready, KT * (n + 1) + d + 1)
                    act.activation(X[:, d, :], X[:, d, :], ACT.Identity, bias=LNB[:, n, d:d + 1]).then_inc(x_ready, 1)

            act.wait_ge(x_loaded, 16)
            for d in range(KT):
                act.activation(XH[:, d, :], X[:, d, :], ACT.Copy).then_inc(xh_ready, 1)
            ahead(0, 0, True)
            ahead(0, 1, True)
            act.wait_ge(lam_step, 2)
            act.activation(EXPD, DOT, ACT.Exp).then_inc(lam_exp, 1)
            act.wait_ge(line_out, 16)
            act.wait_ge(bd_ready, 4)
            ffn(0)
            layer_norm(0)

            ub = UB["ret_in"] // 2
            with act.Fori(0, RH) as h:
                for j in range(6):
                    for c in range(2):
                        act.wait_ge(half_done, h * 12 + (4 * ub + 2 * j + c + 1))
                        if j < 2:
                            act.wait_ge(rope_step, h * 12 + 6 * j)
                            act.wait_ge(rn_sqm, h * 4)
                            a = act.activation(halves(RX[:, c, :]), tile_ps(c), ACT.Copy,
                                               scale=1.0 if j == 0 else DK ** -0.5)
                            a.then_inc(rope_in[c], 1)
                        elif j < 4:
                            act.wait_ge(rn_done, h * 4)
                            a = act.activation(halves(VT[:, 2 * (j - 2) + c, :]), tile_ps(c), ACT.Copy)
                            a.then_inc(v_ready[c], 1)
                        else:
                            act.wait_ge(rn_done, h * 4)
                            a = act.activation(halves(GT[:, 2 * (j - 4) + c, :]), tile_ps(c), ACT.Silu)
                            a.then_inc(g_ready[c], 1)
                    ahead(h * 3 + (ub + j // 2 + 1), j % 2)
                act.wait_ge(rt_loaded, h * 16 + 16)
                act.wait_ge(rst_done, h * 2)
                for t in range(2):
                    act.wait_ge(ktr_done, h * 2 + t + 1)
                    for jb in range(TB):
                        a = act.activation(KTK[:, jb, t * P:(t + 1) * P], PS[:, 4 + t, jb * P:(jb + 1) * P],
                                           ACT.Copy, scale=RT[:, SEQ + jb:SEQ + jb + 1])
                    a.then_inc(ktk_ready, 1)
                for jb in range(TB):
                    act.wait_ge(vtr_done, h * 4 + jb + 1)
                    act.activation(VTK[:, jb, :], PS[:, 6 + jb % 2, :], ACT.Copy).then_inc(vtk_ready, 1)
                act.wait_ge(v8_mm, h + 1)
                act.activation(V8[:, :], PS[0:DEC, 4, :], ACT.Copy).then_inc(v8_ready, 1)
                for e in range(4):
                    act.wait_ge(ro_done, h * 4 + e + 1)
                    act.activation(RO[:, e, 0:SEQ], PS[:, 4 + e, :], ACT.Copy).then_inc(ro_ready, 1)
                act.wait_ge(spr_out, h * 16)
                for t in range(2):
                    act.wait_ge(rst_done, h * 2 + t + 1)
                    act.activation(SPR[:, t, :], PS[:, 4 + t, :], ACT.Copy).then_inc(spr_ready, 1)
                act.wait_ge(vbc_loaded, h * 16 + 16)
                for b in range(DEC):
                    for t in range(2):
                        act.wait_ge(sn_ready, h * 16 + max(0, 2 * b + t - 1))
                        act.activation(TMP[:, t, :], VBC[:, b, :], ACT.Copy,
                                       scale=RK[:, t, SEQ + b:SEQ + b + 1]).then_inc(kv_ready, 1)
                act.wait_ge(snq_done, h * 8 + 8)
                act.activation(RO[:, :, SEQ:T], PS[:, 6, 0:4 * DEC].rearrange("p (e b) -> p e b", e=4),
                               ACT.Copy).then_inc(rod_ready, 1)
                for e in range(4):
                    act.wait_ge(rn_cent, h * 4 + e + 1)
                    act.wait_ge(rope_step, h * 12 + 12)
                    if e >= 2:
                        act.wait_ge(rn_sqm, h * 4 + e - 1)
                    act.activation(RX[:, e % 2, :], RO[:, e, :], ACT.Square).then_inc(rn_sq, 1)
                act.wait_ge(rn_sqm, h * 4 + 4)
                act.activation(halves(RA[:, 0, :]), PS[:, 6:8, 0:HALF], ACT.Ln, bias=EPS_1, scale=1.0 / DV).then_inc(rn_step, 1)
                act.wait_ge(rn_step, h + 1)
                act.activation(RA[:, 0, :], RA[:, 0, :], ACT.Exp, scale=-0.5).then_inc(rn_rs, 1)
            act.wait_ge(rn_done, 4 * RH)
            act.wait_ge(kv_ready, 16 * RH)
            for d in range(4 * RH):
                act.activation(HH[:, d, :], OG[:, d, :], ACT.Copy).then_inc(og_hi, 1)
            u0 = UB["ret_out"] // 2
            with act.Fori(0, 4) as i:
                for r in range(2):
                    ahead(i + (u0 + 1), r)
            layer_norm(1)
            ffn(1)
            layer_norm(2)
            ffn(2)
            layer_norm(3)

            uq, uk = UB["q"] // 2, UB["kv"] // 2
            with act.Fori(0, 2) as i:
                for r in range(2):
                    for c in range(2):
                        act.wait_ge(half_done, i * 4 + (4 * uq + 2 * r + c + 1))
                        a = act.activation(QT[:, bass.ds(i * 4 + (2 * r + c), 1), :].rearrange("p a (h c) -> p (a h) c", h=2),
                                           tile_ps(c), ACT.Copy)
                        a.then_inc(q_ready[c], 1)
                    ahead(i + (uq + 1), r)
            with act.Fori(0, 2) as i:
                for r in range(2):
                    for c in range(2):
                        act.wait_ge(half_done, i * 4 + (4 * uk + 2 * r + c + 1))
                        a = act.activation(KTT[:, bass.ds(i * 4 + (2 * r + c), 1), :].rearrange("p a (h c) -> p (a h) c", h=2),
                                           tile_ps(c), ACT.Copy)
                        a.then_inc(k_ready[c], 1)
                    ahead(i + (uk + 1), r)
            with act.Fori(0, 2) as i:
                for r in range(2):
                    for c in range(2):
                        act.wait_ge(half_done, i * 4 + (4 * uk + 8 + 2 * r + c + 1))
                        kept = i * 4 if r == 0 else i * 4 + (c + 1)
                        act.wait_ge(v8d_done, kept)
                        act.wait_ge(vn_ready, kept)
                        a = act.activation(halves(VS[:, c, :]), tile_ps(c), ACT.Copy)
                        a.then_inc(vs_ready[c], 1)
                    ahead(i + (uk + 3), r)
            with act.Fori(0, NH // 2) as i:
                for r in range(2):
                    for qb in range(TB):
                        n = qb + 4 * r
                        kw = (qb + 1) * P
                        act.wait_ge(mx_ready, i * 8 + n + 1)
                        for m in range(2):
                            act.activation(SS[:, m, 0:kw], SS[:, m, 0:kw], ACT.Exp, bias=ST[:, m:m + 1],
                                           accum_out=ST[:, 2 + m:3 + m]).then_inc(ex_ready, 1)
                        act.wait_ge(wtr_done, i * 8 + n + 1)
                        if qb == 0:
                            act.wait_ge(pv_done, i * 2 + r)
                        act.activation(WT[:, 0:qb + 1, qb * P:(qb + 1) * P],
                                       PS[:, 6, 0:kw].rearrange("p (k c) -> p k c", c=P), ACT.Copy).then_inc(wt_ready, 1)
                    act.wait_ge(pv_done, i * 2 + r + 1)
                    act.activation(OF[:, bass.ds(i * 2 + r, 1), 0:SEQ].rearrange("p a c -> p (a c)"), PS[:, 7, :],
                                   ACT.Copy).then_inc(of_ready, 1)
            act.wait_ge(shifted, 1)
            act.activation(SCA[:, :, :, :], SCA[:, :, :, :], ACT.Exp).then_inc(dec_exp, 1)
            act.wait_ge(shifted, 2)
            act.activation(SN[:, :], SN[:, :], ACT.Exp).then_inc(dec_exp, 1)
            act.wait_ge(new_step, 2)
            for d in range(NH):
                if d >= 2:
                    act.wait_ge(on_mm, d - 1)
                act.activation(SG[:, d % 2, :], OF[:, d, :], ACT.Square).then_inc(on_sq, 1)
                act.wait_ge(on_mm, d + 1)
                if d >= 2:
                    act.wait_ge(on_mul, d - 1)
                act.activation(halves(HF[:, d % 2, :]), PS[:, 6:8, 0:HALF], ACT.Ln, bias=EPS_1,
                               scale=1.0 / (2 * DH)).then_inc(on_step, 1)
                act.wait_ge(on_step, d + 1)
                act.activation(HF[:, d % 2, :], HF[:, d % 2, :], ACT.Exp, scale=-0.5).then_inc(on_rs, 1)
            for d in range(NH):
                act.wait_ge(on_mul, d + 1)
                act.activation(HH[:, d, :], OF[:, d, :], ACT.Copy).then_inc(on_hi, 1)
            u0 = UB["o"] // 2
            with act.Fori(0, 2) as i:
                for r in range(2):
                    ahead(i + (u0 + 1), r)
            layer_norm(4)
            ffn(3)
            layer_norm(5)

        @block.vector
        def _(dve):
            def ahead(half_u, r):
                dve.wait_ge(hi_ready, half_u * 2 + r + 1)
                dve.wait_ge(raw_loaded[r], half_u * 16 + 16)
                dve.tensor_tensor(WL[:, r, :, :], WR[:, r, :, :], WH[:, r, :, :].bitcast(F32), ALU.subtract
                                  ).then_inc(lo_ready, 1)

            def residual(d, pair, c, half, ln, scale, parts=False):
                x = X[:, bass.ds(d, 1), :].rearrange("p a (h c) -> p (a h) c", h=2)
                xf = X[:, bass.ds(d, 1), :].rearrange("p a c -> p (a c)")
                dve.wait_ge(half_done, half)
                if not parts:
                    dve.scalar_tensor_tensor(x, tile_ps(c), scale, x, ALU.mult, ALU.add).then_inc(res_done[c], 1)
                    dve.wait_ge(res_done[c], pair + (4 * ln + 1))
                else:
                    hi = XH[:, bass.ds(d, 1), :].bitcast(F32).rearrange("p a (h c) -> p (a h) c", h=2)
                    lo = XL[:, bass.ds(d, 1), :].bitcast(F32).rearrange("p a c -> p (a c)")
                    dve.scalar_tensor_tensor(x, tile_ps(c), scale, hi, ALU.mult, ALU.add).then_inc(res_done[c], 1)
                    dve.wait_ge(res_done[c], pair + (4 * ln + 1))
                    dve.tensor_tensor(xf, xf, lo, ALU.add).then_inc(y_ready, 1)
                    dve.wait_ge(y_ready, d + (KT * (ln // 4) + 1))
                dve.wait_ge(acc_ready, d + KT * ln)
                dve.tensor_tensor(ACC[:, :], ACC[:, :], xf, ALU.add).then_inc(acc_ready, 1)

            def clear_acc(ln):
                dve.memset(ACC[:, :], 0.0).then_inc(acc_zero, 1)
                dve.wait_ge(acc_zero, ln + 1)

            def layer_norm(n):
                dve.wait_ge(mean_ready, n + 1)
                for d in range(KT):
                    x = halves(X[:, d, :])
                    dve.scalar_tensor_tensor(x, PS[:, 4:6, 0:HALF], -1.0 / D, x, ALU.mult, ALU.add
                                             ).then_inc(cent_ready, 1)
                dve.wait_ge(rs_ready, n + 1)
                dve.wait_ge(cent_ready, KT * (n + 1))
                for d in range(KT + 1):
                    if d < KT:
                        dve.scalar_tensor_tensor(X[:, d, :], X[:, d, :], LNG[:, n, d:d + 1], RS[:, :],
                                                 ALU.mult, ALU.mult).then_inc(scaled, 1)
                    if d >= 1:
                        dve.wait_ge(x_ready, KT * n + d)
                        dve.tensor_tensor(XL[:, d - 1, :], X[:, d - 1, :], XH[:, d - 1, :].bitcast(F32),
                                          ALU.subtract).then_inc(xl_ready, 1)

            def ffn(n):
                u0 = UB[f"in{n}"] // 2
                with dve.Fori(0, 11) as i:
                    ahead(i + (u0 + 1), 0)
                    for c in range(2):
                        dve.wait_ge(half_done, i * 4 + (4 * u0 + c + 3))
                        dve.wait_ge(gate_ready[c], i + (11 * n + 1))
                        dve.wait_ge(hl_ready, i * 2 + (FT * n))
                        dve.tensor_tensor(halves(HF[:, c, :]), halves(SG[:, c, :]), tile_ps(c), ALU.mult
                                          ).then_inc(h_ready[c], 1)
                        dve.wait_ge(hh_ready, i * 2 + (FT * n + c + 1))
                        dve.tensor_tensor(HL[:, bass.ds(i * 2 + c, 1), :].rearrange("p a c -> p (a c)"), HF[:, c, :],
                                          HH[:, bass.ds(i * 2 + c, 1), :].rearrange("p a c -> p (a c)").bitcast(F32),
                                          ALU.subtract).then_inc(hl_ready, 1)
                    ahead(i + (u0 + 1), 1)
                u0 = UB[f"out{n}"] // 2
                ln = (0, 2, 3, 5)[n]
                dve.wait_ge(hl_ready, FT * (n + 1))
                clear_acc(ln)

                def pairs(i):
                    for j in range(6):
                        if j % 3 == 2:
                            for c in range(2):
                                d = 2 * (j // 3) + c
                                residual(i * 4 + d, i * 2 + j // 3, c, i * 12 + (4 * u0 + 2 * j + c + 1), ln, 0.5 / ALPHA)
                        if n < 3 or 6 * i + j < 10:
                            ahead(i * 3 + (u0 + j // 2 + 1), j % 2)

                if n < 3:
                    with dve.Fori(0, 2) as i:
                        pairs(i)
                else:
                    for i in range(2):
                        pairs(i)

            dve.memset(ACC[:, :], 0.0).then_inc(lo_ready, 1)
            dve.wait_ge(x_loaded, 16)
            for d in range(KT):
                dve.wait_ge(xh_ready, d + 1)
                dve.tensor_tensor(XL[:, d, :], X[:, d, :], XH[:, d, :].bitcast(F32), ALU.subtract).then_inc(xl_ready, 1)
            ahead(0, 0)
            ahead(0, 1)
            dve.wait_ge(const_loaded, 16 * 11)
            dve.tensor_tensor(LPR[:, :, :], LV[:, 0:4:2, :], LV[:, 1:4:2, :], ALU.mult).then_inc(lam_step, 1)
            dve.wait_ge(lam_step, 1)
            dve.tensor_reduce(DOT, LPR[:, :, :], AX.X, ALU.add).then_inc(lam_step, 1)
            dve.wait_ge(lam_exp, 1)
            dve.tensor_tensor(NLAM, EXPD[:, 1:2], EXPD[:, 0:1], ALU.subtract).then_inc(lam_step, 1)
            dve.wait_ge(lam_step, 3)
            dve.tensor_scalar(NLAM, NLAM, -LAMBDA_INIT, None, ALU.add).then_inc(lam_step, 1)
            dve.tensor_scalar(SUBG, SUBG, 1.0 - LAMBDA_INIT, None, ALU.mult).then_inc(lam_step, 1)
            dve.wait_ge(line_mm, 1)
            dve.tensor_tensor(LN8[:, :].rearrange("p (h c) -> p h c", h=2), PS[0:NH, 4:6, 0:LINE // 2],
                              LMASK[:, :].rearrange("p (h c) -> p h c", h=2), ALU.add).then_inc(line_sb, 1)
            dve.wait_ge(bd_mm, 1)
            for m in range(2):
                dve.tensor_copy(BD[:, :, :, m], PS[:, 6, 0:NPG * NH].rearrange("p (g h) -> p g h", h=NH)
                                ).then_inc(bd_ready, 1)
                dve.tensor_copy(BN[:, :, m], PS[:, 6, NPG * NH:(NPG + 1) * NH]).then_inc(bd_ready, 1)
            ffn(0)
            layer_norm(0)

            ub = UB["ret_in"] // 2
            with dve.Fori(0, RH) as h:
                for j in range(6):
                    if j < 2:
                        out = (RQ, RK)[j]
                        dve.wait_ge(rope_in[0], h * 2 + (j + 1))
                        dve.wait_ge(rope_in[1], h * 2 + (j + 1))
                        dve.wait_ge(rn_done, h * 4)
                        steps = ((RA[:, 0, :], RX[:, 0, :], COS[:, :], ALU.mult),
                                 (RA[:, 1, :], RX[:, 1, :], SIN[:, :], ALU.mult),
                                 (out[:, 0, :], RA[:, 0, :], RA[:, 1, :], ALU.subtract),
                                 (RA[:, 0, :], RX[:, 0, :], SIN[:, :], ALU.mult),
                                 (RA[:, 1, :], RX[:, 1, :], COS[:, :], ALU.mult),
                                 (out[:, 1, :], RA[:, 0, :], RA[:, 1, :], ALU.add))
                        for n, (dst, a, b, op) in enumerate(steps):
                            dve.wait_ge(rope_step, h * 12 + (6 * j + n))
                            dve.tensor_tensor(dst, a, b, op).then_inc(rope_step, 1)
                    ahead(h * 3 + (ub + j // 2 + 1), j % 2)
                dve.wait_ge(rt_loaded, h * 16 + 16)
                for jb in range(TB):
                    dve.wait_ge(rsc_done, h * 4 + jb + 1)
                    dve.tensor_tensor(PT[:, strip_at(jb):strip_at(jb + 1)], PS[:, 4 + jb, 0:SEQ - P * jb],
                                      RT[:, 0:SEQ - P * jb], ALU.mult).then_inc(pt_ready, 1)
                for b in range(DEC):
                    dve.wait_ge(s0_loaded[b % 2], h * 64 + 16 * (b // 2 + 1))
                    for t in range(2):
                        dve.wait_ge(kv_ready, h * 16 + (2 * b + t + 1))
                        dve.scalar_tensor_tensor(SB[:, b % 2, t, :], SB[:, b % 2, t, :], RT[:, SEQ + 4:SEQ + 5],
                                                 TMP[:, t, :], ALU.mult, ALU.add).then_inc(sn_ready, 1)
                dve.wait_ge(rod_ready, h + 1)
                dve.wait_ge(rope_step, h * 12 + 12)
                for e in range(1, 4):
                    dve.wait_ge(rn_sum, h * 3 + e - 1)
                    dve.tensor_tensor(RA[:, 1, :], RO[:, 0, :] if e == 1 else RA[:, 1, :], RO[:, e, :], ALU.add
                                      ).then_inc(rn_sum, 1)
                dve.wait_ge(rn_mean, h + 1)
                for e in range(4):
                    o_e = halves(RO[:, e, :])
                    dve.scalar_tensor_tensor(o_e, PS[:, 4:6, 0:HALF], -1.0 / DV, o_e, ALU.mult, ALU.add
                                             ).then_inc(rn_cent, 1)
                dve.wait_ge(rn_rs, h + 1)
                dve.wait_ge(rn_cent, h * 4 + 4)
                dve.wait_ge(g_ready[0], h * 2 + 2)
                dve.wait_ge(g_ready[1], h * 2 + 2)
                for e in range(4):
                    dve.tensor_tensor(RO[:, e, :], RO[:, e, :], RA[:, 0, :], ALU.mult).then_inc(rn_mul, 1)
                for e in range(4):
                    dve.wait_ge(rn_mul, h * 4 + e + 1)
                    dve.tensor_tensor(OG[:, bass.ds(h * 4 + e, 1), :].rearrange("p a c -> p (a c)"), RO[:, e, :],
                                      GT[:, e, :], ALU.mult).then_inc(rn_done, 1)
            for d in range(4 * RH):
                dve.wait_ge(og_hi, d + 1)
                dve.tensor_tensor(HL[:, d, :], OG[:, d, :], HH[:, d, :].bitcast(F32), ALU.subtract
                                  ).then_inc(og_lo, 1)
            clear_acc(1)
            u0 = UB["ret_out"] // 2
            with dve.Fori(0, 4) as i:
                ahead(i + (u0 + 1), 0)
                for c in range(2):
                    residual(i * 2 + c, i, c, i * 4 + (4 * u0 + 2 + c + 1), 1, 1.0 / ALPHA, True)
                ahead(i + (u0 + 1), 1)
            layer_norm(1)
            for r in range(2):
                dve.wait_ge(s_out[r], 16 * RH * DEC // 2)
            dve.wait_ge(spr_out, 16 * RH)
            ffn(1)
            layer_norm(2)
            ffn(2)
            layer_norm(3)

            uq, uk = UB["q"] // 2, UB["kv"] // 2
            with dve.Fori(0, 2) as i:
                for r in range(2):
                    ahead(i + (uq + 1), r)
            dve.wait_ge(q_ready[0], NH // 2)
            dve.wait_ge(q_ready[1], NH // 2)
            dve.wait_ge(qb_zero, 1)
            for m in range(2):
                dve.tensor_copy(QB[m * DH:(m + 1) * DH, :, :, m],
                                QT[m * DH:(m + 1) * DH, :, SEQ:T].rearrange("p h b -> p b h")).then_inc(qb_ready, 1)
            with dve.Fori(0, 2) as i:
                for r in range(2):
                    ahead(i + (uk + 1), r)
            with dve.Fori(0, 2) as i:
                for r in range(2):
                    for c in range(2):
                        n = 2 * r + c
                        dve.wait_ge(vs_ready[c], i * 2 + (r + 1))
                        dve.tensor_copy(VN[:, bass.ds(i * 4 + n, 1), :].rearrange("p a c -> p (a c)"),
                                        VS[:, c, SEQ:T]).then_inc(vn_ready, 1)
                        for g in range(2):
                            dve.wait_ge(dvt_done, i * 8 + (2 * n + g + 1))
                            dve.tensor_copy(VTOK[:, 2 * g:2 * g + 2, bass.ds(i * 512 + n * P, P)],
                                            PS[:, 4 + g, 0:2 * P].rearrange("p (j e) -> p j e", j=2)
                                            ).then_inc(dvt_ready, 1)
                        dve.wait_ge(v8d_done, i * 4 + (n + 1))
                        dve.tensor_copy(V8D[:, bass.ds(i * 512 + n * P, P)], PS[0:DEC, 6, 0:P]).then_inc(v8d_ready, 1)
                    ahead(i + (uk + 3), r)
            with dve.Fori(0, NH // 2) as i:
                for r in range(2):
                    dve.wait_ge(strip_loaded[r], i * 16 + 16)
                    for qb in range(TB):
                        n = qb + 4 * r
                        kw = (qb + 1) * P
                        j0 = SEQ - kw
                        dve.wait_ge(sc_done, i * 8 + (n + 1))
                        dve.wait_ge(ww_ready, i * 8 + n)
                        for m in range(2):
                            dve.scalar_tensor_tensor(SS[:, m, 0:kw], PS[:, 4 + m, 0:kw], DH ** -0.5,
                                                     STRIP[:, r, j0:j0 + kw], ALU.mult, ALU.add).then_inc(ss_ready, 1)
                        dve.wait_ge(ss_ready, i * 16 + (2 * n + 2))
                        dve.tensor_reduce(ST[:, 0:2], SS[:, :, 0:kw], AX.X, ALU.max, negate=True).then_inc(mx_ready, 1)
                        dve.wait_ge(ex_ready, i * 16 + (2 * n + 2))
                        dve.reciprocal(ST[:, 4:6], ST[:, 2:4]).then_inc(rc_ready, 1)
                        dve.wait_ge(rc_ready, i * 16 + (2 * n + 1))
                        dve.tensor_tensor(ST[:, 6:7], ST[:, 5:6], NLAM, ALU.mult).then_inc(rc_ready, 1)
                        dve.tensor_scalar(SS[:, 0, 0:kw], SS[:, 0, 0:kw], ST[:, 4:5], None, ALU.mult
                                          ).then_inc(s0n_ready, 1)
                        dve.wait_ge(rc_ready, i * 16 + (2 * n + 2))
                        dve.wait_ge(s0n_ready, i * 8 + (n + 1))
                        dve.wait_ge(wtr_done, i * 8 + n)
                        dve.scalar_tensor_tensor(WW[:, 0:kw], SS[:, 1, 0:kw], ST[:, 6:7], SS[:, 0, 0:kw],
                                                 ALU.mult, ALU.add).then_inc(ww_ready, 1)
                    dve.wait_ge(page_used[3], i * 4 + (2 * r + 2))
                    dve.scalar_tensor_tensor(
                        SCA[:, bass.ds(i * 2 + r, 1), :, :].rearrange("p a g m -> p (a g m)"), PS[:, 0, 0:P],
                        DH ** -0.5, BD[:, :, :, :].rearrange("p g h m -> p (g h m)"), ALU.mult, ALU.add
                    ).then_inc(sca_ready, 1)
            MC = COL[:, 10:11]

            def step(n):
                dve.wait_ge(soft_step, n)

            dve.wait_ge(sca_ready, DEC)
            dve.tensor_reduce(M1[:, :].rearrange("p (b m) -> p b m", b=DEC), SCA[:, :, :, :].rearrange("p b g m -> p b m g"),
                              AX.X, ALU.max).then_inc(pagemax_ready, 1)
            dve.tensor_tensor(PRD[:, 0:DEC * NH].rearrange("p (b h) -> p b h", b=DEC),
                              QT[:, :, SEQ:T].rearrange("p h b -> p b h"), KTT[:, :, SEQ:T].rearrange("p h b -> p b h"),
                              ALU.mult).then_inc(newprod_ready, 1)
            dve.wait_ge(pagemax_turned, 1)
            dve.tensor_reduce(MC, PS[:, 4, 0:P], AX.X, ALU.max).then_inc(soft_step, 1)
            step(1)
            dve.tensor_scalar(DG[:, :], IDN[:, :], MC, None, ALU.mult).then_inc(maxdiag_ready, 1)
            dve.wait_ge(newscore_done, 1)
            sn = SN[:, :].rearrange("p (b h m) -> p b h m", b=DEC, m=2)
            for m in range(2):
                dve.scalar_tensor_tensor(sn[:, :, :, m], PS[:, (6, 2)[m], 0:DEC * NH].rearrange("p (b h) -> p b h", b=DEC),
                                         DH ** -0.5, BN[:, :, m].unsqueeze(1).to_broadcast([P, DEC, NH]),
                                         ALU.mult, ALU.add).then_inc(soft_step, 1)
            step(3)
            dve.wait_ge(max_spread, 1)
            dve.tensor_tensor(MB[:, :], PS[:, 5, 0:P], SN[:, :], ALU.max).then_inc(soft_step, 1)
            step(4)

            def over_pages(t):
                return t[:, :].rearrange("p (b m) -> p b m", b=DEC).unsqueeze(2).to_broadcast([P, DEC, NPG, 2 * NH])

            dve.tensor_tensor(SCA[:, :, :, :], SCA[:, :, :, :], over_pages(MB), ALU.subtract).then_inc(shifted, 1)
            dve.tensor_tensor(SN[:, :], SN[:, :], MB[:, :], ALU.subtract).then_inc(shifted, 1)
            dve.wait_ge(dec_exp, 2)
            dve.tensor_reduce(SUMS[:, :].rearrange("p (b m) -> p b m", b=DEC),
                              SCA[:, :, :, :].rearrange("p b g m -> p b m g"), AX.X, ALU.add).then_inc(pagesum_ready, 1)
            dve.wait_ge(sum_spread, 1)
            dve.tensor_tensor(RC[:, :], PS[:, 7, 0:P], SN[:, :], ALU.add).then_inc(soft_step, 1)
            step(5)
            dve.reciprocal(RC[:, :], RC[:, :]).then_inc(soft_step, 1)
            step(6)
            rc1 = RC[:, :].rearrange("p (x m) -> p x m", m=2)[:, :, 1]
            dve.tensor_scalar(rc1, rc1, NLAM, None, ALU.mult).then_inc(soft_step, 1)
            step(7)
            dve.tensor_tensor(SCA[:, :, :, :], SCA[:, :, :, :], over_pages(RC), ALU.mult).then_inc(soft_step, 1)
            dve.tensor_tensor(SN[:, :], SN[:, :], RC[:, :], ALU.mult).then_inc(soft_step, 1)
            step(9)
            sca = SCA[:, :, :, :].rearrange("p b g (h m) -> p (b g h) m", m=2)
            dve.tensor_tensor(WD[:, :, :, :].rearrange("p b g h -> p (b g h)"), sca[:, :, 0], sca[:, :, 1], ALU.add
                              ).then_inc(wd_ready, 1)
            snx = SN[:, :].rearrange("p (x m) -> p x m", m=2)
            dve.tensor_tensor(WN[:, 0:DEC * NH], snx[:, :, 0], snx[:, :, 1], ALU.add).then_inc(soft_step, 1)
            with dve.Fori(0, DEC // 2) as i:
                for r in range(2):
                    dve.wait_ge(page_used[3], i * 4 + (2 * r + 2 + 2 * DEC))
                    dve.tensor_copy(OF[:, :, bass.ds(i * 2 + (SEQ + r), 1)].rearrange("p h a -> p (h a)"),
                                    PS[:, r, 0:NH]).then_inc(dof_ready, 1)
            step(10)
            own = M1[:, 0:DEC * NH].rearrange("p (h b) -> p h b", b=DEC)
            dve.tensor_tensor(own, WN[:, 0:DEC * NH].rearrange("p (b h) -> p h b", b=DEC), VN[:, :, :], ALU.mult
                              ).then_inc(new_step, 1)
            dve.wait_ge(new_step, 1)
            dve.wait_ge(dof_ready, DEC)
            dve.tensor_tensor(OF[:, :, SEQ:T], OF[:, :, SEQ:T], own, ALU.add).then_inc(new_step, 1)
            for d in range(NH):
                dve.wait_ge(on_rs, d + 1)
                dve.scalar_tensor_tensor(OF[:, d, :], OF[:, d, :], SUBG, HF[:, d % 2, :], ALU.mult, ALU.mult
                                         ).then_inc(on_mul, 1)
            for d in range(NH):
                dve.wait_ge(on_hi, d + 1)
                dve.tensor_tensor(HL[:, d, :], OF[:, d, :], HH[:, d, :].bitcast(F32), ALU.subtract).then_inc(on_lo, 1)
            clear_acc(4)
            u0 = UB["o"] // 2
            with dve.Fori(0, 2) as i:
                for r in range(2):
                    for c in range(2):
                        residual(i * 4 + (2 * r + c), i * 2 + r, c, i * 4 + (4 * u0 + 2 * r + c + 1), 4,
                                 1.0 / ALPHA, True)
                    ahead(i + (u0 + 1), r)
            layer_norm(4)
            ffn(3)
            layer_norm(5)


def shape_tables():
    f = np.float32
    identity = np.eye(P, dtype=f)
    half = DK // 2
    inv = f(10000.0) ** (-np.arange(half, dtype=f) / f(half))
    pos = np.concatenate([np.arange(SEQ), np.full(DEC, PAST)]).astype(f)
    ang = (inv[:, None] * pos[None, :]).astype(f).astype(np.float64)
    rope = np.stack([np.cos(ang), np.sin(ang)]).astype(f)
    gamma = 1.0 - 2.0 ** (-5.0 - np.arange(RH, dtype=np.float64))
    ret = np.zeros((RH, P, T), f)
    d = np.arange(SEQ)[None, :] - np.arange(P)[:, None]
    tok = np.arange(TB)[None, :] * P + np.arange(P)[:, None]
    for h in range(RH):
        ret[h, :, :SEQ] = np.where(d >= 0, gamma[h] ** np.maximum(d, 0), 0.0)
        ret[h, :, SEQ:SEQ + TB] = gamma[h] ** (SEQ - 1 - tok)
        ret[h, :, SEQ + TB] = gamma[h]

    def bucket(n):
        n = np.maximum(n, 0)
        exact = BUCKETS // 2
        nf = np.maximum(n, 1).astype(f)
        large = exact + (np.log(nf / f(exact)) / f(math.log(128 / exact)) * f(BUCKETS - exact)).astype(np.int32)
        return np.where(n < exact, n, np.minimum(large, BUCKETS - 1))

    n = SEQ - 1 - np.arange(LINE)
    line = (bucket(n)[None, :] == np.arange(BUCKETS)[:, None]).astype(f)
    mask = np.repeat(np.where(n < 0, MASKED, 0.0).astype(f)[None, :], NH, 0)
    n = PAST - np.arange(PAST).reshape(NPG, P)
    n = np.concatenate([n, np.zeros((1, P), n.dtype)])
    past = (bucket(n)[None] == np.arange(BUCKETS)[:, None, None]).astype(f)
    return identity, rope, ret, line, mask, past


def kernel(x_prompt, x_sample, state_ret, cache_k, cache_v, page_table, ln_g, ln_b, ffn_w_in, ffn_w_out,
           ret_w_in, ret_w_out, w_kv, diff_w_q, diff_w_o, diff_lambda, diff_subln_g, rel_bias):
    from concourse import bacc
    from concourse.bass_utils import run_bass_kernel_spmd

    def tiles(w):
        w = np.asarray(w)
        return np.ascontiguousarray(w.reshape(-1, P, w.shape[1] // UC, UC).transpose(2, 1, 0, 3))

    x = np.concatenate([np.asarray(x_prompt)[0], np.asarray(x_sample)[:, 0]])
    ffn_in = np.asarray(ffn_w_in).reshape(4, D, 2 * FFN)
    w_in = np.stack([tiles(w).reshape(2, FFN // UC, P, KT, UC).swapaxes(0, 1) for w in ffn_in])
    w_out = np.stack([tiles(w) for w in np.asarray(ffn_w_out).reshape(4, FFN, D)])
    r = tiles(np.asarray(ret_w_in)[0])
    r = np.stack([np.stack([r[h], r[4 + h], r[8 + 2 * h], r[9 + 2 * h], r[16 + 2 * h], r[17 + 2 * h]])
                  for h in range(RH)])
    n_pool = np.asarray(cache_k).shape[0]
    identity, rope, ret, line, mask, past = shape_tables()
    arrays = {
        "x_t": x.T.reshape(KT, P, T).swapaxes(0, 1),
        "w_in": w_in.reshape(88, P, KT, UC),
        "w_out": w_out.reshape(16, P, FT, UC),
        "w_ret_in": r.reshape(24, P, KT, UC),
        "w_ret_out": tiles(np.asarray(ret_w_out)[0]),
        "w_q": tiles(np.asarray(diff_w_q)[0]),
        "w_kv": tiles(w_kv),
        "w_o": tiles(np.asarray(diff_w_o)[0]),
        "ln_g": np.asarray(ln_g).reshape(6, KT, P).transpose(2, 0, 1),
        "ln_b": np.asarray(ln_b).reshape(6, KT, P).transpose(2, 0, 1),
        "state": np.asarray(state_ret)[0].reshape(DEC, RH, 2, P, DV).swapaxes(2, 3),
        "cache_kt": np.asarray(cache_k).transpose(0, 3, 2, 1).reshape(n_pool, P, NH * PAGE),
        "cache_v": np.asarray(cache_v).reshape(n_pool, PAGE, D),
        "pages": np.asarray(page_table).reshape(1, DEC * NPG),
        "lam_vecs": np.broadcast_to(np.asarray(diff_lambda)[0], (P, 4, DH)),
        "subln_g": np.asarray(diff_subln_g).reshape(P, 1),
        "rel_bias": np.asarray(rel_bias),
        "identity": identity, "rope": rope, "ret_tab": ret, "onehot_line": line, "line_mask": mask,
        "onehot_past": past,
    }
    arrays = {k: np.ascontiguousarray(v) for k, v in arrays.items()}
    nc = bacc.Bacc("TRN2", target_bir_lowering=False, num_devices=1)
    args = {k: nc.dram_tensor(k, v.shape, mybir.dt.from_np(v.dtype), kind="ExternalInput").ap()
            for k, v in arrays.items()}
    outs = {"y_t": (P, KT, T), "state_p": (RH, P, 2, DV), "state_s": (DEC, RH, P, 2, DV), "k_t": (P, NH, T),
            "v_p": (TB, P, D), "v_s": (DEC, D)}
    for k, shape in outs.items():
        args[k] = nc.dram_tensor(k, shape, F32, kind="ExternalOutput").ap()
    for k, shape in {"bias_rep": (NH, P * LINE), "v_rows": (DEC, DV)}.items():
        args[k] = nc.dram_tensor(k, shape, F32, kind="Internal").ap()
    trunk_kernel(nc, **args)
    r = run_bass_kernel_spmd(nc, [arrays], core_ids=[0]).results[0]
    y = r["y_t"].swapaxes(0, 1).reshape(D, T).T
    k = r["k_t"].transpose(2, 1, 0)
    return (y[None, :SEQ], y[SEQ:, None],
            r["state_p"].swapaxes(1, 2).reshape(1, 1, RH, DK, DV),
            r["state_s"].swapaxes(2, 3).reshape(1, DEC, RH, DK, DV),
            k[None, :SEQ], r["v_p"].reshape(1, SEQ, NH, 2 * DH),
            k[SEQ:, None], r["v_s"].reshape(DEC, 1, NH, 2 * DH))
```

```python
import math
from contextlib import ExitStack

import numpy as np

import concourse.bass as bass
from concourse import mybir

F32 = mybir.dt.float32
F32R = mybir.dt.float32r
I32 = mybir.dt.int32
ACT = mybir.ActivationFunctionType
ALU = mybir.AluOpType
AX = mybir.AxisListType

P = 128
D = 1024
SEQ = 512
DEC = 8
T = SEQ + DEC
HALF = T // 2
KT = D // P
FFN = 2816
FT = FFN // P
DEPTH = 2
PAST = 1024
PAGE = 128
NPG = PAST // PAGE
RH = 4
DK = D // RH
DV = 2 * DK
DH = 64
NH = 8
TB = SEQ // P
BUCKETS = 32
EPS = 1e-5
ALPHA = (2.0 * DEPTH) ** 0.25
LAMBDA_INIT = 0.8 - 0.6 * math.exp(-0.3)
MASKED = -1e30

PAIRS = DEC * NH

UC = 256
UK = 8
USZ = UK * UC
LINE = 640

STAGES = [("in0", 22), ("out0", 12), ("ret_in", 24), ("ret_out", 8), ("in1", 22), ("out1", 12),
          ("in2", 22), ("out2", 12), ("q", 4), ("kv", 8), ("o", 4), ("in3", 22), ("out3", 12)]
UB, UNITS = {}, 0
for _name, _nu in STAGES:
    UB[_name] = UNITS
    UNITS += _nu


def trunk_kernel(nc, x_t, w_in, w_out, w_ret_in, w_ret_out, w_q, w_kv, w_o, ln_g, ln_b, state,
                 cache_kt, cache_v, pages, lam_vecs, subln_g, rel_bias,
                 identity, rope, ret_tab, onehot_line, line_mask, onehot_past, rel_rows, row_tab,
                 y_t, state_p, state_s, k_t, v_p, v_s, bias_rep, v_rows):
    ctx = ExitStack()
    with ctx:
        base = [(nc.sbuf_base + 31) // 32 * 32]

        def at(name, shape, dt, off):
            return nc.alloc_sbuf_tensor_at(name, shape, dt, offset=off)

        def size(shape):
            return int(np.prod(shape[1:])) * 4

        def new(name, shape, dt=F32):
            off = base[0]
            base[0] += (size(shape) + 31) // 32 * 32
            return at(name, shape, dt, off)

        def sem(name):
            return ctx.enter_context(nc.semaphore(name))

        WR = new("WR", [P, 2, UK, UC])
        WH = new("WH", [P, 2, UK, UC], F32R)
        WL = new("WL", [P, 2, UK, UC], F32R)
        XH = new("XH", [P, KT, T], F32R)
        XL = new("XL", [P, KT, T], F32R)
        off_hh = base[0]
        HH = new("HH", [P, FT, T], F32R)
        off_hl = base[0]
        HL = new("HL", [P, FT, T], F32R)
        off_x = base[0]
        X = new("X", [P, KT, T])
        off_ft = base[0]
        SG = new("SG", [P, 2, T])
        HF = new("HF", [P, 2, T])
        IDN = new("IDN", [P, P])
        ONES = new("ONES", [P, P])
        LNG = new("LNG", [P, 6, KT])
        LNB = new("LNB", [P, 6, KT])
        COL = new("COL", [P, 16])
        ROWS = new("ROWS", [P, 2 * PAIRS + 2 + NH])
        PTAB = new("PTAB", [1, DEC * NPG], I32)
        off_sp = base[0]
        EPS_LN, EPS_1, SUBG, NLAM, SIGN = (COL[:, i:i + 1] for i in range(5))
        NMAX, NMAX1, SHIFT, SUM, OWN_EXP, TOTAL = (COL[:, i:i + 1] for i in range(10, 16))
        DOT, EXPD = COL[:, 6:8], COL[:, 8:10]
        SQ = SG
        RS = at("RS", [P, T], F32, off_ft + 2 * T * 4)
        ACC = at("ACC", [P, T], F32, off_ft + 3 * T * 4)

        OHL = at("OHL", [BUCKETS, LINE], F32, off_hh)
        LMASK = at("LMASK", [NH, LINE], F32, off_hh + 2560)
        RB = at("RB", [BUCKETS, NH], F32, off_hh + 9728)
        LN8 = at("LN8", [NH, LINE], F32, off_hh + 9792)
        LV = at("LV", [P, 4, DH], F32, off_hh + 12352)
        LPR = at("LPR", [P, 2, DH], F32, off_hh + 13376)

        VBC = at("VBC", [P, DEC, DV], F32, off_hh)
        VT = at("VT", [P, 4, T], F32, off_hh + 16384)
        RO = at("RO", [P, 4, T], F32, off_hh + 16384)
        GT = at("GT", [P, 4, T], F32, off_hh + 24704)
        VTK = at("VTK", [P, TB, DV], F32, off_hh + 33024)
        KTK = at("KTK", [P, TB, DK], F32, off_hh + 41216)
        OG = at("OG", [P, 4 * RH, T], F32, off_hl)
        SB = at("SB", [P, 2, 2, DV], F32, off_hl + 4 * RH * T * 4)
        TMP = at("TMP", [P, 2, DV], F32, off_hl + 4 * RH * T * 4 + 8192)
        RQ = at("RQ", [P, 2, T], F32, off_x)
        RK = at("RK", [P, 2, T], F32, off_x + 4160)
        RT = at("RT", [P, T], F32, off_x + 8320)
        PT = at("PT", [P, 1280], F32, off_x + 10400)
        COS = at("COS", [P, T], F32, off_sp)
        SIN = at("SIN", [P, T], F32, off_sp + 2080)
        SPR = at("SPR", [P, 2, DV], F32, off_sp + 4160)
        V8 = at("V8", [DEC, DV], F32, off_sp + 8256)
        RX = at("RX", [P, 2, T], F32, off_ft)
        RA = at("RA", [P, 2, T], F32, off_ft + 4160)

        QT = at("QT", [P, NH, T], F32, off_hh)
        KTT = at("KTT", [P, NH, T], F32, off_hh + 16640)
        WT = at("WT", [P, 1280], F32, off_hh + 33280)
        STRIP = at("STRIP", [P, 2, SEQ], F32, off_hh + 41472)
        OF = at("OF", [P, NH, T], F32, off_hl)
        o = off_hl + 16640
        VTOK = at("VTOK", [P, TB, D], F32, o)
        SS = [at("SS0", [P, 2, SEQ], F32, o + 16384), at("SS1", [P, 2, SEQ], F32, off_sp + 4928)]
        QHD = [at("QHD0", [P, SEQ], F32, o + 22528), at("QHD1", [P, SEQ], F32, off_ft + 6208)]
        KHD = [at("KHD0", [P, SEQ], F32, o + 20480), at("KHD1", [P, SEQ], F32, off_hh + 38400)]
        VHD = [at("VHD0", [P, TB, P], F32, o + 26624), at("VHD1", [P, TB, P], F32, o + 24576)]
        RSN = at("RSN", [P, NH, T], F32, off_hh + 16640)
        PG = at("PG", [P, 4, D], F32, off_x)
        SCA = at("SCA", [P, PAST], F32, off_sp)
        OHP = at("OHP", [BUCKETS, PAST], F32, off_sp)
        RBX = at("RBX", [BUCKETS, P], F32, off_sp + 4096)
        VN = at("VN", [P, NH, DEC], F32, off_sp + 4608)
        ST = at("ST", [P, 16], F32, off_sp + 4864)
        V8D = at("V8D", [DEC, D], F32, off_sp + 4928)
        VS = at("VS", [P, 2, T], F32, off_ft)
        QP = at("QP", [P, NH, P], F32, off_ft)
        WP = at("WP", [P, 2, NPG, PAIRS], F32, off_ft)
        WD = at("WD", [P, NPG, PAIRS], F32, off_ft + 4160)
        o = off_sp + 4928 + 4096
        PRD = at("PRD", [P, PAIRS, 2], F32, o)
        OVR = at("OVR", [PAIRS, P], F32, o)
        COMB = at("COMB", [P, PAIRS], F32, o + 512)
        COMB_OWN = at("COMB_OWN", [P, PAIRS], F32, o + 768)
        OWN = at("OWN", [P, NH, DEC], F32, o + 1024)
        end = max(off_sp + 8256 + DV * 4, off_sp + 4928 + D * 4)
        assert end <= nc.sbuf_usable_end, end - nc.sbuf_usable_end

        PS = ctx.enter_context(nc.psum_tensor("PS", [P, 8, 512], F32))

        raw_loaded = [sem("raw_loaded0"), sem("raw_loaded1")]
        hi_ready = sem("hi_ready")
        lo_ready = sem("lo_ready")
        half_done = sem("half_done")
        gate_ready = [sem("gate_ready0"), sem("gate_ready1")]
        h_ready = [sem("h_ready0"), sem("h_ready1")]
        hh_ready = sem("hh_ready")
        hl_ready = sem("hl_ready")
        y_ready = sem("y_ready")
        acc_ready = sem("acc_ready")
        mean_ready = sem("mean_ready")
        cent_ready = sem("cent_ready")
        sq_ready = sem("sq_ready")
        sqm_done = sem("sqm_done")
        ln_step = sem("ln_step")
        rs_ready = sem("rs_ready")
        scaled = sem("scaled")
        xh_ready = sem("xh_ready")
        x_ready = sem("x_ready")
        xl_ready = sem("xl_ready")
        x_loaded = sem("x_loaded")
        const_loaded = sem("const_loaded")
        ones_ready = sem("ones_ready")
        line_mm = sem("line_mm")
        line_sb = sem("line_sb")
        line_out = sem("line_out")
        lam_step = sem("lam_step")
        lam_exp = sem("lam_exp")
        rope_in = [sem("rope_in0"), sem("rope_in1")]
        rope_step = sem("rope_step")
        v_ready = [sem("v_ready0"), sem("v_ready1")]
        g_ready = [sem("g_ready0"), sem("g_ready1")]
        rt_loaded = sem("rt_loaded")
        ktr_done = sem("ktr_done")
        ktk_ready = sem("ktk_ready")
        vtr_done = sem("vtr_done")
        vtk_ready = sem("vtk_ready")
        v8_mm = sem("v8_mm")
        v8_ready = sem("v8_ready")
        v8_out = sem("v8_out")
        vbc_loaded = sem("vbc_loaded")
        rsc_done = sem("rsc_done")
        pt_ready = sem("pt_ready")
        ro_done = sem("ro_done")
        ro_ready = sem("ro_ready")
        rst_done = sem("rst_done")
        spr_ready = sem("spr_ready")
        spr_out = sem("spr_out")
        s0_loaded = [sem("s0_loaded0"), sem("s0_loaded1")]
        kv_ready = sem("kv_ready")
        sn_ready = sem("sn_ready")
        snq_done = sem("snq_done")
        s_out = [sem("s_out0"), sem("s_out1")]
        rod_ready = sem("rod_ready")
        rn_sum = sem("rn_sum")
        rn_mean = sem("rn_mean")
        rn_cent = sem("rn_cent")
        rn_sq = sem("rn_sq")
        rn_sqm = sem("rn_sqm")
        rn_step = sem("rn_step")
        rn_rs = sem("rn_rs")
        rn_mul = sem("rn_mul")
        rn_done = sem("rn_done")
        og_hi = sem("og_hi")
        og_lo = sem("og_lo")
        q_ready = [sem("q_ready0"), sem("q_ready1")]
        k_ready = [sem("k_ready0"), sem("k_ready1")]
        k_out = sem("k_out")
        bias_loaded = sem("bias_loaded")
        rbx_ready = sem("rbx_ready")
        slot_step = sem("slot_step")
        qp_ready = sem("qp_ready")
        wp_ready = sem("wp_ready")
        vs_ready = [sem("vs_ready0"), sem("vs_ready1")]
        vn_ready = sem("vn_ready")
        dvt_done = sem("dvt_done")
        dvt_ready = sem("dvt_ready")
        v8d_done = sem("v8d_done")
        v8d_ready = sem("v8d_ready")
        v_out = sem("v_out")
        head_copied = sem("head_copied")
        strip_loaded = [sem("strip_loaded0"), sem("strip_loaded1")]
        sc_done = sem("sc_done")
        ss_ready = sem("ss_ready")
        mx_ready = sem("mx_ready")
        ex_ready = sem("ex_ready")
        rc_ready = sem("rc_ready")
        s0n_ready = sem("s0n_ready")
        ww_ready = sem("ww_ready")
        wtr_done = sem("wtr_done")
        wt_ready = sem("wt_ready")
        pv_done = sem("pv_done")
        of_ready = sem("of_ready")
        pt_loaded = sem("pt_loaded")
        page_loaded = [sem(f"page_loaded{i}") for i in range(4)]
        page_used = [sem(f"page_used{i}") for i in range(4)]
        newprod_ready = sem("newprod_ready")
        newscore_done = sem("newscore_done")
        shift_ready = sem("shift_ready")
        dec_exp = sem("dec_exp")
        comb_ready = sem("comb_ready")
        wd_done = sem("wd_done")
        wd_ready = sem("wd_ready")
        soft_step = sem("soft_step")
        ov_step = sem("ov_step")
        ov_turned = sem("ov_turned")
        res_done = [sem("res_done0"), sem("res_done1")]
        acc_zero = sem("acc_zero")
        new_step = sem("new_step")
        on_sq = sem("on_sq")
        on_mm = sem("on_mm")
        on_ln = sem("on_ln")
        on_rs = sem("on_rs")
        on_mul = sem("on_mul")
        on_hi = sem("on_hi")
        on_lo = sem("on_lo")
        y_out = sem("y_out")

        block = ctx.enter_context(nc.Block())

        def halves(ap):
            return ap.rearrange("p (h c) -> p h c", h=2)

        def tile_ps(c):
            return PS[:, 2 * c:2 * c + 2, 0:HALF]

        def strip_at(jb):
            return sum(SEQ - P * j for j in range(jb))

        def turned_at(qb):
            return P * qb * (qb + 1) // 2

        @block.sync
        def _(sp):
            sp.dma_start(X[:, :, :], x_t).then_inc(x_loaded, 16)

            def load(src, u, r, nk):
                sp.wait_ge(lo_ready, u * 2 + r)
                sp.dma_start(WR[:, r, 0:nk, :], src).then_inc(raw_loaded[r], 16)

            def ffn_loads(n):
                u_in, u_out = UB[f"in{n}"] // 2, UB[f"out{n}"] // 2
                with sp.Fori(0, 11) as i:
                    for r in range(2):
                        load(w_in[bass.ds(i * 2 + (22 * n + r), 1)].rearrange("a p k c -> (a p) k c"),
                             i + u_in, r, UK)
                with sp.Fori(0, 2) as i:
                    for j in range(6):
                        k0 = UK * (j % 3)
                        nk = min(UK, FT - k0)
                        load(w_out[bass.ds(i * 2 + (4 * n + j // 3), 1)][:, :, k0:k0 + nk, :]
                             .rearrange("a p k c -> (a p) k c"), i * 3 + (u_out + j // 2), j % 2, nk)

            def plain_loads(w, stage, n):
                u0 = UB[stage] // 2
                with sp.Fori(0, n // 2) as i:
                    for r in range(2):
                        load(w[bass.ds(i * 2 + r, 1)].rearrange("a p k c -> (a p) k c"), i + u0, r, UK)

            ffn_loads(0)
            plain_loads(w_ret_in, "ret_in", 24)
            with sp.Fori(0, 4) as i:
                for r in range(2):
                    load(w_ret_out[bass.ds(i, 1)][:, :, UK * r:UK * r + UK, :]
                         .rearrange("a p k c -> (a p) k c"), i + UB["ret_out"] // 2, r, UK)
            ffn_loads(1)
            ffn_loads(2)
            plain_loads(w_q, "q", 4)
            plain_loads(w_kv, "kv", 8)
            for r in range(2):
                load(w_o[r], UB["o"] // 2, r, UK)
            sp.dma_start(PTAB[:, :], pages).then_inc(pt_loaded, 16)
            sp.wait_ge(pt_loaded, 16)
            sp.wait_ge(xl_ready, KT * 5)
            with sp.Fori(0, DEC) as b:
                for pg in range(NPG):
                    s = pg % 4
                    sp.wait_ge(page_used[s], b * 2 + pg // 4)
                    page = sp.value_load(PTAB[0:1, bass.ds(b * NPG + pg, 1)], min_val=0,
                                         max_val=cache_kt.shape[0] - 1)
                    sp.dma_start(PG[:, s, :], cache_kt[bass.ds(page, 1)].rearrange("a p c -> (a p) c")
                                 ).then_inc(page_loaded[s], 16)
            with sp.Fori(0, DEC) as b:
                for pg in range(NPG):
                    s = pg % 4
                    sp.wait_ge(page_used[s], b * 2 + (16 + pg // 4))
                    page = sp.value_load(PTAB[0:1, bass.ds(b * NPG + pg, 1)], min_val=0,
                                         max_val=cache_v.shape[0] - 1)
                    sp.dma_start(PG[:, s, :], cache_v[bass.ds(page, 1)].rearrange("a p c -> (a p) c")
                                 ).then_inc(page_loaded[s], 16)
            for r in range(2):
                load(w_o[2 + r], UB["o"] // 2 + 1, r, UK)
            ffn_loads(3)

        @block.gpsimd
        def _(pool):
            pool.memset(ONES[:, :], 1.0).then_inc(ones_ready, 1)
            pool.memset(COL[:, 0:1], EPS / ALPHA ** 2).then_inc(ones_ready, 1)
            pool.memset(COL[:, 1:2], EPS).then_inc(ones_ready, 1)
            for dst, src in ((IDN[:, :], identity), (LNG[:, :, :], ln_g), (LNB[:, :, :], ln_b),
                             (OHL[:, :], onehot_line), (LMASK[:, :], line_mask), (ROWS[:, :], row_tab),
                             (RB[:, :], rel_bias), (COL[:, 2:3], subln_g), (LV[:, :, :], lam_vecs),
                             (COS[:, :], rope[0]), (SIN[:, :], rope[1])):
                pool.dma_start(dst, src).then_inc(const_loaded, 16)
            pool.wait_ge(line_sb, 1)
            pool.dma_start(bias_rep.rearrange("h (p c) -> h p c", p=P),
                           LN8[:, :].unsqueeze(1).to_broadcast([NH, P, LINE])).then_inc(line_out, 16)
            pool.wait_ge(line_out, 16)

            def strip(h):
                return (bias_rep[bass.ds(h, 1), P - 1:P - 1 + P * (LINE - 1)]
                        .rearrange("a (p c) -> (a p) c", p=P)[:, 0:SEQ])

            for h in range(RH):
                pool.wait_ge(sn_ready, h * 16)
                pool.wait_ge(x_ready, KT)
                pool.wait_ge(xl_ready, KT * 2)
                pool.dma_start(RT[:, :], ret_tab[bass.ds(h, 1)].rearrange("a p c -> (a p) c")
                               ).then_inc(rt_loaded, 16)
                for b in range(DEC):
                    s = b % 2
                    pool.wait_ge(s_out[s], h * 64 + 16 * (b // 2))
                    if b < 2:
                        pool.wait_ge(snq_done, h * 8)
                        pool.wait_ge(half_done, 2 * UB["ret_in"])
                    else:
                        pool.wait_ge(snq_done, h * 8 + (b - 1))
                    pool.dma_start(SB[:, s, :, :], state[b, bass.ds(h, 1)].rearrange("a p t e -> (a p) t e")
                                   ).then_inc(s0_loaded[s], 16)
                    if b == 1:
                        pool.wait_ge(v8_ready, h + 1)
                        pool.dma_start(v_rows, V8[:, :]).then_inc(v8_out, 16)
                        pool.wait_ge(v8_out, h * 16 + 16)
                        pool.wait_ge(kv_ready, h * 16)
                        pool.dma_start(VBC[:, :, :], bass.AP(tensor=v_rows.tensor, offset=v_rows.offset,
                                                             ap=[[0, P], [DV, DEC], [1, DV]])
                                       ).then_inc(vbc_loaded, 16)
                        pool.wait_ge(spr_ready, h * 2 + 2)
                        pool.dma_start(state_p[bass.ds(h, 1)].rearrange("a p t e -> (a p) t e"), SPR[:, :, :]
                                       ).then_inc(spr_out, 16)
                    if b >= 1:
                        pool.wait_ge(sn_ready, h * 16 + 2 * b)
                        pool.dma_start(state_s[b - 1, bass.ds(h, 1)].rearrange("a p t e -> (a p) t e"),
                                       SB[:, 1 - s, :, :]).then_inc(s_out[1 - s], 16)
                pool.wait_ge(sn_ready, h * 16 + 16)
                pool.dma_start(state_s[DEC - 1, bass.ds(h, 1)].rearrange("a p t e -> (a p) t e"),
                               SB[:, 1, :, :]).then_inc(s_out[1], 16)

            pool.wait_ge(half_done, 2 * UB["q"])
            pool.dma_start(OHP[:, :], onehot_past).then_inc(bias_loaded, 16)
            pool.dma_start(RBX[:, :], rel_rows).then_inc(bias_loaded, 16)
            for i in range(4):
                pool.wait_ge(k_ready[0], i + 1)
                pool.wait_ge(k_ready[1], i + 1)
                pool.dma_start(k_t[:, bass.ds(i * 2, 2), :], KTT[:, bass.ds(i * 2, 2), :]).then_inc(k_out, 16)
            pool.wait_ge(dvt_ready, 8 * TB // 2)
            for j in range(TB):
                pool.dma_start(v_p[j], VTOK[:, j, :]).then_inc(v_out, 16)
            pool.wait_ge(v8d_ready, 8)
            pool.dma_start(v_s, V8D[:, :]).then_inc(v_out, 16)
            for r in range(2):
                pool.dma_start(STRIP[:, r, :], strip(r)).then_inc(strip_loaded[r], 16)

            def copy_head(h):
                r = h % 2
                if h >= 2:
                    pool.wait_ge(pv_done, h - 1)
                pool.tensor_copy(QHD[r][:, :], QT[:, h, 0:SEQ]).then_inc(head_copied, 1)
                pool.tensor_copy(KHD[r][:, :], KTT[:, h, 0:SEQ]).then_inc(head_copied, 1)
                pool.tensor_copy(VHD[r][:, :, :], VTOK[:, :, h * P:(h + 1) * P]).then_inc(head_copied, 1)
                if 1 <= h < NH - 1:
                    pool.wait_ge(ss_ready, 8 * h)
                    pool.dma_start(STRIP[:, 1 - r, :], strip(h + 1)).then_inc(strip_loaded[1 - r], 16)

            pool.wait_ge(v8d_done, NH)
            pool.wait_ge(v8d_ready, NH)
            pool.wait_ge(vn_ready, NH)
            copy_head(0)
            pool.memset(QP[:, :, :], 0.0).then_inc(slot_step, 1)
            pool.wait_ge(slot_step, 1)
            qp = QP[:, :, :].rearrange("p h c -> p (h c)")
            for b in range(DEC):
                if b >= 1:
                    pool.wait_ge(page_used[3], 2 * b)
                    pool.memset(QP[:, :, 2 * NH * (b - 1):2 * NH * b], 0.0).then_inc(qp_ready, 1)
                for m in range(2):
                    c = 2 * NH * b + m
                    if b or m:
                        pool.wait_ge(qp_ready, 3 * b + m)
                    pool.tensor_copy(qp[m * DH:(m + 1) * DH, c:c + (NH - 1) * (P + 2) + 1:P + 2],
                                     QT[m * DH:(m + 1) * DH, :, SEQ + b]).then_inc(qp_ready, 1)
                pool.wait_ge(qp_ready, 3 * b + 2)
                if b % 2 == 0:
                    copy_head(b // 2 + 1)
            pool.wait_ge(page_used[3], 2 * DEC)
            pool.memset(WP[:, :, :, :], 0.0).then_inc(slot_step, 1)
            pool.wait_ge(slot_step, 2)
            pool.wait_ge(wd_ready, 1)
            for b in range(DEC):
                if b >= 2:
                    pool.wait_ge(page_used[3], 2 * DEC + 2 * (b - 1))
                    pool.memset(WP[:, b % 2, :, NH * (b - 2):NH * (b - 1)], 0.0).then_inc(wp_ready, 1)
                pool.tensor_copy(WP[:, b % 2, :, NH * b:NH * (b + 1)], WD[:, :, NH * b:NH * (b + 1)]
                                 ).then_inc(wp_ready, 1)
                if b % 2 == 1 and b // 2 + 5 < NH:
                    copy_head(b // 2 + 5)
            pool.wait_ge(x_ready, 6 * KT)
            pool.dma_start(y_t, X[:, :, :]).then_inc(y_out, 16)
            for r in range(2):
                pool.wait_ge(strip_loaded[r], 16 * (NH // 2))
                pool.wait_ge(s_out[r], 16 * RH * 4)
            pool.wait_ge(spr_out, 16 * RH)
            pool.wait_ge(k_out, 16 * 4)
            pool.wait_ge(v_out, 16 * (TB + 1))
            pool.wait_ge(v8_out, 16 * RH)
            pool.wait_ge(y_out, 16)

        @block.tensor
        def _(pe):
            def unit(u, r, nk, k0, xh, xl, first, last, free, fresh=None):
                pe.wait_ge(lo_ready, u + 2)
                if fresh:
                    for c in range(2):
                        if first and free:
                            pe.wait_ge(free[0][c], free[1])
                    for k in range(nk):
                        pe.wait_ge(fresh[0], fresh[1] + k + 1)
                        for c in range(2):
                            for w, a, n in ((WH, xh, 0), (WH, xl, 1), (WL, xh, 2)):
                                for h in range(2):
                                    mm = pe.matmul(PS[:, 2 * c + h, 0:HALF], w[:, r, k, c * P:c * P + P],
                                                   a[:, k0 + k, h * HALF:(h + 1) * HALF],
                                                   start=(first and k == 0 and n == 0),
                                                   stop=(last and k == nk - 1 and n == 2))
                            if k == nk - 1:
                                mm.then_inc(half_done, 1)
                    return
                for c in range(2):
                    if first and free:
                        pe.wait_ge(free[0][c], free[1])
                    for k in range(nk):
                        for w, a, n in ((WH, xh, 0), (WH, xl, 1), (WL, xh, 2)):
                            for h in range(2):
                                mm = pe.matmul(PS[:, 2 * c + h, 0:HALF], w[:, r, k, c * P:c * P + P],
                                               a[:, k0 + k, h * HALF:(h + 1) * HALF],
                                               start=(first and k == 0 and n == 0),
                                               stop=(last and k == nk - 1 and n == 2))
                    mm.then_inc(half_done, 1)

            def plain(stage, n, ready, base):
                with pe.Fori(0, n // 2) as i:
                    for r in range(2):
                        unit(i * 2 + (UB[stage] + r), r, UK, 0, XH, XL, True, True, (ready, i * 2 + (base + r)))

            def ffn(n, ln):
                def pair(i, fresh):
                    unit(i * 2 + UB[f"in{n}"], 0, UK, 0, XH, XL, True, True,
                         (h_ready, i + 11 * n) if n or not fresh else None, fresh)
                    unit(i * 2 + (UB[f"in{n}"] + 1), 1, UK, 0, XH, XL, True, True, (gate_ready, i + (11 * n + 1)))

                pair(0, (xl_ready, KT * ln))
                with pe.Fori(1, 11) as i:
                    pair(i, None)

                def outs(i, fresh):
                    for j in range(6):
                        k0 = UK * (j % 3)
                        unit(i * 6 + (UB[f"out{n}"] + j), j % 2, min(UK, FT - k0), k0, HH, HL, j % 3 == 0,
                             j % 3 == 2, (h_ready, 11 * (n + 1)) if fresh and j == 0 else
                             (res_done, i * 2 + (4 * ln + j // 3)),
                             (hl_ready, FT * n + k0) if fresh and j < 3 else None)

                outs(0, True)
                outs(1, False)

            def layer_norm(n):
                pe.wait_ge(acc_ready, KT * (n + 1))
                for h in range(2):
                    mm = pe.matmul(PS[:, 4 + h, 0:HALF], ONES[:, :], ACC[:, h * HALF:(h + 1) * HALF],
                                   start=True, stop=True)
                mm.then_inc(mean_ready, 1)
                for d in range(KT):
                    pe.wait_ge(sq_ready, KT * n + d + 1)
                    for h in range(2):
                        mm = pe.matmul(PS[:, 6 + h, 0:HALF], ONES[:, :], SQ[:, d % 2, h * HALF:(h + 1) * HALF],
                                       start=(d == 0), stop=(d == KT - 1))
                    mm.then_inc(sqm_done, 1)

            pe.wait_ge(const_loaded, 16 * 11)
            pe.wait_ge(ones_ready, 3)
            for h in range(2):
                mm = pe.matmul(PS[0:NH, 4 + h, 0:LINE // 2], RB[:, :], OHL[:, h * (LINE // 2):(h + 1) * (LINE // 2)],
                               start=True, stop=True)
            mm.then_inc(line_mm, 1)
            ffn(0, 0)
            layer_norm(0)

            pe.wait_ge(xl_ready, KT * 2)
            with pe.Fori(0, RH) as h:
                for j in range(6):
                    free = ((g_ready, 0), (rope_in, 1), (rope_in, 2), (v_ready, 1), (v_ready, 2), (g_ready, 1))[j]
                    unit(h * 6 + (UB["ret_in"] + j), j % 2, UK, 0, XH, XL, True, True, (free[0], h * 2 + free[1]))
                pe.wait_ge(rope_step, h * 12 + 12)
                pe.wait_ge(rn_rs, h)
                pe.wait_ge(rn_cent, h * 4)
                for t in range(2):
                    for jb in range(TB):
                        mm = pe.transpose(PS[:, 4 + t, jb * P:(jb + 1) * P], RK[:, t, jb * P:(jb + 1) * P], IDN[:, :])
                    mm.then_inc(ktr_done, 1)
                pe.wait_ge(v_ready[0], h * 2 + 2)
                pe.wait_ge(v_ready[1], h * 2 + 2)
                for jb in range(TB):
                    if jb >= 2:
                        pe.wait_ge(vtk_ready, h * 4 + jb - 1)
                    for e in range(4):
                        mm = pe.transpose(PS[:, 6 + jb % 2, e * P:(e + 1) * P], VT[:, e, jb * P:(jb + 1) * P], IDN[:, :])
                    mm.then_inc(vtr_done, 1)
                pe.wait_ge(ktk_ready, h * 2 + 2)
                for e in range(4):
                    mm = pe.transpose(PS[0:DEC, 4, e * P:(e + 1) * P], VT[:, e, SEQ:T], IDN[:, :])
                mm.then_inc(v8_mm, 1)
                pe.wait_ge(vtk_ready, h * 4 + 4)
                pe.wait_ge(v8_ready, h + 1)
                for jb in range(TB):
                    for t in range(2):
                        mm = pe.matmul(PS[:, 4 + jb, 0:SEQ - P * jb], RK[:, t, jb * P:(jb + 1) * P],
                                       RQ[:, t, jb * P:SEQ], start=(t == 0), stop=(t == 1))
                    mm.then_inc(rsc_done, 1)
                pe.wait_ge(pt_ready, h * 4 + 4)
                for e in range(4):
                    for jb in range(TB):
                        mm = pe.matmul(PS[:, 4 + e, jb * P:SEQ], VTK[:, jb, e * P:(e + 1) * P],
                                       PT[:, strip_at(jb):strip_at(jb + 1)], start=(jb == 0), stop=(jb == TB - 1))
                    mm.then_inc(ro_done, 1)
                for t in range(2):
                    pe.wait_ge(ro_ready, h * 4 + t + 1)
                    for jb in range(TB):
                        mm = pe.matmul(PS[:, 4 + t, :], KTK[:, jb, t * P:(t + 1) * P], VTK[:, jb, :],
                                       start=(jb == 0), stop=(jb == TB - 1))
                    mm.then_inc(rst_done, 1)
                pe.wait_ge(ro_ready, h * 4 + 3)
                for b in range(DEC):
                    pe.wait_ge(sn_ready, h * 16 + 2 * b + 2)
                    for e in range(4):
                        for t in range(2):
                            mm = pe.matmul(PS[:, 6, e * DEC + b:e * DEC + b + 1], SB[:, b % 2, t, e * P:(e + 1) * P],
                                           RQ[:, t, SEQ + b:SEQ + b + 1], start=(t == 0), stop=(t == 1))
                    mm.then_inc(snq_done, 1)
                pe.wait_ge(rn_sum, h * 3 + 3)
                pe.wait_ge(spr_ready, h * 2 + 2)
                for g in range(2):
                    mm = pe.matmul(PS[:, 4 + g, 0:HALF], ONES[:, :], RA[:, 1, g * HALF:(g + 1) * HALF],
                                   start=True, stop=True)
                mm.then_inc(rn_mean, 1)
                pe.wait_ge(rod_ready, h + 1)
                pe.wait_ge(ro_ready, h * 4 + 4)
                for e in range(4):
                    pe.wait_ge(rn_sq, h * 4 + e + 1)
                    for g in range(2):
                        mm = pe.matmul(PS[:, 6 + g, 0:HALF], ONES[:, :], RX[:, e % 2, g * HALF:(g + 1) * HALF],
                                       start=(e == 0), stop=(e == 3))
                    mm.then_inc(rn_sqm, 1)
            for i in range(4):
                for r in range(2):
                    unit(i * 2 + (UB["ret_out"] + r), r, UK, UK * r, HH, HL, r == 0, r == 1,
                         (res_done, i + 4) if i else (g_ready, 2 * RH),
                         (og_lo, UK * r) if i == 0 else None)
            layer_norm(1)
            ffn(1, 2)
            layer_norm(2)
            ffn(2, 3)
            layer_norm(3)

            pe.wait_ge(xl_ready, KT * 5)
            plain("q", 4, q_ready, 0)
            for c in range(2):
                pe.wait_ge(q_ready[c], 4)
            plain("kv", 4, k_ready, 0)
            for c in range(2):
                pe.wait_ge(k_ready[c], 4)
            with pe.Fori(0, 2) as i:
                for r in range(2):
                    unit(i * 2 + (UB["kv"] + 4 + r), r, UK, 0, XH, XL, True, True, (vs_ready, i * 2 + r))
                    for c in range(2):
                        pe.wait_ge(vs_ready[c], i * 2 + (r + 1))
                        pe.wait_ge(dvt_ready, i * 8 + 4 * r + 2 * c)
                        for jb in range(TB):
                            mm = pe.transpose(PS[:, 4 + jb // 2, (jb % 2) * P:(jb % 2 + 1) * P],
                                              VS[:, c, jb * P:(jb + 1) * P], IDN[:, :])
                            if jb % 2:
                                mm.then_inc(dvt_done, 1)
                        pe.wait_ge(v8d_ready, i * 4 + 2 * r + c)
                        pe.transpose(PS[0:DEC, 6, 0:P], VS[:, c, SEQ:T], IDN[:, :]).then_inc(v8d_done, 1)
            pe.wait_ge(v8d_ready, 8)

            def scores(i, part, n):
                r, qb = n // TB, n % TB
                kw = (qb + 1) * P
                if qb == 0:
                    pe.wait_ge(head_copied, i * 6 + (12 * part + 3 * r + 3))
                pe.wait_ge(ss_ready, i * 16 + (32 * part + 2 * max(n - 1, 0)))
                for m in range(2):
                    mm = pe.matmul(PS[:, (4, 2)[n % 2] + m, 0:kw], QHD[r][m * DH:(m + 1) * DH, qb * P:(qb + 1) * P],
                                   KHD[r][m * DH:(m + 1) * DH, 0:kw], start=True, stop=True)
                mm.then_inc(sc_done, 1)

            def k_pages(i, r, a, pages):
                if 0 in pages:
                    pe.wait_ge(qp_ready, i * 12 + 3 * (2 * r + a) + 2)
                for pg in pages:
                    pe.wait_ge(page_loaded[pg % 4], i * 128 + (64 * r + 32 * a + 16 * (pg // 4) + 16))
                    for hd in range(NH):
                        mm = pe.matmul(PS[:, pg // 4, (pg % 4) * P:(pg % 4 + 1) * P], QP[:, hd, :],
                                       PG[:, pg % 4, hd * P:(hd + 1) * P], start=False, stop=True,
                                       skip_group_check=True)
                    mm.then_inc(page_used[pg % 4], 1)

            def v_pages(i, r, a, pages):
                if 0 in pages:
                    pe.wait_ge(wp_ready, i * 8 + max(1, 2 * (2 * r + a)))
                for pg in pages:
                    pe.wait_ge(page_loaded[pg % 4], i * 128 + (64 * r + 32 * a + 16 * (pg // 4) + 16 + 16 * 16))
                    for g in range(2):
                        mm = pe.matmul(PS[0:PAIRS, g, :], WP[:, a, pg, :], PG[:, pg % 4, g * 512:(g + 1) * 512],
                                       start=False, stop=True, skip_group_check=True)
                    mm.then_inc(page_used[pg % 4], 1)

            def heads(part, pages):
                with pe.Fori(0, NH // 4) as i:
                    scores(i, part, 0)
                    for n in range(2 * TB):
                        r, qb = n // TB, n % TB
                        if n + 1 < 2 * TB:
                            scores(i, part, n + 1)
                        pages(i, r, qb // 2, range(4 * (qb % 2), 4 * (qb % 2) + 4))
                        pe.wait_ge(ww_ready, i * 8 + (16 * part + n + 1))
                        pe.wait_ge(wt_ready, i * 8 + (16 * part + n))
                        for kb in range(qb + 1):
                            mm = pe.transpose(PS[:, 6, kb * P:(kb + 1) * P], SS[n % 2][:, 0, kb * P:(kb + 1) * P],
                                              IDN[:, :])
                        mm.then_inc(wtr_done, 1)
                        if qb == TB - 1:
                            pe.wait_ge(wt_ready, i * 8 + (16 * part + n + 1))
                            pe.wait_ge(of_ready, i * 2 + (4 * part + r))
                            for q in range(TB):
                                for kb in range(q + 1):
                                    mm = pe.matmul(PS[:, 7, q * P:(q + 1) * P], VHD[r][:, kb, :],
                                                   WT[:, turned_at(q) + kb * P:turned_at(q) + (kb + 1) * P],
                                                   start=(kb == 0), stop=(kb == q))
                            mm.then_inc(pv_done, 1)

            pe.wait_ge(bias_loaded, 32)
            pe.wait_ge(rbx_ready, 1)
            for g in range(2):
                pe.matmul(PS[:, g, :], RBX[:, :], OHP[:, g * 512:(g + 1) * 512], start=True, stop=True,
                          skip_group_check=True)
            heads(0, k_pages)
            pe.wait_ge(newprod_ready, 3)
            pe.wait_ge(ss_ready, 4 * NH)
            pe.matmul(PS[:, 2, 0:1], PRD[:, :, :].rearrange("p x m -> p (x m)"), ONES[:, 0:1], start=True, stop=False)
            pe.matmul(PS[:, 2, 0:1], RBX[:, :], IDN[0:BUCKETS, 0:1], start=False, stop=True).then_inc(newscore_done, 1)
            pe.wait_ge(comb_ready, 2)
            for pg in range(NPG):
                mm = pe.matmul(PS[:, 4, pg * PAIRS:(pg + 1) * PAIRS], SCA[:, pg * P:(pg + 1) * P], COMB[:, :],
                               start=True, stop=True)
            mm.then_inc(wd_done, 1)
            pe.matmul(PS[:, 3, 0:PAIRS], ONES[:, :], COMB_OWN[:, :], start=True, stop=True).then_inc(wd_done, 1)
            for g in range(2):
                pe.matmul(PS[0:PAIRS, g, :], ROWS[:, PAIRS + 2:2 * PAIRS + 2], SCA[:, g * 512:(g + 1) * 512],
                          start=True, stop=True, skip_group_check=True)
            pe.wait_ge(wd_ready, 2)
            heads(1, v_pages)
            pe.wait_ge(of_ready, NH)
            pe.wait_ge(ov_step, 2)
            pe.transpose(PS[:, 6, 0:PAIRS], OVR[:, :], IDN[0:PAIRS, 0:PAIRS]).then_inc(ov_turned, 1)
            pe.wait_ge(ss_ready, 8 * NH)
            pe.wait_ge(wt_ready, 4 * NH)
            for d in range(NH):
                pe.wait_ge(on_sq, d + 1)
                if d >= 2:
                    pe.wait_ge(on_ln, d - 1)
                for g in range(2):
                    mm = pe.matmul(PS[:, (6, 4)[d % 2] + g, 0:HALF], ONES[:, :], SG[:, d % 2, g * HALF:(g + 1) * HALF],
                                   start=True, stop=True)
                mm.then_inc(on_mm, 1)
            for j in range(4):
                unit(UB["o"] + j, j % 2, UK, 0, HH, HL, True, True, (res_done, 4 * 4 + j), (on_lo, 0) if j == 0 else None)
            layer_norm(4)
            ffn(3, 5)
            layer_norm(5)

        @block.scalar
        def _(act):
            def ahead(half_u, r, first=False):
                act.wait_ge(raw_loaded[r], half_u * 16 + 16)
                if not first:
                    act.wait_ge(half_done, half_u * 4 + (2 * r - 2))
                act.activation(WH[:, r, :, :], WR[:, r, :, :], ACT.Copy).then_inc(hi_ready, 1)

            def ffn(n):
                u0 = UB[f"in{n}"] // 2
                with act.Fori(0, 11) as i:
                    for c in range(2):
                        act.wait_ge(half_done, i * 4 + (4 * u0 + c + 1))
                        act.wait_ge(h_ready[c], i + 11 * n)
                        act.activation(halves(SG[:, c, :]), tile_ps(c), ACT.Silu).then_inc(gate_ready[c], 1)
                    ahead(i + (u0 + 1), 0)
                    for c in range(2):
                        act.wait_ge(h_ready[c], i + (11 * n + 1))
                        act.activation(HH[:, bass.ds(i * 2 + c, 1), :].rearrange("p a c -> p (a c)"),
                                       HF[:, c, :], ACT.Copy).then_inc(hh_ready, 1)
                    ahead(i + (u0 + 1), 1)
                u0 = UB[f"out{n}"] // 2
                if n < 3:
                    with act.Fori(0, 2) as i:
                        for j in range(6):
                            ahead(i * 3 + (u0 + j // 2 + 1), j % 2)
                else:
                    for j in range(10):
                        ahead(u0 + j // 2 + 1, j % 2)

            def layer_norm(n):
                for d in range(KT):
                    act.wait_ge(cent_ready, KT * n + d + 1)
                    if d >= 2:
                        act.wait_ge(sqm_done, KT * n + d - 1)
                    act.activation(SQ[:, d % 2, :], X[:, d, :], ACT.Square).then_inc(sq_ready, 1)
                act.wait_ge(sqm_done, KT * (n + 1))
                act.activation(halves(RS[:, :]), PS[:, 6:8, 0:HALF], ACT.Ln, bias=EPS_LN, scale=1.0 / D).then_inc(ln_step, 1)
                act.wait_ge(ln_step, n + 1)
                act.activation(RS[:, :], RS[:, :], ACT.Exp, scale=-0.5).then_inc(rs_ready, 1)
                for d in range(KT):
                    act.wait_ge(scaled, KT * n + d + 1)
                    act.activation(XH[:, d, :], X[:, d, :], ACT.Identity, bias=LNB[:, n, d:d + 1]).then_inc(xh_ready, 1)
                    act.wait_ge(xh_ready, KT * (n + 1) + d + 1)
                    act.activation(X[:, d, :], X[:, d, :], ACT.Identity, bias=LNB[:, n, d:d + 1]).then_inc(x_ready, 1)

            act.wait_ge(x_loaded, 16)
            for d in range(KT):
                act.activation(XH[:, d, :], X[:, d, :], ACT.Copy).then_inc(xh_ready, 1)
            ahead(0, 0, True)
            ahead(0, 1, True)
            act.wait_ge(lam_step, 2)
            act.activation(EXPD, DOT, ACT.Exp).then_inc(lam_exp, 1)
            act.wait_ge(line_out, 16)
            ffn(0)
            layer_norm(0)

            ub = UB["ret_in"] // 2
            with act.Fori(0, RH) as h:
                for j in range(6):
                    for c in range(2):
                        act.wait_ge(half_done, h * 12 + (4 * ub + 2 * j + c + 1))
                        if j < 2:
                            act.wait_ge(rope_step, h * 12 + 6 * j)
                            act.wait_ge(rn_sqm, h * 4)
                            a = act.activation(halves(RX[:, c, :]), tile_ps(c), ACT.Copy,
                                               scale=1.0 if j == 0 else DK ** -0.5)
                            a.then_inc(rope_in[c], 1)
                        elif j < 4:
                            act.wait_ge(rn_done, h * 4)
                            a = act.activation(halves(VT[:, 2 * (j - 2) + c, :]), tile_ps(c), ACT.Copy)
                            a.then_inc(v_ready[c], 1)
                        else:
                            act.wait_ge(rn_done, h * 4)
                            a = act.activation(halves(GT[:, 2 * (j - 4) + c, :]), tile_ps(c), ACT.Silu)
                            a.then_inc(g_ready[c], 1)
                    ahead(h * 3 + (ub + j // 2 + 1), j % 2)
                act.wait_ge(rt_loaded, h * 16 + 16)
                act.wait_ge(rst_done, h * 2)
                for t in range(2):
                    act.wait_ge(ktr_done, h * 2 + t + 1)
                    for jb in range(TB):
                        a = act.activation(KTK[:, jb, t * P:(t + 1) * P], PS[:, 4 + t, jb * P:(jb + 1) * P],
                                           ACT.Copy, scale=RT[:, SEQ + jb:SEQ + jb + 1])
                    a.then_inc(ktk_ready, 1)
                for jb in range(TB):
                    act.wait_ge(vtr_done, h * 4 + jb + 1)
                    act.activation(VTK[:, jb, :], PS[:, 6 + jb % 2, :], ACT.Copy).then_inc(vtk_ready, 1)
                act.wait_ge(v8_mm, h + 1)
                act.activation(V8[:, :], PS[0:DEC, 4, :], ACT.Copy).then_inc(v8_ready, 1)
                for e in range(4):
                    act.wait_ge(ro_done, h * 4 + e + 1)
                    act.activation(RO[:, e, 0:SEQ], PS[:, 4 + e, :], ACT.Copy).then_inc(ro_ready, 1)
                act.wait_ge(spr_out, h * 16)
                for t in range(2):
                    act.wait_ge(rst_done, h * 2 + t + 1)
                    act.activation(SPR[:, t, :], PS[:, 4 + t, :], ACT.Copy).then_inc(spr_ready, 1)
                act.wait_ge(vbc_loaded, h * 16 + 16)
                for b in range(DEC):
                    for t in range(2):
                        act.wait_ge(sn_ready, h * 16 + max(0, 2 * b + t - 1))
                        act.activation(TMP[:, t, :], VBC[:, b, :], ACT.Copy,
                                       scale=RK[:, t, SEQ + b:SEQ + b + 1]).then_inc(kv_ready, 1)
                act.wait_ge(snq_done, h * 8 + 8)
                act.activation(RO[:, :, SEQ:T], PS[:, 6, 0:4 * DEC].rearrange("p (e b) -> p e b", e=4),
                               ACT.Copy).then_inc(rod_ready, 1)
                for e in range(4):
                    act.wait_ge(rn_cent, h * 4 + e + 1)
                    act.wait_ge(rope_step, h * 12 + 12)
                    if e >= 2:
                        act.wait_ge(rn_sqm, h * 4 + e - 1)
                    act.activation(RX[:, e % 2, :], RO[:, e, :], ACT.Square).then_inc(rn_sq, 1)
                act.wait_ge(rn_sqm, h * 4 + 4)
                act.activation(halves(RA[:, 0, :]), PS[:, 6:8, 0:HALF], ACT.Ln, bias=EPS_1, scale=1.0 / DV).then_inc(rn_step, 1)
                act.wait_ge(rn_step, h + 1)
                act.activation(RA[:, 0, :], RA[:, 0, :], ACT.Exp, scale=-0.5).then_inc(rn_rs, 1)
            act.wait_ge(rn_done, 4 * RH)
            act.wait_ge(kv_ready, 16 * RH)
            for d in range(4 * RH):
                act.activation(HH[:, d, :], OG[:, d, :], ACT.Copy).then_inc(og_hi, 1)
            u0 = UB["ret_out"] // 2
            with act.Fori(0, 4) as i:
                for r in range(2):
                    ahead(i + (u0 + 1), r)
            layer_norm(1)
            ffn(1)
            layer_norm(2)
            ffn(2)
            layer_norm(3)

            uq, uk = UB["q"] // 2, UB["kv"] // 2
            with act.Fori(0, 2) as i:
                for r in range(2):
                    for c in range(2):
                        act.wait_ge(half_done, i * 4 + (4 * uq + 2 * r + c + 1))
                        a = act.activation(QT[:, bass.ds(i * 4 + (2 * r + c), 1), :].rearrange("p a (h c) -> p (a h) c", h=2),
                                           tile_ps(c), ACT.Copy)
                        a.then_inc(q_ready[c], 1)
                    ahead(i + (uq + 1), r)
            with act.Fori(0, 2) as i:
                for r in range(2):
                    for c in range(2):
                        act.wait_ge(half_done, i * 4 + (4 * uk + 2 * r + c + 1))
                        a = act.activation(KTT[:, bass.ds(i * 4 + (2 * r + c), 1), :].rearrange("p a (h c) -> p (a h) c", h=2),
                                           tile_ps(c), ACT.Copy)
                        a.then_inc(k_ready[c], 1)
                    ahead(i + (uk + 1), r)
            with act.Fori(0, 2) as i:
                for r in range(2):
                    for c in range(2):
                        act.wait_ge(half_done, i * 4 + (4 * uk + 8 + 2 * r + c + 1))
                        kept = i * 4 if r == 0 else i * 4 + (c + 1)
                        act.wait_ge(v8d_done, kept)
                        act.wait_ge(vn_ready, kept)
                        a = act.activation(halves(VS[:, c, :]), tile_ps(c), ACT.Copy)
                        a.then_inc(vs_ready[c], 1)
                    ahead(i + (uk + 3), r)
            def exps(i, part, n):
                kw = (n % TB + 1) * P
                o = 8 * (n % 2)
                act.wait_ge(mx_ready, i * 8 + (16 * part + n + 1))
                for m in range(2):
                    act.activation(SS[n % 2][:, m, 0:kw], SS[n % 2][:, m, 0:kw], ACT.Exp, bias=ST[:, o + m:o + m + 1],
                                   accum_out=ST[:, o + 2 + m:o + 3 + m]).then_inc(ex_ready, 1)

            def heads(part):
                with act.Fori(0, NH // 4) as i:
                    exps(i, part, 0)
                    for n in range(2 * TB):
                        r, qb = n // TB, n % TB
                        if n + 1 < 2 * TB:
                            exps(i, part, n + 1)
                        act.wait_ge(wtr_done, i * 8 + (16 * part + n + 1))
                        if qb == 0:
                            act.wait_ge(pv_done, i * 2 + (4 * part + r))
                        act.activation(WT[:, turned_at(qb):turned_at(qb + 1)], PS[:, 6, 0:(qb + 1) * P], ACT.Copy
                                       ).then_inc(wt_ready, 1)
                        if qb == TB - 1:
                            act.wait_ge(pv_done, i * 2 + (4 * part + r + 1))
                            act.activation(OF[:, bass.ds(i * 2 + (4 * part + r), 1), 0:SEQ]
                                           .rearrange("p a c -> p (a c)"), PS[:, 7, :], ACT.Copy).then_inc(of_ready, 1)

            heads(0)
            act.wait_ge(shift_ready, 1)
            act.activation(SCA[:, :], PS[:, 0:2, :].rearrange("p g c -> p (g c)"), ACT.Exp, bias=SHIFT, scale=DH ** -0.5,
                           accum_out=SUM).then_inc(dec_exp, 1)
            act.activation(OWN_EXP, PS[:, 2, 0:1], ACT.Exp, bias=SHIFT, scale=DH ** -0.5).then_inc(dec_exp, 1)
            heads(1)
            for d in range(NH):
                act.wait_ge(on_mm, d + 1)
                act.activation(halves(RSN[:, d, :]), PS[:, (6, 4)[d % 2]:(6, 4)[d % 2] + 2, 0:HALF], ACT.Ln, bias=EPS_1,
                               scale=1.0 / (2 * DH)).then_inc(on_ln, 1)
            for d in range(NH + 1):
                if d < NH:
                    act.wait_ge(on_ln, d + 1)
                    act.activation(RSN[:, d, :], RSN[:, d, :], ACT.Exp, scale=-0.5).then_inc(on_rs, 1)
                if d >= 1:
                    act.wait_ge(on_mul, d)
                    act.activation(HH[:, d - 1, :], OF[:, d - 1, :], ACT.Copy).then_inc(on_hi, 1)
            u0 = UB["o"] // 2
            with act.Fori(0, 2) as i:
                for r in range(2):
                    ahead(i + (u0 + 1), r)
            layer_norm(4)
            ffn(3)
            layer_norm(5)

        @block.vector
        def _(dve):
            def ahead(half_u, r):
                dve.wait_ge(hi_ready, half_u * 2 + r + 1)
                dve.wait_ge(raw_loaded[r], half_u * 16 + 16)
                dve.tensor_tensor(WL[:, r, :, :], WR[:, r, :, :], WH[:, r, :, :].bitcast(F32), ALU.subtract
                                  ).then_inc(lo_ready, 1)

            def residual(d, pair, c, half, ln, scale, parts=False):
                x = X[:, bass.ds(d, 1), :].rearrange("p a (h c) -> p (a h) c", h=2)
                xf = X[:, bass.ds(d, 1), :].rearrange("p a c -> p (a c)")
                dve.wait_ge(half_done, half)
                if not parts:
                    dve.scalar_tensor_tensor(x, tile_ps(c), scale, x, ALU.mult, ALU.add).then_inc(res_done[c], 1)
                    dve.wait_ge(res_done[c], pair + (4 * ln + 1))
                else:
                    hi = XH[:, bass.ds(d, 1), :].bitcast(F32).rearrange("p a (h c) -> p (a h) c", h=2)
                    lo = XL[:, bass.ds(d, 1), :].bitcast(F32).rearrange("p a c -> p (a c)")
                    dve.scalar_tensor_tensor(x, tile_ps(c), scale, hi, ALU.mult, ALU.add).then_inc(res_done[c], 1)
                    dve.wait_ge(res_done[c], pair + (4 * ln + 1))
                    dve.tensor_tensor(xf, xf, lo, ALU.add).then_inc(y_ready, 1)
                    dve.wait_ge(y_ready, d + (KT * (ln // 4) + 1))
                dve.wait_ge(acc_ready, d + KT * ln)
                dve.tensor_tensor(ACC[:, :], ACC[:, :], xf, ALU.add).then_inc(acc_ready, 1)

            def clear_acc(ln):
                dve.memset(ACC[:, :], 0.0).then_inc(acc_zero, 1)
                dve.wait_ge(acc_zero, ln + 1)

            def layer_norm(n):
                dve.wait_ge(mean_ready, n + 1)
                for d in range(KT):
                    x = halves(X[:, d, :])
                    dve.scalar_tensor_tensor(x, PS[:, 4:6, 0:HALF], -1.0 / D, x, ALU.mult, ALU.add
                                             ).then_inc(cent_ready, 1)
                dve.wait_ge(rs_ready, n + 1)
                dve.wait_ge(cent_ready, KT * (n + 1))
                for d in range(KT + 1):
                    if d < KT:
                        dve.scalar_tensor_tensor(X[:, d, :], X[:, d, :], LNG[:, n, d:d + 1], RS[:, :],
                                                 ALU.mult, ALU.mult).then_inc(scaled, 1)
                    if d >= 1:
                        dve.wait_ge(x_ready, KT * n + d)
                        dve.tensor_tensor(XL[:, d - 1, :], X[:, d - 1, :], XH[:, d - 1, :].bitcast(F32),
                                          ALU.subtract).then_inc(xl_ready, 1)

            def ffn(n):
                u0 = UB[f"in{n}"] // 2
                with dve.Fori(0, 11) as i:
                    ahead(i + (u0 + 1), 0)
                    for c in range(2):
                        dve.wait_ge(half_done, i * 4 + (4 * u0 + c + 3))
                        dve.wait_ge(gate_ready[c], i + (11 * n + 1))
                        dve.wait_ge(hl_ready, i * 2 + (FT * n))
                        dve.tensor_tensor(halves(HF[:, c, :]), halves(SG[:, c, :]), tile_ps(c), ALU.mult
                                          ).then_inc(h_ready[c], 1)
                        dve.wait_ge(hh_ready, i * 2 + (FT * n + c + 1))
                        dve.tensor_tensor(HL[:, bass.ds(i * 2 + c, 1), :].rearrange("p a c -> p (a c)"), HF[:, c, :],
                                          HH[:, bass.ds(i * 2 + c, 1), :].rearrange("p a c -> p (a c)").bitcast(F32),
                                          ALU.subtract).then_inc(hl_ready, 1)
                    ahead(i + (u0 + 1), 1)
                u0 = UB[f"out{n}"] // 2
                ln = (0, 2, 3, 5)[n]
                dve.wait_ge(hl_ready, FT * (n + 1))
                clear_acc(ln)

                def pairs(i):
                    for j in range(6):
                        if j % 3 == 2:
                            for c in range(2):
                                d = 2 * (j // 3) + c
                                residual(i * 4 + d, i * 2 + j // 3, c, i * 12 + (4 * u0 + 2 * j + c + 1), ln, 0.5 / ALPHA)
                        if n < 3 or 6 * i + j < 10:
                            ahead(i * 3 + (u0 + j // 2 + 1), j % 2)

                if n < 3:
                    with dve.Fori(0, 2) as i:
                        pairs(i)
                else:
                    for i in range(2):
                        pairs(i)

            dve.memset(ACC[:, :], 0.0).then_inc(lo_ready, 1)
            dve.wait_ge(x_loaded, 16)
            for d in range(KT):
                dve.wait_ge(xh_ready, d + 1)
                dve.tensor_tensor(XL[:, d, :], X[:, d, :], XH[:, d, :].bitcast(F32), ALU.subtract).then_inc(xl_ready, 1)
            ahead(0, 0)
            ahead(0, 1)
            dve.wait_ge(const_loaded, 16 * 11)
            dve.tensor_tensor(LPR[:, :, :], LV[:, 0:4:2, :], LV[:, 1:4:2, :], ALU.mult).then_inc(lam_step, 1)
            dve.wait_ge(lam_step, 1)
            dve.tensor_reduce(DOT, LPR[:, :, :], AX.X, ALU.add).then_inc(lam_step, 1)
            dve.wait_ge(lam_exp, 1)
            dve.tensor_tensor(NLAM, EXPD[:, 1:2], EXPD[:, 0:1], ALU.subtract).then_inc(lam_step, 1)
            dve.wait_ge(lam_step, 3)
            dve.tensor_scalar(NLAM, NLAM, -LAMBDA_INIT, None, ALU.add).then_inc(lam_step, 1)
            dve.tensor_scalar(SUBG, SUBG, 1.0 - LAMBDA_INIT, None, ALU.mult).then_inc(lam_step, 1)
            dve.wait_ge(line_mm, 1)
            dve.tensor_tensor(LN8[:, :].rearrange("p (h c) -> p h c", h=2), PS[0:NH, 4:6, 0:LINE // 2],
                              LMASK[:, :].rearrange("p (h c) -> p h c", h=2), ALU.add).then_inc(line_sb, 1)
            dve.wait_ge(lam_step, 4)
            dve.scalar_tensor_tensor(SIGN, ROWS[:, PAIRS + 1:PAIRS + 2], NLAM, ROWS[:, PAIRS:PAIRS + 1],
                                     ALU.mult, ALU.add).then_inc(lam_step, 1)
            ffn(0)
            layer_norm(0)

            ub = UB["ret_in"] // 2
            with dve.Fori(0, RH) as h:
                for j in range(6):
                    if j < 2:
                        out = (RQ, RK)[j]
                        dve.wait_ge(rope_in[0], h * 2 + (j + 1))
                        dve.wait_ge(rope_in[1], h * 2 + (j + 1))
                        dve.wait_ge(rn_done, h * 4)
                        steps = ((RA[:, 0, :], RX[:, 0, :], COS[:, :], ALU.mult),
                                 (RA[:, 1, :], RX[:, 1, :], SIN[:, :], ALU.mult),
                                 (out[:, 0, :], RA[:, 0, :], RA[:, 1, :], ALU.subtract),
                                 (RA[:, 0, :], RX[:, 0, :], SIN[:, :], ALU.mult),
                                 (RA[:, 1, :], RX[:, 1, :], COS[:, :], ALU.mult),
                                 (out[:, 1, :], RA[:, 0, :], RA[:, 1, :], ALU.add))
                        for n, (dst, a, b, op) in enumerate(steps):
                            dve.wait_ge(rope_step, h * 12 + (6 * j + n))
                            dve.tensor_tensor(dst, a, b, op).then_inc(rope_step, 1)
                    ahead(h * 3 + (ub + j // 2 + 1), j % 2)
                dve.wait_ge(rt_loaded, h * 16 + 16)
                for jb in range(TB):
                    dve.wait_ge(rsc_done, h * 4 + jb + 1)
                    dve.tensor_tensor(PT[:, strip_at(jb):strip_at(jb + 1)], PS[:, 4 + jb, 0:SEQ - P * jb],
                                      RT[:, 0:SEQ - P * jb], ALU.mult).then_inc(pt_ready, 1)
                for b in range(DEC):
                    dve.wait_ge(s0_loaded[b % 2], h * 64 + 16 * (b // 2 + 1))
                    for t in range(2):
                        dve.wait_ge(kv_ready, h * 16 + (2 * b + t + 1))
                        dve.scalar_tensor_tensor(SB[:, b % 2, t, :], SB[:, b % 2, t, :], RT[:, SEQ + 4:SEQ + 5],
                                                 TMP[:, t, :], ALU.mult, ALU.add).then_inc(sn_ready, 1)
                dve.wait_ge(rod_ready, h + 1)
                dve.wait_ge(rope_step, h * 12 + 12)
                for e in range(1, 4):
                    dve.wait_ge(rn_sum, h * 3 + e - 1)
                    dve.tensor_tensor(RA[:, 1, :], RO[:, 0, :] if e == 1 else RA[:, 1, :], RO[:, e, :], ALU.add
                                      ).then_inc(rn_sum, 1)
                dve.wait_ge(rn_mean, h + 1)
                for e in range(4):
                    o_e = halves(RO[:, e, :])
                    dve.scalar_tensor_tensor(o_e, PS[:, 4:6, 0:HALF], -1.0 / DV, o_e, ALU.mult, ALU.add
                                             ).then_inc(rn_cent, 1)
                dve.wait_ge(rn_rs, h + 1)
                dve.wait_ge(rn_cent, h * 4 + 4)
                dve.wait_ge(g_ready[0], h * 2 + 2)
                dve.wait_ge(g_ready[1], h * 2 + 2)
                for e in range(4):
                    dve.tensor_tensor(RO[:, e, :], RO[:, e, :], RA[:, 0, :], ALU.mult).then_inc(rn_mul, 1)
                for e in range(4):
                    dve.wait_ge(rn_mul, h * 4 + e + 1)
                    dve.tensor_tensor(OG[:, bass.ds(h * 4 + e, 1), :].rearrange("p a c -> p (a c)"), RO[:, e, :],
                                      GT[:, e, :], ALU.mult).then_inc(rn_done, 1)
            for d in range(4 * RH):
                dve.wait_ge(og_hi, d + 1)
                dve.tensor_tensor(HL[:, d, :], OG[:, d, :], HH[:, d, :].bitcast(F32), ALU.subtract
                                  ).then_inc(og_lo, 1)
            clear_acc(1)
            u0 = UB["ret_out"] // 2
            with dve.Fori(0, 4) as i:
                ahead(i + (u0 + 1), 0)
                for c in range(2):
                    residual(i * 2 + c, i, c, i * 4 + (4 * u0 + 2 + c + 1), 1, 1.0 / ALPHA, True)
                ahead(i + (u0 + 1), 1)
            layer_norm(1)
            for r in range(2):
                dve.wait_ge(s_out[r], 16 * RH * DEC // 2)
            dve.wait_ge(spr_out, 16 * RH)
            ffn(1)
            layer_norm(2)
            ffn(2)
            layer_norm(3)

            uq, uk = UB["q"] // 2, UB["kv"] // 2
            with dve.Fori(0, 2) as i:
                for r in range(2):
                    ahead(i + (uq + 1), r)
            with dve.Fori(0, 2) as i:
                for r in range(2):
                    ahead(i + (uk + 1), r)
            with dve.Fori(0, 2) as i:
                for r in range(2):
                    for c in range(2):
                        n = 2 * r + c
                        dve.wait_ge(vs_ready[c], i * 2 + (r + 1))
                        dve.tensor_copy(VN[:, bass.ds(i * 4 + n, 1), :].rearrange("p a c -> p (a c)"),
                                        VS[:, c, SEQ:T]).then_inc(vn_ready, 1)
                        for g in range(2):
                            dve.wait_ge(dvt_done, i * 8 + (2 * n + g + 1))
                            dve.tensor_copy(VTOK[:, 2 * g:2 * g + 2, bass.ds(i * 512 + n * P, P)],
                                            PS[:, 4 + g, 0:2 * P].rearrange("p (j e) -> p j e", j=2)
                                            ).then_inc(dvt_ready, 1)
                        dve.wait_ge(v8d_done, i * 4 + (n + 1))
                        dve.tensor_copy(V8D[:, bass.ds(i * 512 + n * P, P)], PS[0:DEC, 6, 0:P]).then_inc(v8d_ready, 1)
                    ahead(i + (uk + 3), r)
            dve.wait_ge(bias_loaded, 32)
            dve.tensor_scalar(RBX[:, :], RBX[:, :], DH ** 0.5, None, ALU.mult).then_inc(rbx_ready, 1)
            dve.memset(PRD[:, :, :], 0.0).then_inc(newprod_ready, 1)
            dve.wait_ge(newprod_ready, 1)
            dve.wait_ge(q_ready[0], NH // 2)
            dve.wait_ge(q_ready[1], NH // 2)
            dve.wait_ge(k_ready[0], NH // 2)
            dve.wait_ge(k_ready[1], NH // 2)
            for m in range(2):
                rows = slice(m * DH, (m + 1) * DH)
                dve.tensor_tensor(PRD[rows, :, m].rearrange("p (b h) -> p b h", b=DEC),
                                  QT[rows, :, SEQ:T].rearrange("p h b -> p b h"),
                                  KTT[rows, :, SEQ:T].rearrange("p h b -> p b h"), ALU.mult).then_inc(newprod_ready, 1)
            dve.wait_ge(v_out, 16 * (TB + 1))

            def biased(i, part, n):
                r, qb = n // TB, n % TB
                kw = (qb + 1) * P
                j0 = SEQ - kw
                ss = SS[n % 2]
                if qb == 0:
                    dve.wait_ge(strip_loaded[r], i * 16 + (32 * part + 16))
                dve.wait_ge(sc_done, i * 8 + (16 * part + n + 1))
                dve.wait_ge(wtr_done, i * 8 + (16 * part + max(n - 1, 0)))
                for m in range(2):
                    dve.scalar_tensor_tensor(ss[:, m, 0:kw], PS[:, (4, 2)[n % 2] + m, 0:kw], DH ** -0.5,
                                             STRIP[:, r, j0:j0 + kw], ALU.mult, ALU.add).then_inc(ss_ready, 1)
                dve.wait_ge(ss_ready, i * 16 + (32 * part + 2 * n + 2))
                dve.tensor_reduce(ST[:, 8 * (n % 2):8 * (n % 2) + 2], ss[:, :, 0:kw], AX.X, ALU.max, negate=True
                                  ).then_inc(mx_ready, 1)

            def weights(i, part, n):
                kw = (n % TB + 1) * P
                o = 8 * (n % 2)
                ss = SS[n % 2]
                dve.wait_ge(ex_ready, i * 16 + (32 * part + 2 * n + 2))
                dve.reciprocal(ST[:, o + 4:o + 6], ST[:, o + 2:o + 4]).then_inc(rc_ready, 1)
                dve.wait_ge(rc_ready, i * 16 + (32 * part + 2 * n + 1))
                dve.tensor_tensor(ST[:, o + 6:o + 7], ST[:, o + 5:o + 6], NLAM, ALU.mult).then_inc(rc_ready, 1)
                dve.tensor_scalar(ss[:, 0, 0:kw], ss[:, 0, 0:kw], ST[:, o + 4:o + 5], None, ALU.mult
                                  ).then_inc(s0n_ready, 1)
                dve.wait_ge(rc_ready, i * 16 + (32 * part + 2 * n + 2))
                dve.wait_ge(s0n_ready, i * 8 + (16 * part + n + 1))
                dve.scalar_tensor_tensor(ss[:, 0, 0:kw], ss[:, 1, 0:kw], ST[:, o + 6:o + 7], ss[:, 0, 0:kw],
                                         ALU.mult, ALU.add).then_inc(ww_ready, 1)

            def heads(part):
                with dve.Fori(0, NH // 4) as i:
                    biased(i, part, 0)
                    for n in range(2 * TB):
                        if n + 1 < 2 * TB:
                            biased(i, part, n + 1)
                        weights(i, part, n)

            heads(0)
            def step(n):
                dve.wait_ge(soft_step, n)

            dve.wait_ge(page_used[3], 2 * DEC)
            dve.tensor_reduce(NMAX, PS[:, 0:2, :].rearrange("p g c -> p (g c)"), AX.X, ALU.max, negate=True
                              ).then_inc(soft_step, 1)
            step(1)
            dve.wait_ge(newscore_done, 1)
            dve.tensor_scalar(NMAX1, PS[:, 2, 0:1], -1.0, NMAX, ALU.mult, ALU.min).then_inc(soft_step, 1)
            step(2)
            dve.tensor_scalar(SHIFT, NMAX1, DH ** -0.5, None, ALU.mult).then_inc(shift_ready, 1)
            dve.wait_ge(dec_exp, 2)
            dve.tensor_tensor(TOTAL, SUM, OWN_EXP, ALU.add).then_inc(soft_step, 1)
            step(3)
            dve.reciprocal(TOTAL, TOTAL).then_inc(soft_step, 1)
            step(4)
            dve.tensor_tensor(TOTAL, TOTAL, SIGN, ALU.mult).then_inc(soft_step, 1)
            step(5)
            dve.tensor_scalar(COMB[:, :], ROWS[:, 0:PAIRS], TOTAL, None, ALU.mult).then_inc(comb_ready, 1)
            dve.wait_ge(comb_ready, 1)
            dve.tensor_scalar(COMB_OWN[:, :], COMB[:, :], OWN_EXP, None, ALU.mult).then_inc(comb_ready, 1)
            dve.wait_ge(wd_done, 1)
            dve.tensor_copy(WD[:, :, :].rearrange("p g x -> p (g x)"), PS[:, 4, :]).then_inc(wd_ready, 1)
            dve.wait_ge(wd_done, 2)
            dve.wait_ge(vn_ready, NH)
            dve.tensor_tensor(OWN[:, :, :], PS[:, 3, 0:PAIRS].rearrange("p (b h) -> p h b", b=DEC), VN[:, :, :], ALU.mult
                              ).then_inc(wd_ready, 1)
            heads(1)
            dve.wait_ge(page_used[3], 4 * DEC)
            dve.tensor_tensor(SCA[0:PAIRS, :].rearrange("p (h c) -> p h c", h=NH),
                              PS[0:PAIRS, 0:2, :].rearrange("p g (h c) -> p (g h) c", c=P),
                              ROWS[0:PAIRS, 2 * PAIRS + 2:2 * PAIRS + 2 + NH].unsqueeze(2).to_broadcast([PAIRS, NH, P]),
                              ALU.mult).then_inc(ov_step, 1)
            dve.wait_ge(ov_step, 1)
            dve.tensor_reduce(OVR[:, :], SCA[0:PAIRS, :].rearrange("p (h c) -> p c h", h=NH), AX.X, ALU.add
                              ).then_inc(ov_step, 1)
            dve.wait_ge(ov_turned, 1)
            dve.tensor_tensor(OF[:, :, SEQ:T], PS[:, 6, 0:PAIRS].rearrange("p (b h) -> p h b", b=DEC), OWN[:, :, :],
                              ALU.add).then_inc(new_step, 1)
            dve.wait_ge(of_ready, NH)
            dve.wait_ge(new_step, 1)
            for d in range(NH):
                if d >= 2:
                    dve.wait_ge(on_mm, d - 1)
                dve.tensor_tensor(SG[:, d % 2, :], OF[:, d, :], OF[:, d, :], ALU.mult).then_inc(on_sq, 1)
            for d in range(NH + 1):
                if d < NH:
                    dve.wait_ge(on_rs, d + 1)
                    dve.scalar_tensor_tensor(OF[:, d, :], OF[:, d, :], SUBG, RSN[:, d, :], ALU.mult, ALU.mult
                                             ).then_inc(on_mul, 1)
                if d >= 1:
                    dve.wait_ge(on_hi, d)
                    dve.tensor_tensor(HL[:, d - 1, :], OF[:, d - 1, :], HH[:, d - 1, :].bitcast(F32), ALU.subtract
                                      ).then_inc(on_lo, 1)
            clear_acc(4)
            u0 = UB["o"] // 2
            with dve.Fori(0, 2) as i:
                for r in range(2):
                    for c in range(2):
                        residual(i * 4 + (2 * r + c), i * 2 + r, c, i * 4 + (4 * u0 + 2 * r + c + 1), 4,
                                 1.0 / ALPHA, True)
                    ahead(i + (u0 + 1), r)
            layer_norm(4)
            ffn(3)
            layer_norm(5)


def shape_tables():
    f = np.float32
    identity = np.eye(P, dtype=f)
    half = DK // 2
    inv = f(10000.0) ** (-np.arange(half, dtype=f) / f(half))
    pos = np.concatenate([np.arange(SEQ), np.full(DEC, PAST)]).astype(f)
    ang = (inv[:, None] * pos[None, :]).astype(f).astype(np.float64)
    rope = np.stack([np.cos(ang), np.sin(ang)]).astype(f)
    gamma = 1.0 - 2.0 ** (-5.0 - np.arange(RH, dtype=np.float64))
    ret = np.zeros((RH, P, T), f)
    d = np.arange(SEQ)[None, :] - np.arange(P)[:, None]
    tok = np.arange(TB)[None, :] * P + np.arange(P)[:, None]
    for h in range(RH):
        ret[h, :, :SEQ] = np.where(d >= 0, gamma[h] ** np.maximum(d, 0), 0.0)
        ret[h, :, SEQ:SEQ + TB] = gamma[h] ** (SEQ - 1 - tok)
        ret[h, :, SEQ + TB] = gamma[h]

    def bucket(n):
        n = np.maximum(n, 0)
        exact = BUCKETS // 2
        nf = np.maximum(n, 1).astype(f)
        large = exact + (np.log(nf / f(exact)) / f(math.log(128 / exact)) * f(BUCKETS - exact)).astype(np.int32)
        return np.where(n < exact, n, np.minimum(large, BUCKETS - 1))

    n = SEQ - 1 - np.arange(LINE)
    line = (bucket(n)[None, :] == np.arange(BUCKETS)[:, None]).astype(f)
    mask = np.repeat(np.where(n < 0, MASKED, 0.0).astype(f)[None, :], NH, 0)
    past = (bucket(PAST - np.arange(PAST))[None] == np.arange(BUCKETS)[:, None]).astype(f)
    row = np.arange(P)
    rows = np.concatenate([row[:, None] // 2 == np.arange(PAIRS), row[:, None] % 2 == np.arange(2),
                           np.zeros((P, PAIRS)), row[:, None] % NH == np.arange(NH)], 1).astype(f)
    return identity, rope, ret, line, mask, past, rows


def kernel(x_prompt, x_sample, state_ret, cache_k, cache_v, page_table, ln_g, ln_b, ffn_w_in, ffn_w_out,
           ret_w_in, ret_w_out, w_kv, diff_w_q, diff_w_o, diff_lambda, diff_subln_g, rel_bias):
    from concourse import bacc
    from concourse.bass_utils import run_bass_kernel_spmd

    def tiles(w):
        w = np.asarray(w)
        return np.ascontiguousarray(w.reshape(-1, P, w.shape[1] // UC, UC).transpose(2, 1, 0, 3))

    x = np.concatenate([np.asarray(x_prompt)[0], np.asarray(x_sample)[:, 0]])
    ffn_in = np.asarray(ffn_w_in).reshape(4, D, 2 * FFN)
    w_in = np.stack([tiles(w).reshape(2, FFN // UC, P, KT, UC).swapaxes(0, 1) for w in ffn_in])
    w_out = np.stack([tiles(w) for w in np.asarray(ffn_w_out).reshape(4, FFN, D)])
    r = tiles(np.asarray(ret_w_in)[0])
    r = np.stack([np.stack([r[h], r[4 + h], r[8 + 2 * h], r[9 + 2 * h], r[16 + 2 * h], r[17 + 2 * h]])
                  for h in range(RH)])
    n_pool = np.asarray(cache_k).shape[0]
    identity, rope, ret, line, mask, past, rows = shape_tables()
    arrays = {
        "x_t": x.T.reshape(KT, P, T).swapaxes(0, 1),
        "w_in": w_in.reshape(88, P, KT, UC),
        "w_out": w_out.reshape(16, P, FT, UC),
        "w_ret_in": r.reshape(24, P, KT, UC),
        "w_ret_out": tiles(np.asarray(ret_w_out)[0]),
        "w_q": tiles(np.asarray(diff_w_q)[0]),
        "w_kv": tiles(w_kv),
        "w_o": tiles(np.asarray(diff_w_o)[0]),
        "ln_g": np.asarray(ln_g).reshape(6, KT, P).transpose(2, 0, 1),
        "ln_b": np.asarray(ln_b).reshape(6, KT, P).transpose(2, 0, 1),
        "state": np.asarray(state_ret)[0].reshape(DEC, RH, 2, P, DV).swapaxes(2, 3),
        "cache_kt": np.asarray(cache_k).transpose(0, 3, 2, 1).reshape(n_pool, P, NH * PAGE),
        "cache_v": np.asarray(cache_v).reshape(n_pool, PAGE, D),
        "pages": np.asarray(page_table).reshape(1, DEC * NPG),
        "lam_vecs": np.broadcast_to(np.asarray(diff_lambda)[0], (P, 4, DH)),
        "subln_g": np.asarray(diff_subln_g).reshape(P, 1),
        "rel_bias": np.asarray(rel_bias),
        "identity": identity, "rope": rope, "ret_tab": ret, "onehot_line": line, "line_mask": mask,
        "onehot_past": past, "row_tab": rows,
        "rel_rows": np.broadcast_to(np.asarray(rel_bias)[:, None, :, None], (BUCKETS, DEC, NH, 2)).reshape(BUCKETS, P),
    }
    arrays = {k: np.ascontiguousarray(v) for k, v in arrays.items()}
    nc = bacc.Bacc("TRN2", target_bir_lowering=False, num_devices=1)
    args = {k: nc.dram_tensor(k, v.shape, mybir.dt.from_np(v.dtype), kind="ExternalInput").ap()
            for k, v in arrays.items()}
    outs = {"y_t": (P, KT, T), "state_p": (RH, P, 2, DV), "state_s": (DEC, RH, P, 2, DV), "k_t": (P, NH, T),
            "v_p": (TB, P, D), "v_s": (DEC, D)}
    for k, shape in outs.items():
        args[k] = nc.dram_tensor(k, shape, F32, kind="ExternalOutput").ap()
    for k, shape in {"bias_rep": (NH, P * LINE), "v_rows": (DEC, DV)}.items():
        args[k] = nc.dram_tensor(k, shape, F32, kind="Internal").ap()
    trunk_kernel(nc, **args)
    r = run_bass_kernel_spmd(nc, [arrays], core_ids=[0]).results[0]
    y = r["y_t"].swapaxes(0, 1).reshape(D, T).T
    k = r["k_t"].transpose(2, 1, 0)
    return (y[None, :SEQ], y[SEQ:, None],
            r["state_p"].swapaxes(1, 2).reshape(1, 1, RH, DK, DV),
            r["state_s"].swapaxes(2, 3).reshape(1, DEC, RH, DK, DV),
            k[None, :SEQ], r["v_p"].reshape(1, SEQ, NH, 2 * DH),
            k[SEQ:, None], r["v_s"].reshape(DEC, 1, NH, 2 * DH))
```

```python
import math
from contextlib import ExitStack

import numpy as np

import concourse.bass as bass
from concourse import mybir

F32 = mybir.dt.float32
F32R = mybir.dt.float32r
I32 = mybir.dt.int32
ACT = mybir.ActivationFunctionType
ALU = mybir.AluOpType
AX = mybir.AxisListType

P = 128
D = 1024
SEQ = 512
DEC = 8
T = SEQ + DEC
HALF = T // 2
KT = D // P
FFN = 2816
FT = FFN // P
DEPTH = 2
PAST = 1024
PAGE = 128
NPG = PAST // PAGE
RH = 4
DK = D // RH
DV = 2 * DK
DH = 64
NH = 8
TB = SEQ // P
BUCKETS = 32
EPS = 1e-5
ALPHA = (2.0 * DEPTH) ** 0.25
LAMBDA_INIT = 0.8 - 0.6 * math.exp(-0.3)
MASKED = -1e30

PAIRS = DEC * NH

UC = 256
UK = 8
USZ = UK * UC
LINE = 640

STAGES = [("in0", 22), ("out0", 12), ("ret_in", 24), ("ret_out", 8), ("in1", 22), ("out1", 12),
          ("in2", 22), ("out2", 12), ("q", 4), ("kv", 8), ("o", 4), ("in3", 22), ("out3", 12)]
UB, UNITS = {}, 0
for _name, _nu in STAGES:
    UB[_name] = UNITS
    UNITS += _nu


def trunk_kernel(nc, x_t, w_in, w_out, w_ret_in, w_ret_out, w_q, w_kv, w_o, ln_g, ln_b, state,
                 cache_kt, cache_v, pages, lam_vecs, subln_g, rel_bias,
                 identity, rope, ret_tab, onehot_line, line_mask, onehot_past, rel_rows, row_tab,
                 y_t, state_p, state_s, k_t, v_p, v_s, bias_rep, v_rows):
    ctx = ExitStack()
    with ctx:
        base = [(nc.sbuf_base + 31) // 32 * 32]

        def at(name, shape, dt, off):
            return nc.alloc_sbuf_tensor_at(name, shape, dt, offset=off)

        def size(shape):
            return int(np.prod(shape[1:])) * 4

        def new(name, shape, dt=F32):
            off = base[0]
            base[0] += (size(shape) + 31) // 32 * 32
            return at(name, shape, dt, off)

        def sem(name):
            return ctx.enter_context(nc.semaphore(name))

        WR = new("WR", [P, 2, UK, UC])
        WH = new("WH", [P, 2, UK, UC], F32R)
        WL = new("WL", [P, 2, UK, UC], F32R)
        XH = new("XH", [P, KT, T], F32R)
        XL = new("XL", [P, KT, T], F32R)
        off_hh = base[0]
        HH = new("HH", [P, FT, T], F32R)
        off_hl = base[0]
        HL = new("HL", [P, FT, T], F32R)
        off_x = base[0]
        X = new("X", [P, KT, T])
        off_ft = base[0]
        SG = new("SG", [P, 2, T])
        HF = new("HF", [P, 2, T])
        IDN = new("IDN", [P, P])
        ONES = new("ONES", [P, P])
        LNG = new("LNG", [P, 6, KT])
        LNB = new("LNB", [P, 6, KT])
        COL = new("COL", [P, 16])
        ROWS = new("ROWS", [P, 2 * PAIRS + 2 + NH])
        PTAB = new("PTAB", [1, DEC * NPG], I32)
        off_sp = base[0]
        EPS_LN, EPS_1, SUBG, NLAM, SIGN = (COL[:, i:i + 1] for i in range(5))
        NMAX, NMAX1, SHIFT, SUM, OWN_EXP, TOTAL = (COL[:, i:i + 1] for i in range(10, 16))
        DOT, EXPD = COL[:, 6:8], COL[:, 8:10]
        SQ = SG
        RS = at("RS", [P, T], F32, off_ft + 2 * T * 4)
        ACC = at("ACC", [P, T], F32, off_ft + 3 * T * 4)

        off_t = off_hh + 15 * T * 4
        OHL = at("OHL", [BUCKETS, LINE], F32, off_t)
        LMASK = at("LMASK", [NH, LINE], F32, off_t + 2560)
        RB = at("RB", [BUCKETS, NH], F32, off_t + 9728)
        LN8 = at("LN8", [NH, LINE], F32, off_t + 9792)
        LV = at("LV", [P, 4, DH], F32, off_t + 12352)
        LPR = at("LPR", [P, 2, DH], F32, off_t + 13376)

        VBC = at("VBC", [P, 4, DV], F32, off_hh + 8192)
        VT = at("VT", [P, 4, T], F32, off_hh + 16384)
        RO = at("RO", [P, 4, T], F32, off_hh + 16384)
        GT = at("GT", [P, 4, T], F32, off_hh + 24704)
        VTK = at("VTK", [P, TB, DV], F32, off_hh + 33024)
        KTK = at("KTK", [P, TB, DK], F32, off_hh + 41216)
        OG = at("OG", [P, 4 * RH, T], F32, off_hl)
        SB = [at("SB0", [P, 2, DV], F32, off_hl + 4 * RH * T * 4),
              at("SB1", [P, 2, DV], F32, off_hl + 4 * RH * T * 4 + 4096),
              at("SB2", [P, 2, DV], F32, off_hh),
              at("SB3", [P, 2, DV], F32, off_hh + 4096),
              at("SB4", [P, 2, DV], F32, off_hh + 4 * RH * T * 4),
              at("SB5", [P, 2, DV], F32, off_hh + 4 * RH * T * 4 + 4096),
              at("SB6", [P, 2, DV], F32, off_hh + 4 * RH * T * 4 + 8192)]
        TMP = at("TMP", [P, 2, DV], F32, off_hl + 4 * RH * T * 4 + 8192)
        RQ = at("RQ", [P, 2, T], F32, off_x)
        RK = at("RK", [P, 2, T], F32, off_x + 4160)
        RT = at("RT", [P, T], F32, off_x + 8320)
        PT = at("PT", [P, 1280], F32, off_x + 10400)
        ODEC, ODEC2 = TMP[0:DEC, 0, :], TMP[0:DEC, 1, :]
        QD = at("QD", [P, 2, DEC * DEC], F32, off_x + 15520)
        KD = at("KD", [P, 2, DEC], F32, off_x + 16032)
        GD = at("GD", [P, 4, DEC], F32, off_x + 16096)
        DST = at("DST", [P, 8], F32, off_x + 16224)
        COS = at("COS", [P, T], F32, off_sp)
        SIN = at("SIN", [P, T], F32, off_sp + 2080)
        SPR = at("SPR", [P, 2, DV], F32, off_sp + 4160)
        V8 = at("V8", [DEC, DV], F32, off_sp + 8256)
        RX = at("RX", [P, 2, T], F32, off_ft)
        RA = at("RA", [P, 2, T], F32, off_ft + 4160)

        QT = at("QT", [P, NH, T], F32, off_hh)
        KTT = at("KTT", [P, NH, T], F32, off_hh + 16640)
        WT = at("WT", [P, 1280], F32, off_hh + 33280)
        STRIP = at("STRIP", [P, 2, SEQ], F32, off_hh + 41472)
        OF = at("OF", [P, NH, T], F32, off_hl)
        o = off_hl + 16640
        VTOK = at("VTOK", [P, TB, D], F32, o)
        SS = [at("SS0", [P, 2, SEQ], F32, o + 16384), at("SS1", [P, 2, SEQ], F32, off_sp + 4928)]
        QHD = [at("QHD0", [P, SEQ], F32, o + 22528), at("QHD1", [P, SEQ], F32, off_ft + 6208)]
        KHD = [at("KHD0", [P, SEQ], F32, o + 20480), at("KHD1", [P, SEQ], F32, off_hh + 38400)]
        VHD = [at("VHD0", [P, TB, P], F32, o + 26624), at("VHD1", [P, TB, P], F32, o + 24576)]
        RSN = at("RSN", [P, NH, T], F32, off_hh + 16640)
        PG = at("PG", [P, 4, D], F32, off_x)
        SCA = at("SCA", [P, PAST], F32, off_sp)
        OHP = at("OHP", [BUCKETS, PAST], F32, off_sp)
        RBX = at("RBX", [BUCKETS, P], F32, off_sp + 4096)
        VN = at("VN", [P, NH, DEC], F32, off_sp + 4608)
        ST = at("ST", [P, 16], F32, off_sp + 4864)
        V8D = at("V8D", [DEC, D], F32, off_sp + 4928)
        VS = at("VS", [P, 2, T], F32, off_ft)
        QP = at("QP", [P, NH, P], F32, off_ft)
        WP = at("WP", [P, 2, NPG, PAIRS], F32, off_ft)
        WD = at("WD", [P, NPG, PAIRS], F32, off_ft + 4160)
        o = off_sp + 4928 + 4096
        PRD = at("PRD", [P, PAIRS, 2], F32, o)
        OVR = at("OVR", [PAIRS, P], F32, o)
        COMB = at("COMB", [P, PAIRS], F32, o + 512)
        COMB_OWN = at("COMB_OWN", [P, PAIRS], F32, o + 768)
        OWN = at("OWN", [P, NH, DEC], F32, o + 1024)
        end = max(off_sp + 8256 + DV * 4, off_sp + 4928 + D * 4)
        assert end <= nc.sbuf_usable_end, end - nc.sbuf_usable_end

        PS = ctx.enter_context(nc.psum_tensor("PS", [P, 8, 512], F32))

        raw_loaded = [sem("raw_loaded0"), sem("raw_loaded1")]
        hi_ready = sem("hi_ready")
        lo_ready = sem("lo_ready")
        half_done = sem("half_done")
        gate_ready = [sem("gate_ready0"), sem("gate_ready1")]
        h_ready = [sem("h_ready0"), sem("h_ready1")]
        hh_ready = sem("hh_ready")
        hl_ready = sem("hl_ready")
        y_ready = sem("y_ready")
        acc_ready = sem("acc_ready")
        mean_ready = sem("mean_ready")
        cent_ready = sem("cent_ready")
        sq_ready = sem("sq_ready")
        sqm_done = sem("sqm_done")
        ln_step = sem("ln_step")
        rs_ready = sem("rs_ready")
        scaled = sem("scaled")
        xh_ready = sem("xh_ready")
        x_ready = sem("x_ready")
        xl_ready = sem("xl_ready")
        x_loaded = [sem(f"x_loaded{i}") for i in range(KT // 2)]
        const_loaded = sem("const_loaded")
        ones_ready = sem("ones_ready")
        line_mm = sem("line_mm")
        line_sb = sem("line_sb")
        line_out = sem("line_out")
        lam_step = sem("lam_step")
        lam_exp = sem("lam_exp")
        rope_in = [sem("rope_in0"), sem("rope_in1")]
        rope_step = sem("rope_step")
        v_ready = [sem("v_ready0"), sem("v_ready1")]
        g_ready = [sem("g_ready0"), sem("g_ready1")]
        rt_loaded = sem("rt_loaded")
        ktr_done = sem("ktr_done")
        ktk_ready = sem("ktk_ready")
        vtr_done = sem("vtr_done")
        vtk_ready = sem("vtk_ready")
        v8_mm = sem("v8_mm")
        v8_ready = sem("v8_ready")
        v8_out = sem("v8_out")
        vbc_loaded = [sem("vbc_loaded0"), sem("vbc_loaded1")]
        rsc_done = sem("rsc_done")
        pt_ready = sem("pt_ready")
        ro_done = sem("ro_done")
        ro_ready = sem("ro_ready")
        rst_done = sem("rst_done")
        spr_ready = sem("spr_ready")
        spr_out = sem("spr_out")
        s0_loaded = [sem(f"s0_loaded{i}") for i in range(7)]
        kv_ready = sem("kv_ready")
        sn_ready = sem("sn_ready")
        snq_done = sem("snq_done")
        s_out = [sem(f"s_out{i}") for i in range(7)]
        qd_zero = sem("qd_zero")
        dec_ready = sem("dec_ready")
        dn_step = sem("dn_step")
        dn_act = sem("dn_act")
        dn_ready = sem("dn_ready")
        dt_done = sem("dt_done")
        dp_ready = sem("dp_ready")
        rn_sum = sem("rn_sum")
        rn_mean = sem("rn_mean")
        rn_cent = sem("rn_cent")
        rn_sq = sem("rn_sq")
        rn_sqm = sem("rn_sqm")
        rn_step = sem("rn_step")
        rn_rs = sem("rn_rs")
        rn_mul = sem("rn_mul")
        rn_done = sem("rn_done")
        og_hi = sem("og_hi")
        og_lo = sem("og_lo")
        q_ready = [sem("q_ready0"), sem("q_ready1")]
        k_ready = [sem("k_ready0"), sem("k_ready1")]
        k_out = sem("k_out")
        bias_loaded = sem("bias_loaded")
        rbx_ready = sem("rbx_ready")
        slot_step = sem("slot_step")
        qp_ready = sem("qp_ready")
        wp_ready = sem("wp_ready")
        vs_ready = [sem("vs_ready0"), sem("vs_ready1")]
        vn_ready = sem("vn_ready")
        dvt_done = sem("dvt_done")
        dvt_ready = sem("dvt_ready")
        v8d_done = sem("v8d_done")
        v8d_ready = sem("v8d_ready")
        v_out = sem("v_out")
        head_copied = sem("head_copied")
        strip_loaded = [sem("strip_loaded0"), sem("strip_loaded1")]
        sc_done = sem("sc_done")
        ss_ready = sem("ss_ready")
        mx_ready = sem("mx_ready")
        ex_ready = sem("ex_ready")
        rc_ready = sem("rc_ready")
        s0n_ready = sem("s0n_ready")
        ww_ready = sem("ww_ready")
        wtr_done = sem("wtr_done")
        wt_ready = sem("wt_ready")
        pv_done = sem("pv_done")
        of_ready = sem("of_ready")
        pt_loaded = sem("pt_loaded")
        page_loaded = [sem(f"page_loaded{i}") for i in range(4)]
        page_used = [sem(f"page_used{i}") for i in range(4)]
        newprod_ready = sem("newprod_ready")
        newscore_done = sem("newscore_done")
        shift_ready = sem("shift_ready")
        dec_exp = sem("dec_exp")
        comb_ready = sem("comb_ready")
        wd_done = sem("wd_done")
        wd_ready = sem("wd_ready")
        soft_step = sem("soft_step")
        ov_step = sem("ov_step")
        ov_turned = sem("ov_turned")
        res_done = [sem("res_done0"), sem("res_done1")]
        acc_zero = sem("acc_zero")
        new_step = sem("new_step")
        on_sq = sem("on_sq")
        on_mm = sem("on_mm")
        on_ln = sem("on_ln")
        on_rs = sem("on_rs")
        on_mul = sem("on_mul")
        on_hi = sem("on_hi")
        on_lo = sem("on_lo")
        y_out = sem("y_out")

        block = ctx.enter_context(nc.Block())

        def halves(ap):
            return ap.rearrange("p (h c) -> p h c", h=2)

        def tile_ps(c):
            return PS[:, 2 * c:2 * c + 2, 0:HALF]

        def strip_at(jb):
            return sum(SEQ - P * j for j in range(jb))

        def s0_slot(h, b):
            if h is None:
                return b % 7, (2 * (RH - 1) if b % 7 < 4 else 0) + b // 7 + 1
            return b % 4, h * 2 + (b // 4 + 1)

        def turned_at(qb):
            return P * qb * (qb + 1) // 2

        @block.sync
        def _(sp):
            def load(src, u, r, nk, first=False):
                if not first:
                    sp.wait_ge(lo_ready, u * 2 + r)
                sp.dma_start(WR[:, r, 0:nk, :], src).then_inc(raw_loaded[r], 16)

            def ffn_loads(n):
                u_in, u_out = UB[f"in{n}"] // 2, UB[f"out{n}"] // 2
                for r in range(2):
                    load(w_in[22 * n + r], u_in, r, UK, n == 0)
                    if n == 0:
                        for d in range(KT // 4 * r, KT // 4 * (r + 1)):
                            sp.dma_start(X[:, 2 * d:2 * d + 2, :], x_t[:, 2 * d:2 * d + 2, :]).then_inc(x_loaded[d], 16)
                with sp.Fori(1, 11) as i:
                    for r in range(2):
                        load(w_in[bass.ds(i * 2 + (22 * n + r), 1)].rearrange("a p k c -> (a p) k c"),
                             i + u_in, r, UK)
                with sp.Fori(0, 2) as i:
                    for j in range(6):
                        k0 = UK * (j % 3)
                        nk = min(UK, FT - k0)
                        load(w_out[bass.ds(i * 2 + (4 * n + j // 3), 1)][:, :, k0:k0 + nk, :]
                             .rearrange("a p k c -> (a p) k c"), i * 3 + (u_out + j // 2), j % 2, nk)

            def plain_loads(w, stage, n):
                u0 = UB[stage] // 2
                with sp.Fori(0, n // 2) as i:
                    for r in range(2):
                        load(w[bass.ds(i * 2 + r, 1)].rearrange("a p k c -> (a p) k c"), i + u0, r, UK)

            ffn_loads(0)
            plain_loads(w_ret_in, "ret_in", 24)
            with sp.Fori(0, 4) as i:
                for r in range(2):
                    load(w_ret_out[bass.ds(i, 1)][:, :, UK * r:UK * r + UK, :]
                         .rearrange("a p k c -> (a p) k c"), i + UB["ret_out"] // 2, r, UK)
            ffn_loads(1)
            ffn_loads(2)
            plain_loads(w_q, "q", 4)
            plain_loads(w_kv, "kv", 8)
            for r in range(2):
                load(w_o[r], UB["o"] // 2, r, UK)
            sp.dma_start(PTAB[:, :], pages).then_inc(pt_loaded, 16)
            sp.wait_ge(pt_loaded, 16)
            sp.wait_ge(xl_ready, KT * 5)

            def k_page(b, pg):
                s = pg % 4
                if pg >= 4 or not isinstance(b, int):
                    sp.wait_ge(page_used[s], b * 2 + pg // 4)
                page = sp.value_load(PTAB[0:1, bass.ds(b * NPG + pg, 1)], min_val=0,
                                     max_val=cache_kt.shape[0] - 1)
                sp.dma_start(PG[:, s, :], cache_kt[bass.ds(page, 1)].rearrange("a p c -> (a p) c")
                             ).then_inc(page_loaded[s], 16)

            for pg in range(NPG):
                k_page(0, pg)
            with sp.Fori(1, DEC) as b:
                for pg in range(NPG):
                    k_page(b, pg)
            with sp.Fori(0, DEC) as b:
                for pg in range(NPG):
                    s = pg % 4
                    sp.wait_ge(page_used[s], b * 2 + (16 + pg // 4))
                    page = sp.value_load(PTAB[0:1, bass.ds(b * NPG + pg, 1)], min_val=0,
                                         max_val=cache_v.shape[0] - 1)
                    sp.dma_start(PG[:, s, :], cache_v[bass.ds(page, 1)].rearrange("a p c -> (a p) c")
                                 ).then_inc(page_loaded[s], 16)
            for r in range(2):
                load(w_o[2 + r], UB["o"] // 2 + 1, r, UK)
            ffn_loads(3)

        @block.gpsimd
        def _(pool):
            pool.memset(ONES[:, :], 1.0).then_inc(ones_ready, 1)
            pool.memset(COL[:, 0:1], EPS / ALPHA ** 2).then_inc(ones_ready, 1)
            pool.memset(COL[:, 1:2], EPS).then_inc(ones_ready, 1)
            for dst, src in ((IDN[:, :], identity), (LNG[:, :, :], ln_g), (LNB[:, :, :], ln_b),
                             (OHL[:, :], onehot_line), (LMASK[:, :], line_mask), (ROWS[:, :], row_tab),
                             (RB[:, :], rel_bias), (COL[:, 2:3], subln_g), (LV[:, :, :], lam_vecs),
                             (COS[:, :], rope[0]), (SIN[:, :], rope[1])):
                pool.dma_start(dst, src).then_inc(const_loaded, 16)
            pool.wait_ge(line_sb, 1)
            pool.dma_start(bias_rep.rearrange("h (p c) -> h p c", p=P),
                           LN8[:, :].unsqueeze(1).to_broadcast([NH, P, LINE])).then_inc(line_out, 16)
            pool.wait_ge(line_out, 16)

            def strip(h):
                return (bias_rep[bass.ds(h, 1), P - 1:P - 1 + P * (LINE - 1)]
                        .rearrange("a (p c) -> (a p) c", p=P)[:, 0:SEQ])

            used = {}

            def load_state(h, b):
                s, _ = s0_slot(None if h == RH - 1 else h, b)
                if s in used:
                    last, n_out = used[s]
                    pool.wait_ge(s_out[s], 16 * n_out)
                    pool.wait_ge(snq_done, last + 1)
                used[s] = (h * DEC + b, used[s][1] + 1 if s in used else 1)
                pool.dma_start(SB[s][:, :, :], state[b, h]).then_inc(s0_loaded[s], 16)

            def store_state(h, b):
                s, _ = s0_slot(None if h == RH - 1 else h, b)
                pool.wait_ge(sn_ready, h * 16 + 2 * b + 2)
                pool.dma_start(state_s[b, h], SB[s][:, :, :]).then_inc(s_out[s], 16)

            def load_v(h, p):
                if h or p >= 2:
                    pool.wait_ge(kv_ready, 16 * h + 4 * (p - 1))
                pool.dma_start(VBC[:, 2 * (p % 2):2 * (p % 2) + 2, :],
                               bass.AP(tensor=v_rows.tensor, offset=v_rows.offset + 2 * p * DV,
                                       ap=[[0, P], [DV, 2], [1, DV]])).then_inc(vbc_loaded[p % 2], 16)

            for h in range(RH):
                if h >= 1:
                    pool.wait_ge(dec_ready, 4 * h)
                pool.wait_ge(xl_ready, KT * 2)
                pool.dma_start(RT[:, :], ret_tab[h]).then_inc(rt_loaded, 16)
                if h == 0:
                    pool.wait_ge(half_done, 2 * UB["ret_in"])
                    load_state(0, 0)
                    load_state(0, 1)
                for p in range(4 if h >= 1 else 0):
                    for b in (2 * p + 2, 2 * p + 3):
                        load_state(*((h - 1, b) if b < DEC else (h, b - DEC)))
                    for b in (2 * p, 2 * p + 1):
                        store_state(h - 1, b)
                    if p < 2:
                        load_v(h - 1, p + 2)
                pool.wait_ge(v8_ready, h + 1)
                pool.dma_start(v_rows, V8[:, :]).then_inc(v8_out, 16)
                pool.wait_ge(v8_out, h * 16 + 16)
                load_v(h, 0)
                load_v(h, 1)
                pool.wait_ge(spr_ready, h * 2 + 2)
                pool.dma_start(state_p[h], SPR[:, :, :]).then_inc(spr_out, 16)
            for b in (2, 3):
                load_state(RH - 1, b)
            pool.wait_ge(rst_done, 2 * RH)
            for b in range(4, 7):
                load_state(RH - 1, b)
            for b in range(DEC - 1):
                store_state(RH - 1, b)
                if b in (1, 3):
                    load_v(RH - 1, b // 2 + 2)
                if b == 2:
                    load_state(RH - 1, 7)
            store_state(RH - 1, 7)

            pool.wait_ge(half_done, 2 * UB["q"])
            pool.dma_start(OHP[:, :], onehot_past).then_inc(bias_loaded, 16)
            pool.dma_start(RBX[:, :], rel_rows).then_inc(bias_loaded, 16)
            for i in range(4):
                pool.wait_ge(k_ready[0], i + 1)
                pool.wait_ge(k_ready[1], i + 1)
                pool.dma_start(k_t[:, bass.ds(i * 2, 2), :], KTT[:, bass.ds(i * 2, 2), :]).then_inc(k_out, 16)
            def copy_head(h):
                r = h % 2
                if h >= 2:
                    pool.wait_ge(pv_done, h - 1)
                pool.tensor_copy(QHD[r][:, :], QT[:, h, 0:SEQ]).then_inc(head_copied, 1)
                pool.tensor_copy(KHD[r][:, :], KTT[:, h, 0:SEQ]).then_inc(head_copied, 1)
                pool.tensor_copy(VHD[r][:, :, :], VTOK[:, :, h * P:(h + 1) * P]).then_inc(head_copied, 1)

            def next_strip(h):
                pool.wait_ge(ss_ready, 8 * h)
                pool.dma_start(STRIP[:, (h + 1) % 2, :], strip(h + 1)).then_inc(strip_loaded[(h + 1) % 2], 16)

            for h in range(2):
                pool.wait_ge(dvt_ready, 2 * (h + 1))
                copy_head(h)
            pool.wait_ge(dvt_ready, 8 * TB // 2)
            for j in range(TB):
                pool.dma_start(v_p[j], VTOK[:, j, :]).then_inc(v_out, 16)
            pool.wait_ge(v8d_ready, 8)
            pool.dma_start(v_s, V8D[:, :]).then_inc(v_out, 16)
            for r in range(2):
                pool.dma_start(STRIP[:, r, :], strip(r)).then_inc(strip_loaded[r], 16)

            pool.wait_ge(v8d_done, NH)
            pool.wait_ge(v8d_ready, NH)
            pool.wait_ge(vn_ready, NH)
            pool.memset(QP[:, :, :], 0.0).then_inc(slot_step, 1)
            pool.wait_ge(slot_step, 1)
            qp = QP[:, :, :].rearrange("p h c -> p (h c)")
            for b in range(DEC):
                if b >= 1:
                    pool.wait_ge(page_used[3], 2 * b)
                    pool.memset(QP[:, :, 2 * NH * (b - 1):2 * NH * b], 0.0).then_inc(qp_ready, 1)
                for m in range(2):
                    c = 2 * NH * b + m
                    if b or m:
                        pool.wait_ge(qp_ready, 3 * b + m)
                    pool.tensor_copy(qp[m * DH:(m + 1) * DH, c:c + (NH - 1) * (P + 2) + 1:P + 2],
                                     QT[m * DH:(m + 1) * DH, :, SEQ + b]).then_inc(qp_ready, 1)
                pool.wait_ge(qp_ready, 3 * b + 2)
                if b % 2 == 1:
                    next_strip(b // 2 + 1)
                elif b >= 2:
                    copy_head(b // 2 + 1)
            pool.wait_ge(page_used[3], 2 * DEC)
            pool.memset(WP[:, :, :, :], 0.0).then_inc(slot_step, 1)
            pool.wait_ge(slot_step, 2)
            pool.wait_ge(wd_ready, 1)
            for b in range(DEC):
                if b >= 2:
                    pool.wait_ge(page_used[3], 2 * DEC + 2 * (b - 1))
                    pool.memset(WP[:, b % 2, :, NH * (b - 2):NH * (b - 1)], 0.0).then_inc(wp_ready, 1)
                pool.tensor_copy(WP[:, b % 2, :, NH * b:NH * (b + 1)], WD[:, :, NH * b:NH * (b + 1)]
                                 ).then_inc(wp_ready, 1)
                if b % 2 == 1 and b // 2 + 5 < NH:
                    copy_head(b // 2 + 5)
                elif b in (2, 4):
                    next_strip(b // 2 + 4)
            for d in range(0, KT, 2):
                pool.wait_ge(x_ready, 3 * KT + d + 2)
                pool.dma_start(y_t[:, d:d + 2, :], X[:, d:d + 2, :]).then_inc(y_out, 16)
            for r in range(2):
                pool.wait_ge(strip_loaded[r], 16 * (NH // 2))
            for place in used:
                pool.wait_ge(s_out[place], 16 * used[place][1])
            pool.wait_ge(spr_out, 16 * RH)
            pool.wait_ge(k_out, 16 * 4)
            pool.wait_ge(v_out, 16 * (TB + 1))
            pool.wait_ge(v8_out, 16 * RH)
            pool.wait_ge(y_out, 16 * KT // 2)

        @block.tensor
        def _(pe):
            def unit(u, r, nk, k0, xh, xl, first, last, free, fresh=None):
                pe.wait_ge(lo_ready, u + 2)
                if fresh:
                    for c in range(2):
                        if first and free:
                            pe.wait_ge(free[0][c], free[1])
                    for k in range(nk):
                        pe.wait_ge(fresh[0], fresh[1] + k + 1)
                        for c in range(2):
                            for w, a, n in ((WH, xh, 0), (WH, xl, 1), (WL, xh, 2)):
                                for h in range(2):
                                    mm = pe.matmul(PS[:, 2 * c + h, 0:HALF], w[:, r, k, c * P:c * P + P],
                                                   a[:, k0 + k, h * HALF:(h + 1) * HALF],
                                                   start=(first and k == 0 and n == 0),
                                                   stop=(last and k == nk - 1 and n == 2))
                            if k == nk - 1:
                                mm.then_inc(half_done, 1)
                    return
                for c in range(2):
                    if first and free:
                        pe.wait_ge(free[0][c], free[1])
                    for k in range(nk):
                        for w, a, n in ((WH, xh, 0), (WH, xl, 1), (WL, xh, 2)):
                            for h in range(2):
                                mm = pe.matmul(PS[:, 2 * c + h, 0:HALF], w[:, r, k, c * P:c * P + P],
                                               a[:, k0 + k, h * HALF:(h + 1) * HALF],
                                               start=(first and k == 0 and n == 0),
                                               stop=(last and k == nk - 1 and n == 2))
                    mm.then_inc(half_done, 1)

            def plain(stage, n, ready, base):
                for j in range(n):
                    unit(UB[stage] + j, j % 2, UK, 0, XH, XL, True, True, (ready, base + j) if base + j else None,
                         (xl_ready, KT * 4) if stage == "q" and j == 0 else None)

            def bias_line():
                pe.wait_ge(const_loaded, 16 * 11)
                pe.wait_ge(ones_ready, 3)
                for h in range(2):
                    mm = pe.matmul(PS[0:NH, 4 + h, 0:LINE // 2], RB[:, :], OHL[:, h * (LINE // 2):(h + 1) * (LINE // 2)],
                                   start=True, stop=True)
                mm.then_inc(line_mm, 1)

            def ffn(n, ln):
                def pair(i, fresh):
                    unit(i * 2 + UB[f"in{n}"], 0, UK, 0, XH, XL, True, True,
                         (h_ready, i + 11 * n) if n or not fresh else None, fresh)
                    unit(i * 2 + (UB[f"in{n}"] + 1), 1, UK, 0, XH, XL, True, True, (gate_ready, i + (11 * n + 1)))

                pair(0, (xl_ready, KT * ln))
                if n == 0:
                    bias_line()
                with pe.Fori(1, 11) as i:
                    pair(i, None)

                def outs(i, fresh):
                    for j in range(6):
                        k0 = UK * (j % 3)
                        unit(i * 6 + (UB[f"out{n}"] + j), j % 2, min(UK, FT - k0), k0, HH, HL, j % 3 == 0,
                             j % 3 == 2, (h_ready, 11 * (n + 1)) if fresh and j == 0 else
                             (res_done, i * 2 + (4 * ln + j // 3)),
                             (hl_ready, FT * n + k0) if fresh and j < 3 else None)

                outs(0, True)
                outs(1, False)

            def layer_norm(n):
                pe.wait_ge(acc_ready, KT * (n + 1))
                for h in range(2):
                    mm = pe.matmul(PS[:, 4 + h, 0:HALF], ONES[:, :], ACC[:, h * HALF:(h + 1) * HALF],
                                   start=True, stop=True)
                mm.then_inc(mean_ready, 1)
                for d in range(KT):
                    pe.wait_ge(sq_ready, KT * n + d + 1)
                    for h in range(2):
                        mm = pe.matmul(PS[:, 6 + h, 0:HALF], ONES[:, :], SQ[:, d % 2, h * HALF:(h + 1) * HALF],
                                       start=(d == 0), stop=(d == KT - 1))
                    mm.then_inc(sqm_done, 1)

            ffn(0, 0)
            layer_norm(0)

            def states_by_q(h, last, seqs):
                for b in seqs:
                    place, _ = s0_slot(None if last else 0, b)
                    if b == 0:
                        pe.wait_ge(spr_ready, h * 2 + 2)
                        pe.wait_ge(dec_ready, h * 4 + 4)
                    pe.wait_ge(sn_ready, h * 16 + (2 * b + 2))
                    for t in range(2):
                        mm = pe.matmul(PS[0:DEC, 6, :], QD[:, t, b * DEC:(b + 1) * DEC], SB[place][:, t, :],
                                       start=(b == 0 and t == 0), stop=(b == DEC - 1 and t == 1))
                    mm.then_inc(snq_done, 1)

            def new_turned(h):
                pe.wait_ge(dn_ready, h + 1)
                for e in range(4):
                    mm = pe.matmul(PS[:, 4, e * DEC:(e + 1) * DEC], ODEC[:, e * P:(e + 1) * P], IDN[0:DEC, 0:DEC],
                                   start=True, stop=True)
                mm.then_inc(dt_done, 1)

            def ret_head(h, first):
                def head_unit(j):
                    free = ((g_ready, 0), (rope_in, 1), (rope_in, 2), (v_ready, 1), (v_ready, 2), (g_ready, 1))[j]
                    fresh = first and j == 0
                    unit(h * 6 + (UB["ret_in"] + j), j % 2, UK, 0, XH, XL, True, True,
                         None if fresh else (free[0], h * 2 + free[1]), (xl_ready, KT) if fresh else None)

                for j in range(4):
                    head_unit(j)
                    if j and not first:
                        states_by_q(h - 1, False, (2 * j - 2, 2 * j - 1))
                pe.wait_ge(rope_step, h * 12 + 12)
                if not first:
                    pe.wait_ge(rn_rs, h)
                    pe.wait_ge(rn_cent, h * 4)
                    pe.wait_ge(dec_ready, h * 4)
                for t in range(2):
                    for jb in range(TB):
                        mm = pe.transpose(PS[:, 4 + t, jb * P:(jb + 1) * P], RK[:, t, jb * P:(jb + 1) * P], IDN[:, :])
                    mm.then_inc(ktr_done, 1)
                head_unit(4)
                pe.wait_ge(ktk_ready, h * 2 + 2)
                if not first:
                    states_by_q(h - 1, False, (6, 7))
                pe.wait_ge(v_ready[0], h * 2 + 2)
                pe.wait_ge(v_ready[1], h * 2 + 2)
                for e in range(4):
                    mm = pe.transpose(PS[0:DEC, 4, e * P:(e + 1) * P], VT[:, e, SEQ:T], IDN[:, :])
                mm.then_inc(v8_mm, 1)
                for jb in range(TB):
                    if jb >= 2:
                        pe.wait_ge(vtk_ready, h * 4 + jb - 1)
                    for e in range(4):
                        mm = pe.transpose(PS[:, (7, 5)[jb % 2], e * P:(e + 1) * P], VT[:, e, jb * P:(jb + 1) * P], IDN[:, :])
                    mm.then_inc(vtr_done, 1)
                for jb in range(TB):
                    if jb == 0:
                        pe.wait_ge(v8_ready, h + 1)
                    elif jb == 1:
                        pe.wait_ge(vtk_ready, h * 4 + 4)
                    elif jb == 2 and not first:
                        pe.wait_ge(dn_step, h * 3)
                    for t in range(2):
                        mm = pe.matmul(PS[:, 4 + jb, 0:SEQ - P * jb], RK[:, t, jb * P:(jb + 1) * P],
                                       RQ[:, t, jb * P:SEQ], start=(t == 0), stop=(t == 1))
                    mm.then_inc(rsc_done, 1)
                head_unit(5)
                pe.wait_ge(pt_ready, h * 4 + 4)
                for e in range(4):
                    for jb in range(TB):
                        mm = pe.matmul(PS[:, (6, 7, 4, 5)[e], jb * P:SEQ], VTK[:, jb, e * P:(e + 1) * P],
                                       PT[:, strip_at(jb):strip_at(jb + 1)], start=(jb == 0), stop=(jb == TB - 1))
                    mm.then_inc(ro_done, 1)
                for t in range(2):
                    pe.wait_ge(ro_ready, h * 4 + t + 1)
                    for jb in range(TB):
                        mm = pe.matmul(PS[:, 6 + t, :], KTK[:, jb, t * P:(t + 1) * P], VTK[:, jb, :],
                                       start=(jb == 0), stop=(jb == TB - 1))
                    mm.then_inc(rst_done, 1)
                pe.wait_ge(rn_sum, h * 3 + 3)
                pe.wait_ge(ro_ready, h * 4 + 4)
                pe.matmul(PS[:, 4, :], ONES[:, :], RA[:, 1, 0:SEQ], start=True, stop=True).then_inc(rn_mean, 1)
                for e in range(4):
                    pe.wait_ge(rn_sq, h * 4 + e + 1)
                    pe.matmul(PS[:, 5, :], ONES[:, :], RX[:, e % 2, 0:SEQ], start=(e == 0), stop=(e == 3)
                              ).then_inc(rn_sqm, 1)
                if not first:
                    new_turned(h - 1)

            ret_head(0, True)
            with pe.Fori(1, RH) as h:
                ret_head(h, False)
            states_by_q(RH - 1, True, range(DEC))
            new_turned(RH - 1)
            for i in range(4):
                for r in range(2):
                    unit(i * 2 + (UB["ret_out"] + r), r, UK, UK * r, HH, HL, r == 0, r == 1,
                         (res_done, i + 4) if i else (g_ready, 2 * RH),
                         (og_lo, UK * r) if i == 0 else None)
            layer_norm(1)
            ffn(1, 2)
            layer_norm(2)
            ffn(2, 3)
            layer_norm(3)

            plain("q", 4, q_ready, 0)
            for c in range(2):
                pe.wait_ge(q_ready[c], 4)
            plain("kv", 4, k_ready, 0)
            for c in range(2):
                pe.wait_ge(k_ready[c], 4)
            for i in range(2):
                for r in range(2):
                    unit(i * 2 + (UB["kv"] + 4 + r), r, UK, 0, XH, XL, True, True,
                         (vs_ready, i * 2 + r) if i + r else None)
                    for c in range(2):
                        pe.wait_ge(vs_ready[c], i * 2 + (r + 1))
                        if i + r + c:
                            pe.wait_ge(dvt_ready, i * 8 + 4 * r + 2 * c)
                        for jb in range(TB):
                            mm = pe.transpose(PS[:, 4 + jb // 2, (jb % 2) * P:(jb % 2 + 1) * P],
                                              VS[:, c, jb * P:(jb + 1) * P], IDN[:, :])
                            if jb % 2:
                                mm.then_inc(dvt_done, 1)
                        if i + r + c:
                            pe.wait_ge(v8d_ready, i * 4 + 2 * r + c)
                        pe.transpose(PS[0:DEC, 6, 0:P], VS[:, c, SEQ:T], IDN[:, :]).then_inc(v8d_done, 1)
            pe.wait_ge(v8d_ready, 8)

            def scores(i, part, n):
                r, qb = n // TB, n % TB
                kw = (qb + 1) * P
                if qb == 0:
                    pe.wait_ge(head_copied, i * 6 + (12 * part + 3 * r + 3))
                if n >= 2:
                    pe.wait_ge(ss_ready, i * 16 + (32 * part + 2 * (n - 1)))
                for m in range(2):
                    mm = pe.matmul(PS[:, (4, 2)[n % 2] + m, 0:kw], QHD[r][m * DH:(m + 1) * DH, qb * P:(qb + 1) * P],
                                   KHD[r][m * DH:(m + 1) * DH, 0:kw], start=True, stop=True)
                mm.then_inc(sc_done, 1)

            def k_pages(i, r, a, pages):
                if 0 in pages:
                    pe.wait_ge(qp_ready, i * 12 + 3 * (2 * r + a) + 2)
                for pg in pages:
                    pe.wait_ge(page_loaded[pg % 4], i * 128 + (64 * r + 32 * a + 16 * (pg // 4) + 16))
                    for hd in range(NH):
                        mm = pe.matmul(PS[:, pg // 4, (pg % 4) * P:(pg % 4 + 1) * P], QP[:, hd, :],
                                       PG[:, pg % 4, hd * P:(hd + 1) * P], start=False, stop=True,
                                       skip_group_check=True)
                    mm.then_inc(page_used[pg % 4], 1)

            def v_pages(i, r, a, pages):
                if 0 in pages:
                    pe.wait_ge(wp_ready, i * 8 + max(1, 2 * (2 * r + a)))
                for pg in pages:
                    pe.wait_ge(page_loaded[pg % 4], i * 128 + (64 * r + 32 * a + 16 * (pg // 4) + 16 + 16 * 16))
                    for g in range(2):
                        mm = pe.matmul(PS[0:PAIRS, g, :], WP[:, a, pg, :], PG[:, pg % 4, g * 512:(g + 1) * 512],
                                       start=False, stop=True, skip_group_check=True)
                    mm.then_inc(page_used[pg % 4], 1)

            def heads(part, pages):
                with pe.Fori(0, NH // 4) as i:
                    scores(i, part, 0)
                    for n in range(2 * TB):
                        r, qb = n // TB, n % TB
                        if n + 1 < 2 * TB:
                            scores(i, part, n + 1)
                        pages(i, r, qb // 2, range(4 * (qb % 2), 4 * (qb % 2) + 4))
                        pe.wait_ge(ww_ready, i * 8 + (16 * part + n + 1))
                        if n:
                            pe.wait_ge(wt_ready, i * 8 + (16 * part + n))
                        for kb in range(qb + 1):
                            mm = pe.transpose(PS[:, 6, kb * P:(kb + 1) * P], SS[n % 2][:, 0, kb * P:(kb + 1) * P],
                                              IDN[:, :])
                        mm.then_inc(wtr_done, 1)
                        if qb == TB - 1:
                            pe.wait_ge(wt_ready, i * 8 + (16 * part + n + 1))
                            for q in range(TB):
                                for kb in range(q + 1):
                                    mm = pe.matmul(PS[:, 7, q * P:(q + 1) * P], VHD[r][:, kb, :],
                                                   WT[:, turned_at(q) + kb * P:turned_at(q) + (kb + 1) * P],
                                                   start=(kb == 0), stop=(kb == q))
                            mm.then_inc(pv_done, 1)

            pe.wait_ge(bias_loaded, 32)
            pe.wait_ge(rbx_ready, 1)
            for g in range(2):
                pe.matmul(PS[:, g, :], RBX[:, :], OHP[:, g * 512:(g + 1) * 512], start=True, stop=True,
                          skip_group_check=True)
            heads(0, k_pages)
            pe.wait_ge(newprod_ready, 3)
            pe.wait_ge(ss_ready, 4 * NH)
            pe.matmul(PS[:, 2, 0:1], PRD[:, :, :].rearrange("p x m -> p (x m)"), ONES[:, 0:1], start=True, stop=False)
            pe.matmul(PS[:, 2, 0:1], RBX[:, :], IDN[0:BUCKETS, 0:1], start=False, stop=True).then_inc(newscore_done, 1)
            pe.wait_ge(comb_ready, 2)
            for pg in range(NPG):
                mm = pe.matmul(PS[:, 4, pg * PAIRS:(pg + 1) * PAIRS], SCA[:, pg * P:(pg + 1) * P], COMB[:, :],
                               start=True, stop=True)
            mm.then_inc(wd_done, 1)
            pe.matmul(PS[:, 3, 0:PAIRS], ONES[:, :], COMB_OWN[:, :], start=True, stop=True).then_inc(wd_done, 1)
            for g in range(2):
                pe.matmul(PS[0:PAIRS, g, :], ROWS[:, PAIRS + 2:2 * PAIRS + 2], SCA[:, g * 512:(g + 1) * 512],
                          start=True, stop=True, skip_group_check=True)
            pe.wait_ge(wd_ready, 2)
            heads(1, v_pages)
            pe.wait_ge(of_ready, NH)
            pe.wait_ge(ov_step, 2)
            pe.transpose(PS[:, 6, 0:PAIRS], OVR[:, :], IDN[0:PAIRS, 0:PAIRS]).then_inc(ov_turned, 1)
            pe.wait_ge(ss_ready, 8 * NH)
            pe.wait_ge(wt_ready, 4 * NH)
            for d in range(NH):
                pe.wait_ge(on_sq, d + 1)
                if d >= 2:
                    pe.wait_ge(on_ln, d - 1)
                for g in range(2):
                    mm = pe.matmul(PS[:, (6, 4)[d % 2] + g, 0:HALF], ONES[:, :], SG[:, d % 2, g * HALF:(g + 1) * HALF],
                                   start=True, stop=True)
                mm.then_inc(on_mm, 1)
            for j in range(4):
                unit(UB["o"] + j, j % 2, UK, 0, HH, HL, True, True, (res_done, 4 * 4 + j), (on_lo, 0) if j == 0 else None)
            layer_norm(4)
            ffn(3, 5)
            layer_norm(5)

        @block.scalar
        def _(act):
            def ahead(half_u, r, first=False):
                act.wait_ge(raw_loaded[r], half_u * 16 + 16)
                if not first:
                    act.wait_ge(half_done, half_u * 4 + (2 * r - 2))
                act.activation(WH[:, r, :, :], WR[:, r, :, :], ACT.Copy).then_inc(hi_ready, 1)

            def ffn(n):
                u0 = UB[f"in{n}"] // 2

                def pair(i):
                    for c in range(2):
                        act.wait_ge(half_done, i * 4 + (4 * u0 + c + 1))
                        if not (isinstance(i, int) and n == 0):
                            act.wait_ge(h_ready[c], i + 11 * n)
                        act.activation(halves(SG[:, c, :]), tile_ps(c), ACT.Silu).then_inc(gate_ready[c], 1)
                    ahead(i + (u0 + 1), 0)
                    for c in range(2):
                        act.wait_ge(h_ready[c], i + (11 * n + 1))
                        act.activation(HH[:, bass.ds(i * 2 + c, 1), :].rearrange("p a c -> p (a c)"),
                                       HF[:, c, :], ACT.Copy).then_inc(hh_ready, 1)
                    ahead(i + (u0 + 1), 1)

                pair(0)
                if n == 0:
                    act.wait_ge(lam_step, 2)
                    act.activation(EXPD, DOT, ACT.Exp).then_inc(lam_exp, 1)
                    with act.Fori(1, 7) as i:
                        pair(i)
                    act.wait_ge(line_out, 16)
                else:
                    ln = (None, 1, 2, 4)[n]
                    act.wait_ge(xl_ready, KT * (ln + 2))
                    for d in range(KT):
                        act.activation(X[:, d, :], X[:, d, :], ACT.Identity, bias=LNB[:, ln, d:d + 1]
                                       ).then_inc(x_ready, 1)
                with act.Fori(1 if n else 7, 11) as i:
                    pair(i)
                u0 = UB[f"out{n}"] // 2
                if n < 3:
                    with act.Fori(0, 2) as i:
                        for j in range(6):
                            ahead(i * 3 + (u0 + j // 2 + 1), j % 2)
                else:
                    for j in range(10):
                        ahead(u0 + j // 2 + 1, j % 2)

            def layer_norm(n):
                for d in range(KT):
                    act.wait_ge(cent_ready, KT * n + d + 1)
                    if d >= 2:
                        act.wait_ge(sqm_done, KT * n + d - 1)
                    act.activation(SQ[:, d % 2, :], X[:, d, :], ACT.Square).then_inc(sq_ready, 1)
                act.wait_ge(sqm_done, KT * (n + 1))
                act.activation(halves(RS[:, :]), PS[:, 6:8, 0:HALF], ACT.Ln, bias=EPS_LN, scale=1.0 / D).then_inc(ln_step, 1)
                act.wait_ge(ln_step, n + 1)
                act.activation(RS[:, :], RS[:, :], ACT.Exp, scale=-0.5).then_inc(rs_ready, 1)
                for d in range(KT):
                    act.wait_ge(scaled, KT * n + d + 1)
                    if n < 5:
                        act.activation(XH[:, d, :], X[:, d, :], ACT.Identity, bias=LNB[:, n, d:d + 1]
                                       ).then_inc(xh_ready, 1)
                    else:
                        act.activation(X[:, d, :], X[:, d, :], ACT.Identity, bias=LNB[:, n, d:d + 1]
                                       ).then_inc(x_ready, 1)

            ahead(0, 0, True)
            for d in range(KT):
                act.wait_ge(x_loaded[d // 2], 16)
                act.activation(XH[:, d, :], X[:, d, :], ACT.Copy).then_inc(xh_ready, 1)
            ahead(0, 1, True)
            ffn(0)
            layer_norm(0)

            ub = UB["ret_in"] // 2

            def k_by_v(h, seqs):
                for b in seqs:
                    if b % 2 == 0:
                        act.wait_ge(vbc_loaded[b // 2 % 2], h * 32 + (16 * (b // 4) + 16))
                    if b == 0:
                        act.wait_ge(dec_ready, h * 4 + 4)
                    for t in range(2):
                        if b >= 1:
                            act.wait_ge(sn_ready, h * 16 + (2 * b + t - 1))
                        act.activation(TMP[:, t, :], VBC[:, b % 4, :], ACT.Copy, scale=KD[:, t, b:b + 1]
                                       ).then_inc(kv_ready, 1)

            def new_norm(h):
                act.wait_ge(dn_step, h * 3 + 3)
                act.activation(ODEC2, ODEC, ACT.Square, accum_out=DST[0:DEC, 2:3]).then_inc(dn_act, 1)
                act.wait_ge(dn_act, h * 3 + 1)
                act.activation(DST[0:DEC, 3:4], DST[0:DEC, 2:3], ACT.Ln, bias=EPS_1[0:DEC], scale=1.0 / DV
                               ).then_inc(dn_act, 1)
                act.wait_ge(dn_act, h * 3 + 2)
                act.activation(DST[0:DEC, 4:5], DST[0:DEC, 3:4], ACT.Exp, scale=-0.5).then_inc(dn_act, 1)

            def ret_head(h, first):
                for j in range(6):
                    for c in range(2):
                        act.wait_ge(half_done, h * 12 + (4 * ub + 2 * j + c + 1))
                        if j < 2:
                            if j or not first:
                                act.wait_ge(rope_step, h * 12 + 6 * j)
                            if not first:
                                act.wait_ge(rn_sqm, h * 4)
                            a = act.activation(halves(RX[:, c, :]), tile_ps(c), ACT.Copy,
                                               scale=1.0 if j == 0 else DK ** -0.5)
                            a.then_inc(rope_in[c], 1)
                        elif j < 4:
                            if not first:
                                act.wait_ge(rn_done, h * 4)
                            a = act.activation(halves(VT[:, 2 * (j - 2) + c, :]), tile_ps(c), ACT.Copy)
                            a.then_inc(v_ready[c], 1)
                        else:
                            a = act.activation(halves(GT[:, 2 * (j - 4) + c, :]), tile_ps(c), ACT.Silu)
                            a.then_inc(g_ready[c], 1)
                    ahead(h * 3 + (ub + j // 2 + 1), j % 2)
                    if j < 4 and not first:
                        k_by_v(h - 1, (2 * j, 2 * j + 1))
                    if j == 3:
                        act.wait_ge(rt_loaded, h * 16 + 16)
                        if not first:
                            act.wait_ge(rst_done, h * 2)
                        for t in range(2):
                            act.wait_ge(ktr_done, h * 2 + t + 1)
                            for jb in range(TB):
                                a = act.activation(KTK[:, jb, t * P:(t + 1) * P], PS[:, 4 + t, jb * P:(jb + 1) * P],
                                                   ACT.Copy, scale=RT[:, SEQ + jb:SEQ + jb + 1])
                            a.then_inc(ktk_ready, 1)
                    if j == 4:
                        act.wait_ge(v8_mm, h + 1)
                        act.activation(V8[:, :], PS[0:DEC, 4, :], ACT.Copy).then_inc(v8_ready, 1)
                        for jb in range(TB):
                            act.wait_ge(vtr_done, h * 4 + jb + 1)
                            act.activation(VTK[:, jb, :], PS[:, (7, 5)[jb % 2], :], ACT.Copy).then_inc(vtk_ready, 1)
                        if not first:
                            new_norm(h - 1)
                for e in range(4):
                    act.wait_ge(ro_done, h * 4 + e + 1)
                    act.activation(RO[:, e, 0:SEQ], PS[:, (6, 7, 4, 5)[e], :], ACT.Copy).then_inc(ro_ready, 1)
                if not first:
                    act.wait_ge(spr_out, h * 16)
                for t in range(2):
                    act.wait_ge(rst_done, h * 2 + t + 1)
                    act.activation(SPR[:, t, :], PS[:, 6 + t, :], ACT.Copy).then_inc(spr_ready, 1)
                for e in range(4):
                    act.wait_ge(rn_cent, h * 4 + e + 1)
                    act.wait_ge(rope_step, h * 12 + 12)
                    if e >= 2:
                        act.wait_ge(rn_sqm, h * 4 + e - 1)
                    act.activation(RX[:, e % 2, 0:SEQ], RO[:, e, 0:SEQ], ACT.Square).then_inc(rn_sq, 1)
                act.wait_ge(rn_sqm, h * 4 + 4)
                act.activation(RA[:, 0, 0:SEQ], PS[:, 5, :], ACT.Ln, bias=EPS_1, scale=1.0 / DV).then_inc(rn_step, 1)
                act.wait_ge(rn_step, h + 1)
                act.activation(RA[:, 0, 0:SEQ], RA[:, 0, 0:SEQ], ACT.Exp, scale=-0.5).then_inc(rn_rs, 1)

            ret_head(0, True)
            with act.Fori(1, RH) as h:
                ret_head(h, False)
            k_by_v(RH - 1, range(DEC))
            new_norm(RH - 1)
            act.wait_ge(rn_done, 4 * RH)
            act.wait_ge(dp_ready, RH)
            act.wait_ge(kv_ready, 16 * RH)
            for place in (2, 3):
                act.wait_ge(s_out[place], 16 * (2 * RH - 1))
            for d in range(4 * RH):
                act.activation(HH[:, d, :], OG[:, d, :], ACT.Copy).then_inc(og_hi, 1)
            u0 = UB["ret_out"] // 2
            with act.Fori(0, 4) as i:
                for r in range(2):
                    ahead(i + (u0 + 1), r)
            layer_norm(1)
            ffn(1)
            layer_norm(2)
            ffn(2)
            layer_norm(3)

            uq, uk = UB["q"] // 2, UB["kv"] // 2
            with act.Fori(0, 2) as i:
                for r in range(2):
                    for c in range(2):
                        act.wait_ge(half_done, i * 4 + (4 * uq + 2 * r + c + 1))
                        a = act.activation(QT[:, bass.ds(i * 4 + (2 * r + c), 1), :].rearrange("p a (h c) -> p (a h) c", h=2),
                                           tile_ps(c), ACT.Copy)
                        a.then_inc(q_ready[c], 1)
                    ahead(i + (uq + 1), r)
            with act.Fori(0, 2) as i:
                for r in range(2):
                    for c in range(2):
                        act.wait_ge(half_done, i * 4 + (4 * uk + 2 * r + c + 1))
                        a = act.activation(KTT[:, bass.ds(i * 4 + (2 * r + c), 1), :].rearrange("p a (h c) -> p (a h) c", h=2),
                                           tile_ps(c), ACT.Copy)
                        a.then_inc(k_ready[c], 1)
                    ahead(i + (uk + 1), r)
            for i in range(2):
                for r in range(2):
                    for c in range(2):
                        act.wait_ge(half_done, i * 4 + (4 * uk + 8 + 2 * r + c + 1))
                        kept = i * 4 if r == 0 else i * 4 + (c + 1)
                        if kept:
                            act.wait_ge(v8d_done, kept)
                            act.wait_ge(vn_ready, kept)
                        a = act.activation(halves(VS[:, c, :]), tile_ps(c), ACT.Copy)
                        a.then_inc(vs_ready[c], 1)
                    ahead(i + (uk + 3), r)
            def exps(i, part, n):
                kw = (n % TB + 1) * P
                o = 8 * (n % 2)
                act.wait_ge(mx_ready, i * 8 + (16 * part + n + 1))
                for m in range(2):
                    act.activation(SS[n % 2][:, m, 0:kw], SS[n % 2][:, m, 0:kw], ACT.Exp, bias=ST[:, o + m:o + m + 1],
                                   accum_out=ST[:, o + 2 + m:o + 3 + m]).then_inc(ex_ready, 1)

            def heads(part):
                with act.Fori(0, NH // 4) as i:
                    exps(i, part, 0)
                    for n in range(2 * TB):
                        r, qb = n // TB, n % TB
                        if n + 1 < 2 * TB:
                            exps(i, part, n + 1)
                        act.wait_ge(wtr_done, i * 8 + (16 * part + n + 1))
                        act.activation(WT[:, turned_at(qb):turned_at(qb + 1)], PS[:, 6, 0:(qb + 1) * P], ACT.Copy
                                       ).then_inc(wt_ready, 1)
                        if qb == TB - 1:
                            act.wait_ge(pv_done, i * 2 + (4 * part + r + 1))
                            act.activation(OF[:, bass.ds(i * 2 + (4 * part + r), 1), 0:SEQ]
                                           .rearrange("p a c -> p (a c)"), PS[:, 7, :], ACT.Copy).then_inc(of_ready, 1)

            heads(0)
            act.wait_ge(shift_ready, 1)
            act.activation(SCA[:, :], PS[:, 0:2, :].rearrange("p g c -> p (g c)"), ACT.Exp, bias=SHIFT, scale=DH ** -0.5,
                           accum_out=SUM).then_inc(dec_exp, 1)
            act.activation(OWN_EXP, PS[:, 2, 0:1], ACT.Exp, bias=SHIFT, scale=DH ** -0.5).then_inc(dec_exp, 1)
            heads(1)
            for d in range(NH):
                act.wait_ge(on_mm, d + 1)
                act.activation(halves(RSN[:, d, :]), PS[:, (6, 4)[d % 2]:(6, 4)[d % 2] + 2, 0:HALF], ACT.Ln, bias=EPS_1,
                               scale=1.0 / (2 * DH)).then_inc(on_ln, 1)
            for d in range(NH + 1):
                if d < NH:
                    act.wait_ge(on_ln, d + 1)
                    act.activation(RSN[:, d, :], RSN[:, d, :], ACT.Exp, scale=-0.5).then_inc(on_rs, 1)
                if d >= 1:
                    act.wait_ge(on_mul, d)
                    act.activation(HH[:, d - 1, :], OF[:, d - 1, :], ACT.Copy).then_inc(on_hi, 1)
            u0 = UB["o"] // 2
            with act.Fori(0, 2) as i:
                for r in range(2):
                    ahead(i + (u0 + 1), r)
            layer_norm(4)
            ffn(3)
            layer_norm(5)

        @block.vector
        def _(dve):
            def ahead(half_u, r):
                dve.wait_ge(hi_ready, half_u * 2 + r + 1)
                dve.wait_ge(raw_loaded[r], half_u * 16 + 16)
                dve.tensor_tensor(WL[:, r, :, :], WR[:, r, :, :], WH[:, r, :, :].bitcast(F32), ALU.subtract
                                  ).then_inc(lo_ready, 1)

            def residual(d, pair, c, half, ln, scale, parts=False):
                x = X[:, bass.ds(d, 1), :].rearrange("p a (h c) -> p (a h) c", h=2)
                xf = X[:, bass.ds(d, 1), :].rearrange("p a c -> p (a c)")
                dve.wait_ge(half_done, half)
                if not parts:
                    dve.scalar_tensor_tensor(x, tile_ps(c), scale, x, ALU.mult, ALU.add).then_inc(res_done[c], 1)
                    dve.wait_ge(res_done[c], pair + (4 * ln + 1))
                else:
                    hi = XH[:, bass.ds(d, 1), :].bitcast(F32).rearrange("p a (h c) -> p (a h) c", h=2)
                    lo = XL[:, bass.ds(d, 1), :].bitcast(F32).rearrange("p a c -> p (a c)")
                    dve.scalar_tensor_tensor(x, tile_ps(c), scale, hi, ALU.mult, ALU.add).then_inc(res_done[c], 1)
                    dve.wait_ge(res_done[c], pair + (4 * ln + 1))
                    dve.tensor_tensor(xf, xf, lo, ALU.add).then_inc(y_ready, 1)
                    dve.wait_ge(y_ready, d + (KT * (ln // 4) + 1))
                if not (isinstance(d, int) and d + ln == 0):
                    dve.wait_ge(acc_ready, d + KT * ln)
                dve.tensor_tensor(ACC[:, :], ACC[:, :], xf, ALU.add).then_inc(acc_ready, 1)

            def clear_acc(ln):
                dve.memset(ACC[:, :], 0.0).then_inc(acc_zero, 1)
                dve.wait_ge(acc_zero, ln + 1)

            def layer_norm(n):
                dve.wait_ge(mean_ready, n + 1)
                for d in range(KT):
                    x = halves(X[:, d, :])
                    dve.scalar_tensor_tensor(x, PS[:, 4:6, 0:HALF], -1.0 / D, x, ALU.mult, ALU.add
                                             ).then_inc(cent_ready, 1)
                dve.wait_ge(rs_ready, n + 1)
                dve.wait_ge(cent_ready, KT * (n + 1))
                for d in range(KT + 1):
                    if d < KT:
                        dve.scalar_tensor_tensor(X[:, d, :], X[:, d, :], LNG[:, n, d:d + 1], RS[:, :],
                                                 ALU.mult, ALU.mult).then_inc(scaled, 1)
                    if d >= 1 and n < 5:
                        dve.wait_ge(xh_ready, KT * (n + 1) + d)
                        dve.scalar_tensor_tensor(XL[:, d - 1, :], X[:, d - 1, :], LNB[:, n, d - 1:d],
                                                 XH[:, d - 1, :].bitcast(F32), ALU.add, ALU.subtract
                                                 ).then_inc(xl_ready, 1)

            def start():
                dve.wait_ge(const_loaded, 16 * 11)
                dve.tensor_tensor(LPR[:, :, :], LV[:, 0:4:2, :], LV[:, 1:4:2, :], ALU.mult).then_inc(lam_step, 1)
                dve.wait_ge(lam_step, 1)
                dve.tensor_reduce(DOT, LPR[:, :, :], AX.X, ALU.add).then_inc(lam_step, 1)
                dve.wait_ge(lam_exp, 1)
                dve.tensor_tensor(NLAM, EXPD[:, 1:2], EXPD[:, 0:1], ALU.subtract).then_inc(lam_step, 1)
                dve.wait_ge(lam_step, 3)
                dve.tensor_scalar(NLAM, NLAM, -LAMBDA_INIT, None, ALU.add).then_inc(lam_step, 1)
                dve.tensor_scalar(SUBG, SUBG, 1.0 - LAMBDA_INIT, None, ALU.mult).then_inc(lam_step, 1)
                dve.wait_ge(line_mm, 1)
                dve.tensor_tensor(LN8[:, :].rearrange("p (h c) -> p h c", h=2), PS[0:NH, 4:6, 0:LINE // 2],
                                  LMASK[:, :].rearrange("p (h c) -> p h c", h=2), ALU.add).then_inc(line_sb, 1)
                dve.wait_ge(lam_step, 4)
                dve.scalar_tensor_tensor(SIGN, ROWS[:, PAIRS + 1:PAIRS + 2], NLAM, ROWS[:, PAIRS:PAIRS + 1],
                                         ALU.mult, ALU.add).then_inc(lam_step, 1)

            def ffn(n):
                u0 = UB[f"in{n}"] // 2

                def pair(i):
                    ahead(i + (u0 + 1), 0)
                    for c in range(2):
                        dve.wait_ge(half_done, i * 4 + (4 * u0 + c + 3))
                        dve.wait_ge(gate_ready[c], i + (11 * n + 1))
                        if not (isinstance(i, int) and n == 0):
                            dve.wait_ge(hl_ready, i * 2 + (FT * n))
                        dve.tensor_tensor(halves(HF[:, c, :]), halves(SG[:, c, :]), tile_ps(c), ALU.mult
                                          ).then_inc(h_ready[c], 1)
                        dve.wait_ge(hh_ready, i * 2 + (FT * n + c + 1))
                        dve.tensor_tensor(HL[:, bass.ds(i * 2 + c, 1), :].rearrange("p a c -> p (a c)"), HF[:, c, :],
                                          HH[:, bass.ds(i * 2 + c, 1), :].rearrange("p a c -> p (a c)").bitcast(F32),
                                          ALU.subtract).then_inc(hl_ready, 1)
                    ahead(i + (u0 + 1), 1)

                pair(0)
                if n == 0:
                    start()
                with dve.Fori(1, 11) as i:
                    pair(i)
                u0 = UB[f"out{n}"] // 2
                ln = (0, 2, 3, 5)[n]
                dve.wait_ge(hl_ready, FT * (n + 1))
                if n:
                    dve.wait_ge(x_ready, KT * n)
                clear_acc(ln)

                def pairs(i):
                    for j in range(6):
                        if j % 3 == 2:
                            for c in range(2):
                                d = 2 * (j // 3) + c
                                residual(i * 4 + d, i * 2 + j // 3, c, i * 12 + (4 * u0 + 2 * j + c + 1), ln, 0.5 / ALPHA)
                        if n < 3 or 6 * i + j < 10:
                            ahead(i * 3 + (u0 + j // 2 + 1), j % 2)

                for i in range(2):
                    pairs(i)

            dve.memset(ACC[:, :], 0.0).then_inc(lo_ready, 1)
            ahead(0, 0)
            for d in range(KT):
                dve.wait_ge(x_loaded[d // 2], 16)
                dve.wait_ge(xh_ready, d + 1)
                dve.tensor_tensor(XL[:, d, :], X[:, d, :], XH[:, d, :].bitcast(F32), ALU.subtract).then_inc(xl_ready, 1)
            ahead(0, 1)
            ffn(0)
            layer_norm(0)

            ub = UB["ret_in"] // 2
            dve.wait_ge(xl_ready, KT * 2)
            dve.memset(QD[:, :, :], 0.0).then_inc(qd_zero, 1)

            def new_states(h, last, seqs):
                for b in seqs:
                    place, nth = s0_slot(None if last else h, b)
                    dve.wait_ge(s0_loaded[place], nth * 16)
                    for t in range(2):
                        dve.wait_ge(kv_ready, h * 16 + (2 * b + t + 1))
                        dve.scalar_tensor_tensor(SB[place][:, t, :], SB[place][:, t, :], DST[:, 5:6], TMP[:, t, :],
                                                 ALU.mult, ALU.add).then_inc(sn_ready, 1)

            def new_centred(h):
                dve.wait_ge(snq_done, h * 8 + 8)
                dve.tensor_reduce(DST[0:DEC, 0:1], PS[0:DEC, 6, :], AX.X, ALU.add).then_inc(dn_step, 1)
                dve.wait_ge(dn_step, h * 3 + 1)
                dve.tensor_scalar(DST[0:DEC, 1:2], DST[0:DEC, 0:1], -1.0 / DV, None, ALU.mult).then_inc(dn_step, 1)
                dve.wait_ge(dn_step, h * 3 + 2)
                dve.tensor_scalar(ODEC, PS[0:DEC, 6, :], DST[0:DEC, 1:2], None, ALU.add).then_inc(dn_step, 1)

            def new_normed(h):
                dve.wait_ge(dn_act, h * 3 + 3)
                dve.wait_ge(dn_step, h * 3 + 3)
                dve.tensor_scalar(ODEC, ODEC, DST[0:DEC, 4:5], None, ALU.mult).then_inc(dn_ready, 1)

            def new_gated(h):
                dve.wait_ge(dt_done, h + 1)
                dve.tensor_tensor(OG[:, bass.ds(h * 4, 4), SEQ:T], PS[:, 4, 0:4 * DEC].rearrange("p (e b) -> p e b", e=4),
                                  GD[:, :, :], ALU.mult).then_inc(dp_ready, 1)

            def ret_head(h, first):
                for j in range(6):
                    if j < 2:
                        out = (RQ, RK)[j]
                        dve.wait_ge(rope_in[0], h * 2 + (j + 1))
                        dve.wait_ge(rope_in[1], h * 2 + (j + 1))
                        if not first:
                            dve.wait_ge(rn_done, h * 4)
                            dve.wait_ge(dec_ready, h * 4)
                        steps = ((RA[:, 0, :], RX[:, 0, :], COS[:, :], ALU.mult),
                                 (RA[:, 1, :], RX[:, 1, :], SIN[:, :], ALU.mult),
                                 (out[:, 0, :], RA[:, 0, :], RA[:, 1, :], ALU.subtract),
                                 (RA[:, 0, :], RX[:, 0, :], SIN[:, :], ALU.mult),
                                 (RA[:, 1, :], RX[:, 1, :], COS[:, :], ALU.mult),
                                 (out[:, 1, :], RA[:, 0, :], RA[:, 1, :], ALU.add))
                        for n, (dst, a, b, op) in enumerate(steps):
                            if not first or 6 * j + n:
                                dve.wait_ge(rope_step, h * 12 + (6 * j + n))
                            dve.tensor_tensor(dst, a, b, op).then_inc(rope_step, 1)
                    if j < 5:
                        ahead(h * 3 + (ub + j // 2 + 1), j % 2)
                    if j < 4 and not first:
                        new_states(h - 1, False, (2 * j, 2 * j + 1))
                    if j == 4:
                        if not first:
                            new_centred(h - 1)
                        dve.wait_ge(rt_loaded, h * 16 + 16)
                        for jb in range(TB):
                            dve.wait_ge(rsc_done, h * 4 + jb + 1)
                            dve.tensor_tensor(PT[:, strip_at(jb):strip_at(jb + 1)], PS[:, 4 + jb, 0:SEQ - P * jb],
                                              RT[:, 0:SEQ - P * jb], ALU.mult).then_inc(pt_ready, 1)
                ahead(h * 3 + (ub + 3), 1)
                if not first:
                    new_normed(h - 1)
                dve.wait_ge(rope_step, h * 12 + 12)
                for e in range(1, 4):
                    dve.wait_ge(ro_ready, h * 4 + e + 1)
                    if e > 1:
                        dve.wait_ge(rn_sum, h * 3 + e - 1)
                    dve.tensor_tensor(RA[:, 1, 0:SEQ], RO[:, 0, 0:SEQ] if e == 1 else RA[:, 1, 0:SEQ], RO[:, e, 0:SEQ],
                                      ALU.add).then_inc(rn_sum, 1)
                dve.wait_ge(rn_mean, h + 1)
                for e in range(4):
                    dve.scalar_tensor_tensor(RO[:, e, 0:SEQ], PS[:, 4, :], -1.0 / DV, RO[:, e, 0:SEQ], ALU.mult, ALU.add
                                             ).then_inc(rn_cent, 1)
                dve.wait_ge(rn_rs, h + 1)
                dve.wait_ge(rn_cent, h * 4 + 4)
                dve.wait_ge(g_ready[0], h * 2 + 2)
                dve.wait_ge(g_ready[1], h * 2 + 2)
                for e in range(4):
                    dve.tensor_tensor(RO[:, e, 0:SEQ], RO[:, e, 0:SEQ], RA[:, 0, 0:SEQ], ALU.mult).then_inc(rn_mul, 1)
                for e in range(4):
                    dve.wait_ge(rn_mul, h * 4 + e + 1)
                    dve.tensor_tensor(OG[:, bass.ds(h * 4 + e, 1), 0:SEQ].rearrange("p a c -> p (a c)"),
                                      RO[:, e, 0:SEQ], GT[:, e, 0:SEQ], ALU.mult).then_inc(rn_done, 1)
                if not first:
                    new_gated(h - 1)
                dve.wait_ge(g_ready[0], h * 2 + 2)
                dve.wait_ge(g_ready[1], h * 2 + 2)
                dve.wait_ge(rope_step, h * 12 + 12)
                if first:
                    dve.wait_ge(qd_zero, 1)
                else:
                    dve.wait_ge(sn_ready, h * 16)
                    dve.wait_ge(snq_done, h * 8)
                    dve.wait_ge(dp_ready, h)
                for dst, src in ((QD[:, :, 0:DEC * DEC:DEC + 1], RQ[:, :, SEQ:T]), (KD[:, :, :], RK[:, :, SEQ:T]),
                                 (GD[:, :, :], GT[:, :, SEQ:T]), (DST[:, 5:6], RT[:, SEQ + 4:SEQ + 5])):
                    dve.tensor_copy(dst, src).then_inc(dec_ready, 1)

            ret_head(0, True)
            with dve.Fori(1, RH) as h:
                ret_head(h, False)
            new_states(RH - 1, True, range(DEC))
            new_centred(RH - 1)
            new_normed(RH - 1)
            new_gated(RH - 1)
            for d in range(4 * RH):
                dve.wait_ge(og_hi, d + 1)
                dve.tensor_tensor(HL[:, d, :], OG[:, d, :], HH[:, d, :].bitcast(F32), ALU.subtract
                                  ).then_inc(og_lo, 1)
            clear_acc(1)
            u0 = UB["ret_out"] // 2
            with dve.Fori(0, 4) as i:
                ahead(i + (u0 + 1), 0)
                for c in range(2):
                    residual(i * 2 + c, i, c, i * 4 + (4 * u0 + 2 + c + 1), 1, 1.0 / ALPHA, True)
                ahead(i + (u0 + 1), 1)
            layer_norm(1)
            for b in range(DEC):
                place, nth = s0_slot(None, b)
                dve.wait_ge(s_out[place], 16 * nth)
            dve.wait_ge(spr_out, 16 * RH)
            ffn(1)
            layer_norm(2)
            ffn(2)
            layer_norm(3)

            uq, uk = UB["q"] // 2, UB["kv"] // 2
            with dve.Fori(0, 2) as i:
                for r in range(2):
                    ahead(i + (uq + 1), r)
            with dve.Fori(0, 2) as i:
                for r in range(2):
                    ahead(i + (uk + 1), r)
            dve.wait_ge(bias_loaded, 32)
            dve.tensor_scalar(RBX[:, :], RBX[:, :], DH ** 0.5, None, ALU.mult).then_inc(rbx_ready, 1)
            dve.memset(PRD[:, :, :], 0.0).then_inc(newprod_ready, 1)
            dve.wait_ge(newprod_ready, 1)
            dve.wait_ge(q_ready[0], NH // 2)
            dve.wait_ge(q_ready[1], NH // 2)
            dve.wait_ge(k_ready[0], NH // 2)
            dve.wait_ge(k_ready[1], NH // 2)
            for m in range(2):
                rows = slice(m * DH, (m + 1) * DH)
                dve.tensor_tensor(PRD[rows, :, m].rearrange("p (b h) -> p b h", b=DEC),
                                  QT[rows, :, SEQ:T].rearrange("p h b -> p b h"),
                                  KTT[rows, :, SEQ:T].rearrange("p h b -> p b h"), ALU.mult).then_inc(newprod_ready, 1)
            with dve.Fori(0, 2) as i:
                for r in range(2):
                    for c in range(2):
                        n = 2 * r + c
                        dve.wait_ge(vs_ready[c], i * 2 + (r + 1))
                        dve.tensor_copy(VN[:, bass.ds(i * 4 + n, 1), :].rearrange("p a c -> p (a c)"),
                                        VS[:, c, SEQ:T]).then_inc(vn_ready, 1)
                        for g in range(2):
                            dve.wait_ge(dvt_done, i * 8 + (2 * n + g + 1))
                            dve.tensor_copy(VTOK[:, 2 * g:2 * g + 2, bass.ds(i * 512 + n * P, P)],
                                            PS[:, 4 + g, 0:2 * P].rearrange("p (j e) -> p j e", j=2)
                                            ).then_inc(dvt_ready, 1)
                        dve.wait_ge(v8d_done, i * 4 + (n + 1))
                        dve.tensor_copy(V8D[:, bass.ds(i * 512 + n * P, P)], PS[0:DEC, 6, 0:P]).then_inc(v8d_ready, 1)
                    ahead(i + (uk + 3), r)
            dve.wait_ge(v_out, 16 * (TB + 1))

            def biased(i, part, n):
                r, qb = n // TB, n % TB
                kw = (qb + 1) * P
                j0 = SEQ - kw
                ss = SS[n % 2]
                if qb == 0:
                    dve.wait_ge(strip_loaded[r], i * 16 + (32 * part + 16))
                dve.wait_ge(sc_done, i * 8 + (16 * part + n + 1))
                for m in range(2):
                    dve.scalar_tensor_tensor(ss[:, m, 0:kw], PS[:, (4, 2)[n % 2] + m, 0:kw], DH ** -0.5,
                                             STRIP[:, r, j0:j0 + kw], ALU.mult, ALU.add).then_inc(ss_ready, 1)
                dve.wait_ge(ss_ready, i * 16 + (32 * part + 2 * n + 2))
                dve.tensor_reduce(ST[:, 8 * (n % 2):8 * (n % 2) + 2], ss[:, :, 0:kw], AX.X, ALU.max, negate=True
                                  ).then_inc(mx_ready, 1)

            def weights(i, part, n):
                kw = (n % TB + 1) * P
                o = 8 * (n % 2)
                ss = SS[n % 2]
                dve.wait_ge(ex_ready, i * 16 + (32 * part + 2 * n + 2))
                dve.reciprocal(ST[:, o + 4:o + 6], ST[:, o + 2:o + 4]).then_inc(rc_ready, 1)
                dve.wait_ge(rc_ready, i * 16 + (32 * part + 2 * n + 1))
                dve.tensor_tensor(ST[:, o + 6:o + 7], ST[:, o + 5:o + 6], NLAM, ALU.mult).then_inc(rc_ready, 1)
                dve.tensor_scalar(ss[:, 0, 0:kw], ss[:, 0, 0:kw], ST[:, o + 4:o + 5], None, ALU.mult
                                  ).then_inc(s0n_ready, 1)
                dve.wait_ge(rc_ready, i * 16 + (32 * part + 2 * n + 2))
                dve.wait_ge(s0n_ready, i * 8 + (16 * part + n + 1))
                dve.scalar_tensor_tensor(ss[:, 0, 0:kw], ss[:, 1, 0:kw], ST[:, o + 6:o + 7], ss[:, 0, 0:kw],
                                         ALU.mult, ALU.add).then_inc(ww_ready, 1)

            def heads(part):
                with dve.Fori(0, NH // 4) as i:
                    biased(i, part, 0)
                    for n in range(2 * TB):
                        if n + 1 < 2 * TB:
                            biased(i, part, n + 1)
                        weights(i, part, n)

            heads(0)
            def step(n):
                dve.wait_ge(soft_step, n)

            dve.wait_ge(page_used[3], 2 * DEC)
            dve.tensor_reduce(NMAX, PS[:, 0:2, :].rearrange("p g c -> p (g c)"), AX.X, ALU.max, negate=True
                              ).then_inc(soft_step, 1)
            step(1)
            dve.wait_ge(newscore_done, 1)
            dve.tensor_scalar(NMAX1, PS[:, 2, 0:1], -1.0, NMAX, ALU.mult, ALU.min).then_inc(soft_step, 1)
            step(2)
            dve.tensor_scalar(SHIFT, NMAX1, DH ** -0.5, None, ALU.mult).then_inc(shift_ready, 1)
            dve.wait_ge(dec_exp, 2)
            dve.tensor_tensor(TOTAL, SUM, OWN_EXP, ALU.add).then_inc(soft_step, 1)
            step(3)
            dve.reciprocal(TOTAL, TOTAL).then_inc(soft_step, 1)
            step(4)
            dve.tensor_tensor(TOTAL, TOTAL, SIGN, ALU.mult).then_inc(soft_step, 1)
            step(5)
            dve.tensor_scalar(COMB[:, :], ROWS[:, 0:PAIRS], TOTAL, None, ALU.mult).then_inc(comb_ready, 1)
            dve.wait_ge(comb_ready, 1)
            dve.tensor_scalar(COMB_OWN[:, :], COMB[:, :], OWN_EXP, None, ALU.mult).then_inc(comb_ready, 1)
            dve.wait_ge(wd_done, 1)
            dve.tensor_copy(WD[:, :, :].rearrange("p g x -> p (g x)"), PS[:, 4, :]).then_inc(wd_ready, 1)
            dve.wait_ge(wd_done, 2)
            dve.wait_ge(vn_ready, NH)
            dve.tensor_tensor(OWN[:, :, :], PS[:, 3, 0:PAIRS].rearrange("p (b h) -> p h b", b=DEC), VN[:, :, :], ALU.mult
                              ).then_inc(wd_ready, 1)
            heads(1)
            dve.wait_ge(page_used[3], 4 * DEC)
            dve.tensor_tensor(SCA[0:PAIRS, :].rearrange("p (h c) -> p h c", h=NH),
                              PS[0:PAIRS, 0:2, :].rearrange("p g (h c) -> p (g h) c", c=P),
                              ROWS[0:PAIRS, 2 * PAIRS + 2:2 * PAIRS + 2 + NH].unsqueeze(2).to_broadcast([PAIRS, NH, P]),
                              ALU.mult).then_inc(ov_step, 1)
            dve.wait_ge(ov_step, 1)
            dve.tensor_reduce(OVR[:, :], SCA[0:PAIRS, :].rearrange("p (h c) -> p c h", h=NH), AX.X, ALU.add
                              ).then_inc(ov_step, 1)
            dve.wait_ge(ov_turned, 1)
            dve.tensor_tensor(OF[:, :, SEQ:T], PS[:, 6, 0:PAIRS].rearrange("p (b h) -> p h b", b=DEC), OWN[:, :, :],
                              ALU.add).then_inc(new_step, 1)
            dve.wait_ge(of_ready, NH)
            dve.wait_ge(new_step, 1)
            for d in range(NH):
                if d >= 2:
                    dve.wait_ge(on_mm, d - 1)
                dve.tensor_tensor(SG[:, d % 2, :], OF[:, d, :], OF[:, d, :], ALU.mult).then_inc(on_sq, 1)
            for d in range(NH + 1):
                if d < NH:
                    dve.wait_ge(on_rs, d + 1)
                    dve.scalar_tensor_tensor(OF[:, d, :], OF[:, d, :], SUBG, RSN[:, d, :], ALU.mult, ALU.mult
                                             ).then_inc(on_mul, 1)
                if d >= 1:
                    dve.wait_ge(on_hi, d)
                    dve.tensor_tensor(HL[:, d - 1, :], OF[:, d - 1, :], HH[:, d - 1, :].bitcast(F32), ALU.subtract
                                      ).then_inc(on_lo, 1)
            clear_acc(4)
            u0 = UB["o"] // 2
            with dve.Fori(0, 2) as i:
                for r in range(2):
                    for c in range(2):
                        residual(i * 4 + (2 * r + c), i * 2 + r, c, i * 4 + (4 * u0 + 2 * r + c + 1), 4,
                                 1.0 / ALPHA, True)
                    ahead(i + (u0 + 1), r)
            layer_norm(4)
            ffn(3)
            layer_norm(5)


def shape_tables():
    f = np.float32
    identity = np.eye(P, dtype=f)
    half = DK // 2
    inv = f(10000.0) ** (-np.arange(half, dtype=f) / f(half))
    pos = np.concatenate([np.arange(SEQ), np.full(DEC, PAST)]).astype(f)
    ang = (inv[:, None] * pos[None, :]).astype(f).astype(np.float64)
    rope = np.stack([np.cos(ang), np.sin(ang)]).astype(f)
    gamma = 1.0 - 2.0 ** (-5.0 - np.arange(RH, dtype=np.float64))
    ret = np.zeros((RH, P, T), f)
    d = np.arange(SEQ)[None, :] - np.arange(P)[:, None]
    tok = np.arange(TB)[None, :] * P + np.arange(P)[:, None]
    for h in range(RH):
        ret[h, :, :SEQ] = np.where(d >= 0, gamma[h] ** np.maximum(d, 0), 0.0)
        ret[h, :, SEQ:SEQ + TB] = gamma[h] ** (SEQ - 1 - tok)
        ret[h, :, SEQ + TB] = gamma[h]

    def bucket(n):
        n = np.maximum(n, 0)
        exact = BUCKETS // 2
        nf = np.maximum(n, 1).astype(f)
        large = exact + (np.log(nf / f(exact)) / f(math.log(128 / exact)) * f(BUCKETS - exact)).astype(np.int32)
        return np.where(n < exact, n, np.minimum(large, BUCKETS - 1))

    n = SEQ - 1 - np.arange(LINE)
    line = (bucket(n)[None, :] == np.arange(BUCKETS)[:, None]).astype(f)
    mask = np.repeat(np.where(n < 0, MASKED, 0.0).astype(f)[None, :], NH, 0)
    past = (bucket(PAST - np.arange(PAST))[None] == np.arange(BUCKETS)[:, None]).astype(f)
    row = np.arange(P)
    rows = np.concatenate([row[:, None] // 2 == np.arange(PAIRS), row[:, None] % 2 == np.arange(2),
                           np.zeros((P, PAIRS)), row[:, None] % NH == np.arange(NH)], 1).astype(f)
    return identity, rope, ret, line, mask, past, rows


def kernel(x_prompt, x_sample, state_ret, cache_k, cache_v, page_table, ln_g, ln_b, ffn_w_in, ffn_w_out,
           ret_w_in, ret_w_out, w_kv, diff_w_q, diff_w_o, diff_lambda, diff_subln_g, rel_bias):
    from concourse import bacc
    from concourse.bass_utils import run_bass_kernel_spmd

    def tiles(w):
        w = np.asarray(w)
        return np.ascontiguousarray(w.reshape(-1, P, w.shape[1] // UC, UC).transpose(2, 1, 0, 3))

    x = np.concatenate([np.asarray(x_prompt)[0], np.asarray(x_sample)[:, 0]])
    ffn_in = np.asarray(ffn_w_in).reshape(4, D, 2 * FFN)
    w_in = np.stack([tiles(w).reshape(2, FFN // UC, P, KT, UC).swapaxes(0, 1) for w in ffn_in])
    w_out = np.stack([tiles(w) for w in np.asarray(ffn_w_out).reshape(4, FFN, D)])
    r = tiles(np.asarray(ret_w_in)[0])
    r = np.stack([np.stack([r[h], r[4 + h], r[8 + 2 * h], r[9 + 2 * h], r[16 + 2 * h], r[17 + 2 * h]])
                  for h in range(RH)])
    n_pool = np.asarray(cache_k).shape[0]
    identity, rope, ret, line, mask, past, rows = shape_tables()
    arrays = {
        "x_t": x.T.reshape(KT, P, T).swapaxes(0, 1),
        "w_in": w_in.reshape(88, P, KT, UC),
        "w_out": w_out.reshape(16, P, FT, UC),
        "w_ret_in": r.reshape(24, P, KT, UC),
        "w_ret_out": tiles(np.asarray(ret_w_out)[0]),
        "w_q": tiles(np.asarray(diff_w_q)[0]),
        "w_kv": tiles(w_kv),
        "w_o": tiles(np.asarray(diff_w_o)[0]),
        "ln_g": np.asarray(ln_g).reshape(6, KT, P).transpose(2, 0, 1),
        "ln_b": np.asarray(ln_b).reshape(6, KT, P).transpose(2, 0, 1),
        "state": np.asarray(state_ret)[0].reshape(DEC, RH, 2, P, DV).swapaxes(2, 3),
        "cache_kt": np.asarray(cache_k).transpose(0, 3, 2, 1).reshape(n_pool, P, NH * PAGE),
        "cache_v": np.asarray(cache_v).reshape(n_pool, PAGE, D),
        "pages": np.asarray(page_table).reshape(1, DEC * NPG),
        "lam_vecs": np.broadcast_to(np.asarray(diff_lambda)[0], (P, 4, DH)),
        "subln_g": np.asarray(diff_subln_g).reshape(P, 1),
        "rel_bias": np.asarray(rel_bias),
        "identity": identity, "rope": rope, "ret_tab": ret, "onehot_line": line, "line_mask": mask,
        "onehot_past": past, "row_tab": rows,
        "rel_rows": np.broadcast_to(np.asarray(rel_bias)[:, None, :, None], (BUCKETS, DEC, NH, 2)).reshape(BUCKETS, P),
    }
    arrays = {k: np.ascontiguousarray(v) for k, v in arrays.items()}
    nc = bacc.Bacc("TRN2", target_bir_lowering=False, num_devices=1)
    args = {k: nc.dram_tensor(k, v.shape, mybir.dt.from_np(v.dtype), kind="ExternalInput").ap()
            for k, v in arrays.items()}
    outs = {"y_t": (P, KT, T), "state_p": (RH, P, 2, DV), "state_s": (DEC, RH, P, 2, DV), "k_t": (P, NH, T),
            "v_p": (TB, P, D), "v_s": (DEC, D)}
    for k, shape in outs.items():
        args[k] = nc.dram_tensor(k, shape, F32, kind="ExternalOutput").ap()
    for k, shape in {"bias_rep": (NH, P * LINE), "v_rows": (DEC, DV)}.items():
        args[k] = nc.dram_tensor(k, shape, F32, kind="Internal").ap()
    trunk_kernel(nc, **args)
    r = run_bass_kernel_spmd(nc, [arrays], core_ids=[0]).results[0]
    y = r["y_t"].swapaxes(0, 1).reshape(D, T).T
    k = r["k_t"].transpose(2, 1, 0)
    return (y[None, :SEQ], y[SEQ:, None],
            r["state_p"].swapaxes(1, 2).reshape(1, 1, RH, DK, DV),
            r["state_s"].swapaxes(2, 3).reshape(1, DEC, RH, DK, DV),
            k[None, :SEQ], r["v_p"].reshape(1, SEQ, NH, 2 * DH),
            k[SEQ:, None], r["v_s"].reshape(DEC, 1, NH, 2 * DH))
```
